# Optimizing a Trainium2 kernel written in Bass

```python
import jax, jax.numpy as jnp
from jax import lax
import numpy as np

D_MODEL = 1024
BATCH = 1
SEQ = 256
DEPTH = 2

N_MIXERS = 2
CONV_WIDTH = 3
MLA_HEADS = 8
Q_LORA = 384
KV_LORA = 256
QK_NOPE = 128
QK_ROPE = 64
QK_HEAD = QK_NOPE + QK_ROPE
V_HEAD = 128
ROPE_THETA = 10000.0
ATTN_BLOCK = 128
PEER_HEADS = 8
PEER_KEYS = 128
PEER_EXPERTS = PEER_KEYS * PEER_KEYS
PEER_DKEY = 256
PEER_HALF = PEER_DKEY // 2
PEER_TOPK = 16
PEER_CHUNK = 128
NORM_EPS = 1e-6

kernel_name = "hybrid_shortconv_mla_peer_adaln"

def rms_norm(x, g):
    xf = x.astype(jnp.float32)
    y = xf * lax.rsqrt(jnp.mean(xf * xf, axis=-1, keepdims=True) + NORM_EPS)
    return (y * g.astype(jnp.float32)).astype(x.dtype)

def modulate(x, g, shift, scale):
    return rms_norm(x, g) * (1 + scale[:, None, :]) + shift[:, None, :]

def short_conv_mixer(h, w_in, w_conv, w_out):
    b_gate, c_gate, v = jnp.split(h @ w_in, 3, axis=-1)
    u = c_gate * v
    conv = lax.conv_general_dilated(
        u, w_conv[:, None, :].astype(u.dtype), window_strides=(1,),
        padding=[(CONV_WIDTH - 1, 0)], dimension_numbers=("NWC", "WIO", "NWC"),
        feature_group_count=D_MODEL)
    return (b_gate * conv) @ w_out

def apply_rope(x, cos, sin):
    half = x.shape[-1] // 2
    x1, x2 = x[..., :half], x[..., half:]
    return jnp.concatenate([x1 * cos - x2 * sin, x1 * sin + x2 * cos], axis=-1)

def mla_mixer(h, positions, w_in, q_a_g, kv_a_g, w_qb, w_kvb, q_g, k_g, w_out):
    B, S, _ = h.shape
    q_lat, kv_lat, k_rope = jnp.split(h @ w_in, [Q_LORA, Q_LORA + KV_LORA], axis=-1)
    q = (rms_norm(q_lat, q_a_g) @ w_qb).reshape(B, S, MLA_HEADS, QK_HEAD)
    kv = (rms_norm(kv_lat, kv_a_g) @ w_kvb).reshape(B, S, MLA_HEADS, QK_NOPE + V_HEAD)
    k_nope, v = kv[..., :QK_NOPE], kv[..., QK_NOPE:]
    k = jnp.concatenate(
        [k_nope, jnp.broadcast_to(k_rope[:, :, None, :], (B, S, MLA_HEADS, QK_ROPE))], axis=-1)
    q = rms_norm(q, q_g)
    k = rms_norm(k, k_g)
    inv_freq = ROPE_THETA ** (-jnp.arange(0, QK_ROPE, 2, dtype=jnp.float32) / QK_ROPE)
    ang = positions[..., None].astype(jnp.float32) * inv_freq
    cos = jnp.cos(ang)[:, :, None, :].astype(h.dtype)
    sin = jnp.sin(ang)[:, :, None, :].astype(h.dtype)
    q = jnp.concatenate([q[..., :QK_NOPE], apply_rope(q[..., QK_NOPE:], cos, sin)], axis=-1)
    k = jnp.concatenate([k[..., :QK_NOPE], apply_rope(k[..., QK_NOPE:], cos, sin)], axis=-1)
    scale = QK_HEAD ** -0.5
    outs = []
    for start in range(0, S, ATTN_BLOCK):
        end = start + ATTN_BLOCK
        s = jnp.einsum("bqhd,bkhd->bhqk", q[:, start:end], k[:, :end]).astype(jnp.float32) * scale
        mask = (start + jnp.arange(ATTN_BLOCK))[:, None] >= jnp.arange(end)[None, :]
        p = jax.nn.softmax(jnp.where(mask, s, -jnp.inf), axis=-1).astype(v.dtype)
        outs.append(jnp.einsum("bhqk,bkhd->bqhd", p, v[:, :end]))
    o = jnp.concatenate(outs, axis=1).reshape(B, S, MLA_HEADS * V_HEAD)
    return o @ w_out

def peer_mixer(h, w_q, subkeys, u_tab, v_tab):
    B, S, D = h.shape
    tokens = h.reshape(-1, PEER_CHUNK, D)

    def chunk_fn(xc):
        C = xc.shape[0]
        q = (xc @ w_q).reshape(C, PEER_HEADS, 2, PEER_HALF)
        s = jnp.einsum("chpd,hpnd->chpn", q, subkeys).astype(jnp.float32)
        top_s, top_i = lax.top_k(s, PEER_TOPK)
        cand = top_s[:, :, 0, :, None] + top_s[:, :, 1, None, :]
        best_s, best_pos = lax.top_k(cand.reshape(C, PEER_HEADS, PEER_TOPK * PEER_TOPK), PEER_TOPK)
        ia = jnp.take_along_axis(top_i[:, :, 0], best_pos // PEER_TOPK, axis=-1)
        ib = jnp.take_along_axis(top_i[:, :, 1], best_pos % PEER_TOPK, axis=-1)
        expert = ia * PEER_KEYS + ib
        g = jax.nn.softmax(best_s, axis=-1).astype(xc.dtype)
        act = jax.nn.gelu(jnp.einsum("chkd,cd->chk", u_tab[expert], xc), approximate=False) * g
        return jnp.einsum("chk,chkd->cd", act, v_tab[expert])

    return lax.map(chunk_fn, tokens).reshape(B, S, D)

def setup_inputs(seed: int = 0) -> dict:
    key = jax.random.key(seed)
    ks = jax.random.split(key, 24)
    f32 = jnp.float32
    n_conv = (DEPTH + N_MIXERS - 1) // N_MIXERS
    n_mla = DEPTH // N_MIXERS
    D = D_MODEL

    def nrm(k, shape, std):
        return jax.random.normal(k, shape, f32) * std

    def gain(k, shape):
        return 1.0 + 0.02 * jax.random.normal(k, shape, f32)

    x = jax.random.normal(ks[0], (BATCH, SEQ, D), f32)
    c = jax.random.normal(ks[1], (BATCH, D), f32)
    positions = jnp.broadcast_to(jnp.arange(SEQ, dtype=jnp.int32)[None, :], (BATCH, SEQ))
    return {
        "x": x,
        "c": c,
        "positions": positions,
        "tok_norm": gain(ks[2], (DEPTH, D)),
        "ch_norm": gain(ks[3], (DEPTH, D)),
        "ada_w": nrm(ks[4], (DEPTH, D, 6 * D), 0.5 * D ** -0.5),
        "ada_b": nrm(ks[5], (DEPTH, 6 * D), 0.02),
        "conv_in_w": nrm(ks[6], (n_conv, D, 3 * D), D ** -0.5),
        "conv_w": nrm(ks[7], (n_conv, CONV_WIDTH, D), CONV_WIDTH ** -0.5),
        "conv_out_w": nrm(ks[8], (n_conv, D, D), D ** -0.5),
        "mla_in_w": nrm(ks[9], (n_mla, D, Q_LORA + KV_LORA + QK_ROPE), D ** -0.5),
        "q_a_norm": gain(ks[10], (n_mla, Q_LORA)),
        "kv_a_norm": gain(ks[11], (n_mla, KV_LORA)),
        "q_b_w": nrm(ks[12], (n_mla, Q_LORA, MLA_HEADS * QK_HEAD), Q_LORA ** -0.5),
        "kv_b_w": nrm(ks[13], (n_mla, KV_LORA, MLA_HEADS * (QK_NOPE + V_HEAD)), KV_LORA ** -0.5),
        "q_norm": gain(ks[14], (n_mla, QK_HEAD)),
        "k_norm": gain(ks[15], (n_mla, QK_HEAD)),
        "mla_out_w": nrm(ks[16], (n_mla, MLA_HEADS * V_HEAD, D), (MLA_HEADS * V_HEAD) ** -0.5),
        "peer_q_w": nrm(ks[17], (DEPTH, D, PEER_HEADS * PEER_DKEY), D ** -0.5),
        "peer_subkeys": nrm(ks[18], (DEPTH, PEER_HEADS, 2, PEER_KEYS, PEER_HALF), PEER_HALF ** -0.5),
        "peer_u": nrm(ks[19], (DEPTH, PEER_EXPERTS, D), D ** -0.5),
        "peer_v": nrm(ks[20], (DEPTH, PEER_EXPERTS, D), 0.5),
    }

def reference(x, c, positions, tok_norm, ch_norm, ada_w, ada_b, conv_in_w, conv_w, conv_out_w,
              mla_in_w, q_a_norm, kv_a_norm, q_b_w, kv_b_w, q_norm, k_norm, mla_out_w,
              peer_q_w, peer_subkeys, peer_u, peer_v):
    c_act = jax.nn.silu(c)
    for i in range(DEPTH):
        mod = c_act @ ada_w[i] + ada_b[i]
        sh1, sc1, g1, sh2, sc2, g2 = jnp.split(mod, 6, axis=-1)
        h = modulate(x, tok_norm[i], sh1, sc1)
        j = i // N_MIXERS
        if i % N_MIXERS == 0:
            y = short_conv_mixer(h, conv_in_w[j], conv_w[j], conv_out_w[j])
        else:
            y = mla_mixer(h, positions, mla_in_w[j], q_a_norm[j], kv_a_norm[j], q_b_w[j],
                          kv_b_w[j], q_norm[j], k_norm[j], mla_out_w[j])
        x = x + g1[:, None, :] * y
        h = modulate(x, ch_norm[i], sh2, sc2)
        x = x + g2[:, None, :] * peer_mixer(h, peer_q_w[i], peer_subkeys[i], peer_u[i], peer_v[i])
    return x


_drawn_inputs = setup_inputs


def setup_inputs(seed=0):
    import zlib

    import numpy as np

    out = dict(_drawn_inputs(seed))
    spreads = {}
    factors = {'tok_norm': 3.017,
     'ch_norm': 19.67,
     'q_a_norm': 8.0,
     'kv_a_norm': 8.0,
     'q_norm': 8.0,
     'k_norm': 8.0}
    for name, (base, spread) in spreads.items():
        noise = np.random.default_rng([zlib.crc32(name.encode()), seed]).standard_normal(out[name].shape)
        drawn = base * np.exp(spread * noise) if base else spread * noise
        out[name] = __import__('jax').numpy.asarray(drawn.astype(out[name].dtype))
    for name, factor in factors.items():
        out[name] = (out[name] * factor).astype(out[name].dtype)
    return out
```

```python
from contextlib import ExitStack

import numpy as np

import concourse.bass as bass
from concourse import mybir

F32 = mybir.dt.float32
F32R = mybir.dt.float32r
U32 = mybir.dt.uint32
I32 = mybir.dt.int32
ALU = mybir.AluOpType
ACT = mybir.ActivationFunctionType
AX = mybir.AxisListType

P = 128
D = 1024
KB = D // P
T = 256
TT = T // P
HEADS = 8
Q_LORA, KV_LORA, ROPE, NOPE, VH = 384, 256, 64, 128, 128
HALF_ROPE = ROPE // 2
QB, KVB = Q_LORA // P, KV_LORA // P
KEYS, TOPK = 128, 16
PAIRS = 2 * HEADS
SEL = HEADS * TOPK
EPS = 1e-6
QK_HEAD = NOPE + ROPE
RAW = 4
ADA = 4
BLK = 4
NEG = -3.0e38

C_ID, C_ONE, C_MASK, C_ROW, C_IOTA, C_ROWCOL, C_FREQ = 0, 128, 256, 640, 1152, 1168, 1172
C_N = 1176
V_TOK, V_CH, V_ADAB, V_CONV, V_QA, V_KVA, V_QN, V_KN = 0, 16, 32, 128, 152, 155, 157, 160
V_N = 164

STAGES = [("conv_in", 24), ("conv_out", 8), ("peer_q0", 16), ("mla_in", 7), ("q_b", 6), ("k_b", 4), ("v_b", 2),
          ("mla_out", 8), ("peer_q1", 16)]
BASE, _n = {}, 0
for _name, _count in STAGES:
    BASE[_name] = _n
    _n += _count
PANELS = _n
TWO_PI = 2.0 * np.pi
PI_1 = 6.28125
PI_2 = float(np.float32(np.floor((TWO_PI - PI_1) * 2.0 ** 21) / 2.0 ** 21))
PI_3 = float(np.float32(TWO_PI - PI_1 - PI_2))
ROUND = 12582912.0


def program(nc, xT_in, c_in, pos_in, vec_in, con_in, ada_in, pan_in, key_in, u0_in, u1_in, v0_in, v1_in, out):
    ctx = ExitStack()
    with ctx:
        def sb(name, shape, dt=F32):
            return ctx.enter_context(nc.sbuf_tensor(name, shape, dt))

        def sem(name):
            return ctx.enter_context(nc.semaphore(name))

        xT = sb("xT", [P, KB * T])
        con = sb("con", [P, C_N])
        vec = sb("vec", [P, V_N])
        eps = sb("eps", [P, 1])
        crow = sb("crow", [P, D])
        mod = sb("mod", [P, 96])
        ada_sum = sb("ada_sum", [P, ADA])
        gain = sb("gain", [P, KB])
        raw = sb("raw", [P, RAW, D])
        w_hi = sb("w_hi", [P, 2, D], F32R)
        w_lo = sb("w_lo", [P, 2, D], F32R)
        act_hi = sb("act_hi", [P, KB * T], F32R)
        act_lo = sb("act_lo", [P, KB * T], F32R)
        act32 = sb("act32", [P, KB * T])
        ada = sb("ada", [P, ADA, D])
        rms = sb("rms", [P, 2 * T])
        rstd = sb("rstd", [P, 2 * T])
        arena = sb("arena", [P, 16384])
        keys = sb("keys", [P, PAIRS * KEYS])
        q_sb = sb("q_sb", [P, 2, T])
        top_i = sb("top_i", [P, TT, PAIRS * TOPK], U32)
        best_v = sb("best_v", [P, TT, SEL])
        best_p = sb("best_p", [P, TT, SEL], U32)
        gate = sb("gate", [P, TT, SEL])
        eid = sb("eid", [P, TT, SEL], U32)
        eid_slot = sb("eid_slot", [P, 2, BLK], U32)
        dots = sb("dots", [P, 2, BLK])
        coef = sb("coef", [P, 2, BLK])

        sq = arena[:, 0:2048]
        c_sb = arena[:, 2048:2048 + T]
        u_pad = arena[:, 2560:2560 + T + 2]
        conv_t = arena[:, 3072:3072 + T]
        qn = arena[:, 0:2048]
        qr = arena[:, 2048:3072]
        kn = arena[:, 3072:5120]
        kr = arena[:, 5120:6144]
        vv = arena[:, 6144:8192]
        sqn = arena[:, 8192:10240]
        sqr = arena[:, 10240:11264]
        rot = arena[:, 11264:12288]
        qz = arena[:, 12288:16384]
        kraw = act32[:, 0:512]
        lat = act32[:, 512:512 + 5 * T]
        cosb = sb("cosb", [P, T])
        sinb = sb("sinb", [P, T])
        posi = sb("posi", [P, T], I32)
        ang = sb("ang", [P, T])
        tmp = sb("tmp", [P, T])
        s_sb = sb("s_sb", [P, 2, 384])
        pT = sb("pT", [P, 2, 384])
        smax = sb("smax", [P, 2, 2])
        ssum = sb("ssum", [P, 2, 2])
        topv = arena[:, 0:TT * 4 * TOPK]
        topi = sb("topi", [P, TT * 4 * TOPK], U32)
        work = arena[:, 256:256 + TT * P]
        cand = arena[:, 512:512 + TT * 256]
        cwork = arena[:, 1024:1024 + TT * 256]
        bestv = arena[:, 1536:1536 + TT * 2 * TOPK]
        bestp = sb("bestp", [P, TT * 2 * TOPK], U32)
        dec_u = sb("dec_u", [P, 2, SEL], U32)
        dec_f = arena[:, 2048:2048 + 2 * SEL]
        tif = arena[:, 2560:2560 + PAIRS * TOPK]
        eq = arena[:, 4096:4096 + SEL * TOPK]
        eab = arena[:, 6144:6144 + 2 * SEL]
        esum = arena[:, 6656:6656 + 16]
        hrow = arena[:, 8192:8192 + TT * D]
        yrow = arena[:, 10240:10240 + TT * D]
        gu = arena[:, 12288:12288 + BLK * D]
        gv = arena[:, 0:2 * BLK * D]

        ps = [ctx.enter_context(nc.psum_tensor(f"bank{b}", [P, 512], F32)) for b in range(8)]
        PAN = ps[0:2]
        STAT = ps[2]
        SC = ps[3:5]
        TR = ps[5:7]
        OV = ps[7]

        ident = con[:, C_ID:C_ID + P]
        ones = con[:, C_ONE:C_ONE + P]

        s_const = sem("constants_landed")
        s_eps = sem("eps_set")
        s_key = sem("subkeys_landed")
        s_out = sem("output_stored")
        landed = [sem(f"panel_landed{i}") for i in range(RAW)]
        hi_done = sem("panel_hi_ready")
        lo_done = sem("panel_lo_ready")
        pan_done = sem("panel_multiplied")
        evac = {n: sem(f"evacuated_{n}") for n, _ in STAGES}
        ada_landed = [sem(f"ada_landed{i}") for i in range(ADA)]
        ada_used = sem("ada_rows_used")
        s_silu = sem("silu_c_ready")
        x_ready = sem("x_ready")
        sq_ready = sem("squares_ready")
        sum_ready = sem("square_sums_ready")
        rms_ready = sem("rms_ready")
        f32_ready = sem("activations_f32_ready")
        act_hi_ready = sem("activations_hi_ready")
        act_ready = sem("activations_split")
        sc_done = sem("key_scores_ready")
        sc_used = sem("key_scores_used")
        sc_seen = sem("key_scores_seen")
        gate_in = sem("gate_exponents_ready")
        gate_exp = sem("gate_exp_ready")
        sel_done = sem("selection_done")
        slot_set = sem("expert_slot_set")
        slot_seen = sem("expert_slot_seen")
        u_landed = [sem(f"u_row_landed{i}") for i in range(BLK)]
        v_landed = [sem(f"v_row_landed{i}") for i in range(2 * BLK)]
        u_used = sem("u_rows_used")
        v_used = sem("v_rows_used")
        s_gelu = sem("gelu_ready")
        hr_done = sem("h_rows_transposed")
        hr_copied = sem("h_rows_copied")
        yt_done = sem("y_transposed")
        yt_added = sem("y_added")
        lat_in = sem("latents_copied")
        lat_sq = sem("latent_squares")
        lat_sum = sem("latent_sums")
        lat_rms = sem("latent_rms")
        v_mul = sem("values_multiplied")
        v_copied = sem("values_copied")
        head_sq = sem("head_squares")
        head_sum = sem("head_sums")
        head_rms = sem("head_rms")
        head_rstd = sem("head_rstd")
        trig_in = sem("angles_reduced")
        trig = sem("sin_cos_ready")
        qk_ready = sem("qk_ready")
        s_done = sem("scores_ready")
        s_masked = sem("scores_masked")
        p_exp = sem("probs_exp")
        p_norm = sem("probs_normalised")
        p_tr = sem("probs_transposed")
        p_copied = sem("probs_copied")
        o_done = sem("head_output_ready")
        o_copied = sem("head_output_copied")

        block = ctx.enter_context(nc.Block())

        def ring(stage, j, unroll=0, it=0):
            i = BASE[stage] + j
            step = unroll // RAW * 16
            return i % RAW, i % 2, it * step + 16 * (i // RAW + 1), it * unroll + (i + 1)

        @block.sync
        def _(sp):
            def load_panel(stage, j, unroll=0, it=0, width=D):
                slot, _, _, n = ring(stage, j, unroll, it)
                sp.wait_ge(lo_done, n)
                sp.dma_start(raw[:, slot, 0:width], pan_in[bass.ds(n - 1, 1), :, 0:width].rearrange("o p n -> p (o n)")
                             ).then_inc(landed[slot], 16)

            def load_ada(j, row):
                sp.wait_ge(ada_used, row + 1)
                sp.dma_start(ada[:, j, :], ada_in[bass.ds(row, 1)].rearrange("o p n -> p (o n)")
                             ).then_inc(ada_landed[j], 16)

            sp.dma_start(crow[:], c_in.partition_broadcast(P)).then_inc(s_const, 16)
            sp.dma_start(vec[:], vec_in).then_inc(s_const, 16)
            sp.dma_start(xT[:], xT_in).then_inc(s_const, 16)
            sp.dma_start(con[:], con_in).then_inc(s_const, 16)
            sp.dma_start(posi[:], pos_in.partition_broadcast(P)).then_inc(s_const, 16)
            with sp.Fori(0, 4) as it:
                for j in range(ADA):
                    load_ada(j, it * 4 + j)
            with sp.Fori(0, 2) as it:
                for b in range(4):
                    for j in range(3):
                        load_panel("conv_in", 3 * b + j, 12, it)
                    for j in range(ADA):
                        load_ada(j, it * 16 + (16 + 4 * b + j))
            with sp.Fori(0, 2) as it:
                for j in range(4):
                    load_panel("conv_out", j, 4, it)
            sp.dma_start(keys[:], key_in[0]).then_inc(s_key, 16)
            with sp.Fori(0, 4) as it:
                for j in range(4):
                    load_panel("peer_q0", j, 4, it)
            for j in range(RAW):
                load_panel("mla_in", j)
            with sp.Fori(0, 12) as it:
                for j in range(ADA):
                    load_ada(j, it * 4 + (48 + j))
            sp.wait_ge(sc_done, PAIRS)
            sp.dma_start(keys[:], key_in[1]).then_inc(s_key, 16)
            for j in range(RAW, 7):
                load_panel("mla_in", j)
            for j in range(6):
                load_panel("q_b", j, width=2 * Q_LORA)
            for j in range(4):
                load_panel("k_b", j, width=2 * KV_LORA)
            for j in range(2):
                load_panel("v_b", j)
            with sp.Fori(0, 2) as it:
                for j in range(4):
                    load_panel("mla_out", j, 4, it)
            with sp.Fori(0, 4) as it:
                for j in range(4):
                    load_panel("peer_q1", j, 4, it)
            sp.wait_ge(x_ready, 4)
            sp.dma_start(out, xT[:]).then_inc(s_out, 16)
            sp.wait_ge(s_out, 16)

        @block.tensor
        def _(pe):
            def product(bank, half, col0, kb, act0):
                for k in range(kb):
                    w = slice(col0 + k * P, col0 + (k + 1) * P)
                    a = slice((act0 + k) * T, (act0 + k + 1) * T)
                    pe.matmul(bank, w_hi[:, half, w], act_hi[:, a], start=(k == 0), stop=False)
                    pe.matmul(bank, w_hi[:, half, w], act_lo[:, a], start=False, stop=False)
                    last = pe.matmul(bank, w_lo[:, half, w], act_hi[:, a], start=False, stop=(k == kb - 1))
                return last

            def wait_panel(stage, j, unroll=0, it=0):
                _, half, _, n = ring(stage, j, unroll, it)
                pe.wait_ge(lo_done, n + RAW)
                pe.wait_ge(evac[stage], it * unroll + (j + 1))
                return half

            def full_panel(stage, j, unroll=0, it=0):
                half = wait_panel(stage, j, unroll, it)
                product(PAN[j % 2][:, 0:T], half, 0, KB, 0).then_inc(pan_done, 1)

            def square_sums(n):
                pe.wait_ge(sq_ready, n)
                for k in range(KB):
                    mm = pe.matmul(STAT[:, 0:T], ones, sq[:, k * T:(k + 1) * T], start=(k == 0), stop=(k == KB - 1))
                mm.then_inc(sum_ready, 1)

            def peer(l):
                square_sums(2 * l + 2)
                pe.wait_ge(act_ready, [3, 7][l])
                pe.wait_ge(s_key, 16 * (l + 1))
                stage = f"peer_q{l}"
                with pe.Fori(0, 4) as it:
                    for j in range(4):
                        full_panel(stage, j, 4, it)
                        pe.wait_ge(evac[stage], it * 4 + (j + 3))
                        pe.wait_ge(sc_used, it * 4 + (16 * l + j + 1))
                        for t in range(TT):
                            mm = pe.matmul(SC[j % 2][:, t * P:(t + 1) * P], q_sb[:, j % 2, t * P:(t + 1) * P],
                                           keys[:, bass.ds((it * 4 + j) * KEYS, KEYS)], start=True, stop=True)
                        mm.then_inc(sc_done, 1)
                for t in range(TT):
                    for g in range(2):
                        if 2 * t + g >= 2:
                            pe.wait_ge(hr_copied, 4 * l + 2 * t + g - 1)
                        for k in range(4):
                            o = (4 * g + k) * T + t * P
                            mm = pe.transpose(TR[g][:, k * P:(k + 1) * P], act32[:, o:o + P], ident)
                        mm.then_inc(hr_done, 1)
                pe.wait_ge(hr_copied, 4 * l + 4)
                for t in range(TT):
                    pe.wait_ge(v_used, 2 * BLK + SEL * (TT * l + t + 1))
                    for g in range(2):
                        if 2 * t + g >= 2:
                            pe.wait_ge(yt_added, 4 * l + 2 * t + g - 1)
                        for k in range(4):
                            o = t * D + (4 * g + k) * P
                            mm = pe.transpose(TR[g][:, k * P:(k + 1) * P], yrow[:, o:o + P], ident)
                        mm.then_inc(yt_done, 1)
                pe.wait_ge(yt_added, 4 * l + 4)

            def attention():
                square_sums(3)
                pe.wait_ge(act_ready, 4)
                for j in range(7):
                    full_panel("mla_in", j)
                pe.wait_ge(lat_sq, 1)
                for k in range(QB):
                    pe.matmul(STAT[:, 0:T], ones, sqn[:, k * T:(k + 1) * T], start=(k == 0), stop=(k == QB - 1))
                for k in range(KVB):
                    mm = pe.matmul(STAT[:, T:2 * T], ones, sqn[:, (QB + k) * T:(QB + k + 1) * T],
                                   start=(k == 0), stop=(k == KVB - 1))
                mm.then_inc(lat_sum, 1)
                pe.wait_ge(act_ready, 5)
                for j in range(6):
                    half = wait_panel("q_b", j)
                    product(PAN[j % 2][:, 0:T], half, 0, QB, 0)
                    product(PAN[j % 2][:, T:2 * T], half, Q_LORA, QB, 0).then_inc(pan_done, 1)
                for j in range(4):
                    half = wait_panel("k_b", j)
                    product(PAN[j % 2][:, 0:T], half, 0, KVB, QB)
                    product(PAN[j % 2][:, T:2 * T], half, KV_LORA, KVB, QB).then_inc(pan_done, 1)
                halves = [ring("v_b", k)[1] for k in range(KVB)]
                pe.wait_ge(lo_done, ring("v_b", KVB - 1)[3] + RAW)
                for n, bank in enumerate((SC[0], SC[1], TR[0], TR[1])):
                    for k in range(KVB):
                        a = slice((QB + k) * T + n // 2 * P, (QB + k) * T + n // 2 * P + P)
                        w = slice(n % 2 * 512, n % 2 * 512 + 512)
                        pe.matmul(bank[:], act_hi[:, a], w_hi[:, halves[k], w], start=(k == 0), stop=False)
                        pe.matmul(bank[:], act_lo[:, a], w_hi[:, halves[k], w], start=False, stop=False)
                        mm = pe.matmul(bank[:], act_hi[:, a], w_lo[:, halves[k], w], start=False, stop=(k == KVB - 1))
                mm.then_inc(pan_done, 2)
                for i in range(8):
                    pe.wait_ge(head_sq, i // 4 + 1)
                    if i >= 2:
                        pe.wait_ge(head_rms, i - 1)
                    for e in range(2):
                        h = 2 * (i % 4) + e
                        o = (OV, STAT)[i % 2][:, e * T:(e + 1) * T]
                        pe.matmul(o, ones, sqn[:, h * T:(h + 1) * T], start=True, stop=False)
                        for x in range(2):
                            row = (h % 4) if i < 4 else 0
                            r = (2 * x + h // 4) if i < 4 else x
                            mm = pe.matmul(o, con[:, C_ROW + row * P:C_ROW + (row + 1) * P], sqr[:, r * T:(r + 1) * T],
                                           start=False, stop=(x == 1))
                    mm.then_inc(head_sum, 1)
                pe.wait_ge(qk_ready, 1)
                pe.wait_ge(v_copied, 1)
                for i in range(HEADS + 2):
                    if i < HEADS:
                        h = i
                        if h >= 2:
                            pe.wait_ge(s_masked, h - 1)
                        for t, (c0, c1) in enumerate(((0, P), (P, 3 * P))):
                            o, n = SC[h % 2][:, c0:c1], c1 - c0
                            q0 = h * T + t * P
                            pe.matmul(o, qn[:, q0:q0 + P], kn[:, h * T:h * T + n], start=True, stop=False)
                            for x in range(2):
                                z0 = (2 * h + x) * T + t * P
                                k0 = (2 * x + h // 4) * T
                                mm = pe.matmul(o, qz[:, z0:z0 + P], rot[:, k0:k0 + n], start=False, stop=(x == 1))
                        mm.then_inc(s_done, 1)
                    if 1 <= i <= HEADS:
                        h = i - 1
                        pe.wait_ge(p_norm, h + 1)
                        if h >= 2:
                            pe.wait_ge(p_copied, h - 1)
                        for b in range(3):
                            mm = pe.transpose(TR[h % 2][:, b * P:(b + 1) * P], s_sb[:, h % 2, b * P:(b + 1) * P], ident)
                        mm.then_inc(p_tr, 1)
                    if i >= 2:
                        h = i - 2
                        pe.wait_ge(p_copied, h + 1)
                        if h >= 2:
                            pe.wait_ge(o_copied, h - 1)
                        o = (OV, STAT)[h % 2]
                        v0, v1 = vv[:, h * VH:(h + 1) * VH], vv[:, D + h * VH:D + (h + 1) * VH]
                        pe.matmul(o[:, 0:P], v0, pT[:, h % 2, 0:P], start=True, stop=True)
                        pe.matmul(o[:, P:2 * P], v0, pT[:, h % 2, P:2 * P], start=True, stop=False)
                        pe.matmul(o[:, P:2 * P], v1, pT[:, h % 2, 2 * P:3 * P], start=False, stop=True
                                  ).then_inc(o_done, 1)
                pe.wait_ge(act_ready, 6)
                with pe.Fori(0, 2) as it:
                    for j in range(4):
                        full_panel("mla_out", j, 4, it)

            pe.sem_inc(pan_done, 2)
            pe.wait_ge(s_const, 80)
            square_sums(1)
            pe.wait_ge(act_ready, 1)
            with pe.Fori(0, 2) as it:
                for j in range(12):
                    full_panel("conv_in", j, 12, it)
            pe.wait_ge(act_ready, 2)
            with pe.Fori(0, 2) as it:
                for j in range(4):
                    full_panel("conv_out", j, 4, it)
            peer(0)
            attention()
            peer(1)

        @block.scalar
        def _(act):
            def split_hi(stage, j, unroll=0, it=0, width=D):
                slot, half, count, n = ring(stage, j, unroll, it)
                act.wait_ge(landed[slot], count)
                act.wait_ge(pan_done, n)
                nc.scalar.copy(w_hi[:, half, 0:width], raw[:, slot, 0:width]).then_inc(hi_done, 1)

            def split_act(n, src, width):
                act.wait_ge(f32_ready, n)
                nc.scalar.copy(act_hi[:, 0:width], src).then_inc(act_hi_ready, 1)

            def normalise(n):
                if n > 1:
                    act.wait_ge(x_ready, n - 1)
                nc.scalar.activation(sq, xT[:], ACT.Square).then_inc(sq_ready, 1)
                act.wait_ge(sum_ready, n)
                nc.scalar.activation(rms[:, 0:T], STAT[:, 0:T], ACT.Sqrt, bias=eps[:], scale=1.0 / D
                                     ).then_inc(rms_ready, 1)

            def peer(l):
                normalise(2 * l + 2)
                split_act([3, 7][l], act32[:], KB * T)
                stage = f"peer_q{l}"

                def body(it, end):
                    for j in range(4):
                        if not (end and j == 3):
                            split_hi(stage, j + 1, 4, it)
                        act.wait_ge(pan_done, ring(stage, j, 4, it)[3] + 2)
                        nc.scalar.copy(q_sb[:, j % 2, :], PAN[j % 2][:, 0:T]).then_inc(evac[stage], 1)

                act.sem_inc(evac[stage], 2)
                with act.Fori(0, 3) as it:
                    body(it, False)
                body(3, l == 1)
                for n in range(4):
                    act.wait_ge(hr_done, 4 * l + n + 1)
                    o = n // 2 * D + n % 2 * 512
                    nc.scalar.copy(hrow[:, o:o + 512], TR[n % 2][:]).then_inc(hr_copied, 1)
                act.wait_ge(gate_in, l + 1)
                nc.scalar.activation(gate[:], gate[:], ACT.Exp).then_inc(gate_exp, 1)
                for t in range(TT):
                    with act.Fori(0, SEL // (2 * BLK)) as it:
                        for s in range(2):
                            first = (TT * l + t) * SEL + s * BLK
                            act.wait_ge(u_used, it * (2 * BLK) + (first + 2 * BLK))
                            nc.scalar.activation(coef[:, s, :], dots[:, s, :], ACT.Gelu).then_inc(s_gelu, 1)

            act.wait_ge(s_const, 80)
            nc.scalar.activation(crow[:], crow[:], ACT.Silu).then_inc(s_silu, 1)
            split_hi("conv_in", 0)
            act.wait_ge(s_eps, 1)
            normalise(1)
            split_act(1, act32[:], KB * T)
            with act.Fori(0, 2) as it:
                for j in range(12):
                    split_hi("conv_in", j + 1, 12, it)
            split_act(2, act32[:], KB * T)
            with act.Fori(0, 2) as it:
                for j in range(4):
                    split_hi("conv_out", j + 1, 4, it)
            peer(0)
            act.wait_ge(trig_in, 1)
            nc.scalar.activation(sinb[:], sinb[:], ACT.Sin)
            nc.scalar.activation(cosb[:], cosb[:], ACT.Sin).then_inc(trig, 1)
            normalise(3)
            split_act(4, act32[:], KB * T)
            for j in range(7):
                split_hi("mla_in", j + 1, width=D if j < 6 else 2 * Q_LORA)
            act.wait_ge(lat_in, 1)
            nc.scalar.activation(sqn[:, 0:5 * T], lat, ACT.Square).then_inc(lat_sq, 1)
            act.wait_ge(lat_sum, 1)
            nc.scalar.activation(rms[:, 0:T], STAT[:, 0:T], ACT.Sqrt, bias=eps[:], scale=1.0 / Q_LORA)
            nc.scalar.activation(rms[:, T:2 * T], STAT[:, T:2 * T], ACT.Sqrt, bias=eps[:], scale=1.0 / KV_LORA
                                 ).then_inc(lat_rms, 1)
            split_act(5, lat, 5 * T)
            for j in range(6):
                split_hi("q_b", j + 1, width=2 * Q_LORA if j < 5 else 2 * KV_LORA)
            for j in range(4):
                split_hi("k_b", j + 1, width=2 * KV_LORA if j < 3 else D)
            split_hi("v_b", 1)
            split_hi("mla_out", 0)
            act.wait_ge(evac["q_b"], 6 + 2)
            nc.scalar.activation(sqn, qn, ACT.Square)
            nc.scalar.activation(sqr, qr, ACT.Square).then_inc(head_sq, 1)
            for i in range(8):
                if i == 4:
                    act.wait_ge(head_sum, 4)
                    act.wait_ge(evac["k_b"], 4 + 2)
                    nc.scalar.activation(sqn, kn, ACT.Square)
                    nc.scalar.activation(sqr[:, 0:2 * T], kraw, ACT.Square).then_inc(head_sq, 1)
                act.wait_ge(head_sum, i + 1)
                if i >= 1:
                    act.wait_ge(head_rstd, i)
                nc.scalar.activation(rms[:], (OV, STAT)[i % 2][:], ACT.Sqrt, bias=eps[:], scale=1.0 / QK_HEAD
                                     ).then_inc(head_rms, 1)
            for i in range(HEADS + 1):
                if i < HEADS:
                    act.wait_ge(s_masked, i + 1)
                    for t, (c0, c1) in enumerate(((0, P), (P, 3 * P))):
                        e = nc.scalar.activation(s_sb[:, i % 2, c0:c1], s_sb[:, i % 2, c0:c1], ACT.Exp,
                                                 bias=smax[:, i % 2, t:t + 1], scale=float(QK_HEAD) ** -0.5,
                                                 accum_out=ssum[:, i % 2, t:t + 1])
                    e.then_inc(p_exp, 1)
                if i >= 1:
                    act.wait_ge(p_tr, i)
                    nc.scalar.copy(pT[:, (i - 1) % 2, :], TR[(i - 1) % 2][:, 0:384]).then_inc(p_copied, 1)
            split_act(6, act32[:], KB * T)
            with act.Fori(0, 2) as it:
                for j in range(4):
                    split_hi("mla_out", j + 1, 4, it)
            peer(1)

        @block.gpsimd
        def _(pool):
            for l in range(2):
                pool.wait_ge(sel_done, l + 1)
                for t in range(TT):
                    with pool.Fori(0, SEL // (2 * BLK)) as it:
                        for s in range(2):
                            first = (TT * l + t) * SEL + s * BLK
                            r0 = it * (2 * BLK) + first
                            pool.wait_ge(v_used, r0 + BLK)
                            nc.gpsimd.tensor_copy(eid_slot[:, s, :], eid[:, t, bass.ds(it * (2 * BLK) + s * BLK, BLK)]
                                                  ).then_inc(slot_set, 1)
                            pool.wait_ge(slot_set, it * 2 + ((TT * l + t) * (SEL // BLK) + s + 1))
                            pool.sem_inc(slot_seen, 1)
                            for b in range(BLK):
                                pool.wait_ge(u_used, r0 + (b + 1))
                                pool.sem_inc(slot_seen, 1)
                                nc.gpsimd.indirect_dma_start(
                                    gu[:, b * D:(b + 1) * D], None, (u0_in, u1_in)[l],
                                    bass.IndirectOffsetOnAxis(ap=eid_slot[:, s, b:b + 1], axis=0)
                                ).then_inc(u_landed[b], 16)
                            for b in range(BLK):
                                pool.wait_ge(v_used, r0 + (b + 1))
                                pool.sem_inc(slot_seen, 1)
                                q = s * BLK + b
                                nc.gpsimd.indirect_dma_start(
                                    gv[:, q * D:(q + 1) * D], None, (v0_in, v1_in)[l],
                                    bass.IndirectOffsetOnAxis(ap=eid_slot[:, s, b:b + 1], axis=0)
                                ).then_inc(v_landed[q], 16)

        @block.vector
        def _(dve):
            def split_lo(stage, j, unroll=0, it=0, width=D):
                slot, half, _, n = ring(stage, j, unroll, it)
                dve.wait_ge(hi_done, n)
                dve.tensor_tensor(w_lo[:, half, 0:width], raw[:, slot, 0:width], w_hi[:, half, 0:width].bitcast(F32),
                                  ALU.subtract).then_inc(lo_done, 1)

            def split_act(n, src, width):
                dve.wait_ge(act_hi_ready, n)
                dve.tensor_tensor(act_lo[:, 0:width], src, act_hi[:, 0:width].bitcast(F32), ALU.subtract
                                  ).then_inc(act_ready, 1)

            def wait_product(stage, j, unroll=0, it=0):
                dve.wait_ge(pan_done, ring(stage, j, unroll, it)[3] + 2)

            def mod_col(l, s):
                return l * 48 + s * KB

            def ada_block(m):
                for j in range(ADA):
                    dve.wait_ge(ada_landed[j], m * 16 + 16)
                    dve.tensor_tensor_reduce(out=ada[:, j, :], in0=ada[:, j, :], in1=crow[:], scale=1.0, scalar=0.0,
                                             op0=ALU.mult, op1=ALU.add, accum_out=ada_sum[:, j:j + 1]
                                             ).then_inc(ada_used, 1)
                dve.drain()
                dve.tensor_tensor(mod[:, bass.ds(m * ADA, ADA)], ada_sum[:], vec[:, bass.ds(m * ADA + V_ADAB, ADA)],
                                  ALU.add)
                dve.drain()

            def normalise(n, l, g0, s0):
                sh, sc = mod_col(l, s0), mod_col(l, s0 + 1)
                dve.scalar_tensor_tensor(out=gain[:], in0=mod[:, sc:sc + KB], scalar=1.0, in1=vec[:, g0:g0 + KB],
                                         op0=ALU.add, op1=ALU.mult)
                dve.wait_ge(rms_ready, n)
                dve.reciprocal(rstd[:, 0:T], rms[:, 0:T])
                dve.drain()
                dve.tensor_tensor(act32[:].rearrange("p (k t) -> p k t", t=T), xT[:].rearrange("p (k t) -> p k t", t=T),
                                  rstd[:, 0:T].unsqueeze(1).broadcast_to([P, KB, T]), ALU.mult)
                dve.drain()
                for k in range(KB):
                    i = dve.tensor_scalar(act32[:, k * T:(k + 1) * T], act32[:, k * T:(k + 1) * T], gain[:, k:k + 1],
                                          mod[:, sh + k:sh + k + 1], ALU.mult, ALU.add)
                i.then_inc(f32_ready, 1)

            def add_to_x(stage, l, last_count):
                dve.sem_inc(evac[stage], 2)
                with dve.Fori(0, 2) as it:
                    for j in range(4):
                        split_lo(stage, j + 1, 4, it)
                        wait_product(stage, j, 4, it)
                        xk = xT[:, bass.ds((it * 4 + j) * T, T)]
                        dve.scalar_tensor_tensor(out=xk, in0=PAN[j % 2][:, 0:T],
                                                 scalar=mod[:, bass.ds(it * 4 + (j + mod_col(l, 2)), 1)], in1=xk,
                                                 op0=ALU.mult, op1=ALU.add).then_inc(evac[stage], 1)
                dve.drain()
                dve.sem_inc(x_ready, 1)

            def top16(src, vals, idx, spare, after_read=None):
                for t in range(TT):
                    dve.max(vals[t][:, 0:8], src[t])
                dve.drain()
                for t in range(TT):
                    dve.max_index(idx[t][:, 0:8], vals[t][:, 0:8], src[t])
                for t in range(TT):
                    r = dve.match_replace(spare[t], vals[t][:, 0:8], src[t], NEG)
                if after_read is not None:
                    r.then_inc(after_read, 1)
                dve.drain()
                for t in range(TT):
                    dve.max(vals[t][:, 8:16], spare[t])
                dve.drain()
                for t in range(TT):
                    dve.max_index(idx[t][:, 8:16], vals[t][:, 8:16], spare[t])

            def select(l):
                stage = f"peer_q{l}"
                tv = lambda t, j: topv[:, (t * 4 + j) * TOPK:(t * 4 + j + 1) * TOPK]
                ti = lambda t, j: topi[:, (t * 4 + j) * TOPK:(t * 4 + j + 1) * TOPK]

                def body(it, end):
                    for j in range(4):
                        if not (end and j == 3):
                            split_lo(stage, j + 1, 4, it)
                        dve.wait_ge(sc_done, it * 4 + (16 * l + j + 1))
                        dve.sem_inc(sc_seen, 1)
                        top16([SC[j % 2][:, t * P:(t + 1) * P] for t in range(TT)], [tv(t, j) for t in range(TT)],
                              [ti(t, j) for t in range(TT)], [work[:, t * P:(t + 1) * P] for t in range(TT)], sc_used)
                        if j % 2:
                            dve.drain()
                            for t in range(TT):
                                dve.tensor_tensor(
                                    cand[:, t * 256:(t + 1) * 256].rearrange("p (a b) -> p a b", b=TOPK),
                                    tv(t, j - 1).unsqueeze(2).broadcast_to([P, TOPK, TOPK]),
                                    tv(t, j).unsqueeze(1).broadcast_to([P, TOPK, TOPK]), ALU.add)
                            dve.drain()
                            b0 = [(2 * t + j // 2) * TOPK for t in range(TT)]
                            top16([cand[:, t * 256:(t + 1) * 256] for t in range(TT)],
                                  [bestv[:, b:b + TOPK] for b in b0], [bestp[:, b:b + TOPK] for b in b0],
                                  [cwork[:, t * 256:(t + 1) * 256] for t in range(TT)])
                    dve.drain()
                    dve.tensor_copy(top_i[:, :, bass.ds(it * (4 * TOPK), 4 * TOPK)], topi[:].rearrange("p (t n) -> p t n", t=TT))
                    dve.tensor_copy(best_v[:, :, bass.ds(it * (2 * TOPK), 2 * TOPK)], bestv.rearrange("p (t n) -> p t n", t=TT))
                    dve.tensor_copy(best_p[:, :, bass.ds(it * (2 * TOPK), 2 * TOPK)], bestp[:].rearrange("p (t n) -> p t n", t=TT))
                    dve.drain()

                with dve.Fori(0, 3) as it:
                    body(it, False)
                body(3, l == 1)
                hk = lambda a: a.rearrange("p t (h k) -> p (t h) k", k=TOPK)
                bv = hk(best_v[:])
                dve.tensor_tensor(hk(gate[:]), bv, bv[:, :, 0:1].broadcast_to([P, TT * HEADS, TOPK]), ALU.subtract
                                  ).then_inc(gate_in, 1)
                for t in range(TT):
                    dve.tensor_scalar(dec_u[:, 0, :], best_p[:, t, :], 4, None, ALU.logical_shift_right)
                    dve.tensor_scalar(dec_u[:, 1, :], best_p[:, t, :], 15, None, ALU.bitwise_and)
                    dve.tensor_copy(tif, top_i[:, t, :])
                    dve.drain()
                    dve.tensor_copy(dec_f, dec_u[:].rearrange("p x n -> p (x n)"))
                    for x in range(2):
                        dve.drain()
                        e4 = eq.rearrange("p (h k j) -> p h k j", h=HEADS, k=TOPK)
                        place = dec_f[:, x * SEL:(x + 1) * SEL].rearrange("p (h k) -> p h k", k=TOPK)
                        dve.tensor_tensor(e4, place.unsqueeze(3).broadcast_to([P, HEADS, TOPK, TOPK]),
                                          con[:, C_IOTA:C_IOTA + TOPK].unsqueeze(1).unsqueeze(1)
                                          .broadcast_to([P, HEADS, TOPK, TOPK]), ALU.is_equal)
                        dve.drain()
                        key = tif.rearrange("p (h x j) -> p h x j", h=HEADS, x=2)[:, :, x, :]
                        dve.tensor_tensor(e4, e4, key.unsqueeze(2).broadcast_to([P, HEADS, TOPK, TOPK]), ALU.mult)
                        dve.drain()
                        dve.tensor_reduce(eab[:, x * SEL:(x + 1) * SEL], eq.rearrange("p (n j) -> p n j", j=TOPK),
                                          AX.X, ALU.add)
                    dve.drain()
                    dve.scalar_tensor_tensor(out=eid[:, t, :], in0=eab[:, 0:SEL], scalar=float(KEYS),
                                             in1=eab[:, SEL:2 * SEL], op0=ALU.mult, op1=ALU.add)
                dve.drain()
                dve.memset(yrow, 0.0)
                dve.wait_ge(gate_exp, l + 1)
                dve.tensor_reduce(esum, hk(gate[:]), AX.X, ALU.add)
                dve.drain()
                dve.reciprocal(esum, esum)
                dve.drain()
                dve.tensor_tensor(hk(gate[:]), hk(gate[:]), esum.unsqueeze(2).broadcast_to([P, TT * HEADS, TOPK]),
                                  ALU.mult)
                dve.drain()
                dve.sem_inc(sel_done, 1)

            def experts(l):
                dve.wait_ge(hr_copied, 4 * l + 4)
                for t in range(TT):
                    tile = TT * l + t

                    def dot(s, it):
                        for b in range(BLK):
                            dve.wait_ge(u_landed[b], it * 32 + (16 * (tile * (SEL // BLK) + s + 1)))
                            g = gu[:, b * D:(b + 1) * D]
                            dve.tensor_tensor_reduce(out=g, in0=g, in1=hrow[:, t * D:(t + 1) * D], scale=1.0,
                                                     scalar=0.0, op0=ALU.mult, op1=ALU.add,
                                                     accum_out=dots[:, s, b:b + 1]).then_inc(u_used, 1)

                    def add(s, it):
                        dve.wait_ge(s_gelu, it * 2 + (tile * (SEL // BLK) + s + 1))
                        dve.tensor_tensor(coef[:, s, :], coef[:, s, :],
                                          gate[:, t, bass.ds(it * (2 * BLK) + s * BLK, BLK)], ALU.mult)
                        y = yrow[:, t * D:(t + 1) * D]
                        for b in range(BLK):
                            q = s * BLK + b
                            dve.drain()
                            dve.wait_ge(v_landed[q], it * 16 + 16 * (tile * (SEL // (2 * BLK)) + 1))
                            dve.scalar_tensor_tensor(out=y, in0=gv[:, q * D:(q + 1) * D], scalar=coef[:, s, b:b + 1],
                                                     in1=y, op0=ALU.mult, op1=ALU.add).then_inc(v_used, 1)

                    def body(it):
                        dot(0, it)
                        add(1, it - 1)
                        dot(1, it)
                        add(0, it)

                    dot(0, 0)
                    dot(1, 0)
                    add(0, 0)
                    n = SEL // (2 * BLK)
                    if l == 0 and t == 0:
                        with dve.Fori(1, 13) as it:
                            body(it)
                            ada_block(it + 11)
                        with dve.Fori(13, n) as it:
                            body(it)
                    else:
                        with dve.Fori(1, n) as it:
                            body(it)
                    add(1, n - 1)
                for t in range(TT):
                    for g in range(2):
                        dve.wait_ge(yt_done, 4 * l + 2 * t + g + 1)
                        for k in range(4):
                            kk = 4 * g + k
                            xk = xT[:, kk * T + t * P:kk * T + (t + 1) * P]
                            c = mod_col(l, 5) + kk
                            i = dve.scalar_tensor_tensor(out=xk, in0=TR[g][:, k * P:(k + 1) * P],
                                                         scalar=mod[:, c:c + 1], in1=xk, op0=ALU.mult, op1=ALU.add)
                        i.then_inc(yt_added, 1)
                dve.drain()
                dve.sem_inc(x_ready, 1)

            def peer(l):
                normalise(2 * l + 2, l, V_CH + l * KB, 3)
                split_act([3, 7][l], act32[:], KB * T)
                select(l)
                experts(l)

            def reduced(out_ap, shift):
                dve.tensor_scalar(tmp[:], ang[:], 1.0 / TWO_PI, shift / TWO_PI, ALU.mult, ALU.add)
                dve.drain()
                dve.tensor_scalar(tmp[:], tmp[:], ROUND, None, ALU.add)
                dve.drain()
                dve.tensor_scalar(tmp[:], tmp[:], -ROUND, None, ALU.add)
                dve.drain()
                src = ang[:]
                for part in (PI_1, PI_2, PI_3):
                    dve.scalar_tensor_tensor(out=out_ap, in0=tmp[:], scalar=-part, in1=src, op0=ALU.mult, op1=ALU.add)
                    dve.drain()
                    src = out_ap
                dve.tensor_scalar(out_ap, out_ap, shift, None, ALU.add)
                dve.drain()
                return dve.tensor_scalar(out_ap, out_ap, 3.1415925, -3.1415925, ALU.min, ALU.max)

            def rotate(src):
                two = lambda ap: ap.rearrange("p (i t) -> p i t", t=T)
                cs = cosb[:].unsqueeze(1).broadcast_to([P, 2, T])
                sn = sinb[:].unsqueeze(1).broadcast_to([P, 2, T])
                a, b = two(src[:, 0:2 * T]), two(src[:, 2 * T:4 * T])
                t1, t2 = act32[:, 512:1024], act32[:, 1024:1536]
                for o, (m1, m2, op) in enumerate(((cs, sn, ALU.subtract), (sn, cs, ALU.add))):
                    dve.tensor_tensor(two(t1), a, m1, ALU.mult)
                    dve.tensor_tensor(two(t2), b, m2, ALU.mult)
                    dve.drain()
                    i = dve.tensor_tensor(rot[:, o * 2 * T:(o + 1) * 2 * T], t1, t2, op)
                    dve.drain()
                return i

            def attention():
                normalise(3, 1, V_TOK + KB, 0)
                split_act(4, act32[:], KB * T)
                dve.sem_inc(evac["mla_in"], 2)
                for j in range(7):
                    split_lo("mla_in", j + 1, width=D if j < 6 else 2 * Q_LORA)
                    wait_product("mla_in", j)
                    dst = lat[:, j * T:(j + 1) * T] if j < 5 else kraw[:, (j - 5) * T:(j - 4) * T]
                    i = dve.tensor_copy(dst, PAN[j % 2][:, 0:T])
                    i.then_inc(evac["mla_in"], 1)
                dve.drain()
                dve.sem_inc(lat_in, 1)
                dve.wait_ge(lat_rms, 1)
                dve.reciprocal(rstd[:], rms[:])
                dve.drain()
                for k in range(5):
                    r = rstd[:, 0:T] if k < QB else rstd[:, T:2 * T]
                    c = V_QA + k
                    lk = lat[:, k * T:(k + 1) * T]
                    i = dve.scalar_tensor_tensor(out=lk, in0=lk, scalar=vec[:, c:c + 1], in1=r, op0=ALU.mult,
                                                 op1=ALU.mult)
                i.then_inc(f32_ready, 1)
                split_act(5, lat, 5 * T)
                dve.sem_inc(evac["q_b"], 2)
                for j in range(6):
                    split_lo("q_b", j + 1, width=2 * Q_LORA if j < 5 else 2 * KV_LORA)
                    wait_product("q_b", j)
                    dve.tensor_copy(arena[:, j * 2 * T:(j + 1) * 2 * T], PAN[j % 2][:]).then_inc(evac["q_b"], 1)
                dve.sem_inc(evac["k_b"], 2)
                for j in range(4):
                    split_lo("k_b", j + 1, width=2 * KV_LORA if j < 3 else D)
                    wait_product("k_b", j)
                    dve.tensor_copy(kn[:, j * 2 * T:(j + 1) * 2 * T], PAN[j % 2][:]).then_inc(evac["k_b"], 1)
                split_lo("v_b", 1)
                wait_product("v_b", 1)
                for n, bank in enumerate((SC[0], SC[1], TR[0], TR[1])):
                    i = dve.tensor_copy(vv[:, n * 512:(n + 1) * 512], bank[:])
                i.then_inc(v_copied, 1)
                split_lo("mla_out", 0)
                dve.wait_ge(trig, 1)
                for i in range(8):
                    dve.wait_ge(head_rms, i + 1)
                    dve.reciprocal(rstd[:], rms[:]).then_inc(head_rstd, 1)
                    dve.drain()
                    for e in range(2):
                        h = 2 * (i % 4) + e
                        base, g = (qn, V_QN) if i < 4 else (kn, V_KN)
                        hd = base[:, h * T:(h + 1) * T]
                        dve.scalar_tensor_tensor(out=hd, in0=hd, scalar=vec[:, g:g + 1], in1=rstd[:, e * T:(e + 1) * T],
                                                 op0=ALU.mult, op1=ALU.mult)
                        r = slice(32 * (h % 4), 32 * (h % 4) + 32)
                        for x in range(2):
                            c = slice((2 * x + h // 4) * T, (2 * x + h // 4 + 1) * T)
                            src = qr[r, c] if i < 4 else kraw[r, x * T:(x + 1) * T]
                            dst = qr[r, c] if i < 4 else kr[r, c]
                            dve.scalar_tensor_tensor(out=dst, in0=src, scalar=vec[r, g + 1 + x:g + 2 + x],
                                                     in1=rstd[r, e * T:(e + 1) * T], op0=ALU.mult, op1=ALU.mult)
                    dve.drain()
                    if i == 3:
                        rotate(qr)
                        for h in range(HEADS):
                            z = qz[:, 2 * h * T:(2 * h + 2) * T].rearrange("p (x t) -> p x t", t=T)
                            src = rot.rearrange("p (x i t) -> p x i t", x=2, t=T)[:, :, h // 4, :]
                            c = C_ROWCOL + h % 4
                            dve.tensor_scalar(z, src, con[:, c:c + 1], None, ALU.mult)
                        dve.drain()
                rotate(kr)
                dve.sem_inc(qk_ready, 1)
                for i in range(HEADS + 2):
                    if i < HEADS:
                        h = i
                        dve.wait_ge(s_done, h + 1)
                        dve.tensor_tensor(s_sb[:, h % 2, :], SC[h % 2][:, 0:384], con[:, C_MASK:C_MASK + 384], ALU.add)
                        dve.drain()
                        for t, (c0, c1) in enumerate(((0, P), (P, 3 * P))):
                            dve.tensor_reduce(smax[:, h % 2, t:t + 1], s_sb[:, h % 2, c0:c1], AX.X, ALU.max)
                        dve.drain()
                        dve.tensor_scalar(smax[:, h % 2, :], smax[:, h % 2, :], -float(QK_HEAD) ** -0.5, None, ALU.mult
                                          ).then_inc(s_masked, 1)
                    if 1 <= i <= HEADS:
                        h = i - 1
                        dve.wait_ge(p_exp, h + 1)
                        dve.reciprocal(ssum[:, h % 2, :], ssum[:, h % 2, :])
                        dve.drain()
                        for t, (c0, c1) in enumerate(((0, P), (P, 3 * P))):
                            n = dve.tensor_scalar(s_sb[:, h % 2, c0:c1], s_sb[:, h % 2, c0:c1],
                                                  ssum[:, h % 2, t:t + 1], None, ALU.mult)
                        n.then_inc(p_norm, 1)
                    if i >= 2:
                        h = i - 2
                        dve.wait_ge(o_done, h + 1)
                        dve.tensor_copy(act32[:, h * T:(h + 1) * T], (OV, STAT)[h % 2][:, 0:T]).then_inc(o_copied, 1)
                dve.drain()
                dve.sem_inc(f32_ready, 1)
                split_act(6, act32[:], KB * T)
                add_to_x("mla_out", 1, 3)

            dve.memset(eps[:], EPS)
            dve.memset(u_pad[:, 0:2], 0.0).then_inc(s_eps, 1)
            dve.sem_inc(lo_done, RAW)
            dve.sem_inc(ada_used, ADA)
            dve.sem_inc(sc_used, 2)
            dve.sem_inc(u_used, BLK)
            dve.sem_inc(v_used, 2 * BLK)
            dve.wait_ge(s_const, 80)
            dve.tensor_copy(ang[:], posi[:])
            dve.drain()
            dve.tensor_scalar(ang[:], ang[:], con[:, C_FREQ:C_FREQ + 1], None, ALU.mult)
            dve.drain()
            reduced(sinb[:], 0.0)
            dve.drain()
            reduced(cosb[:], np.pi / 2).then_inc(trig_in, 1)
            dve.wait_ge(s_silu, 1)
            with dve.Fori(0, 4) as it:
                ada_block(it)
            normalise(1, 0, V_TOK, 0)
            split_act(1, act32[:], KB * T)
            split_lo("conv_in", 0)
            dve.sem_inc(evac["conv_in"], 2)
            with dve.Fori(0, 2) as it:
                for b in range(4):
                    split_lo("conv_in", 3 * b + 1, 12, it)
                    wait_product("conv_in", 3 * b, 12, it)
                    dve.tensor_copy(c_sb, PAN[3 * b % 2][:, 0:T]).then_inc(evac["conv_in"], 1)
                    split_lo("conv_in", 3 * b + 2, 12, it)
                    dve.drain()
                    wait_product("conv_in", 3 * b + 1, 12, it)
                    dve.tensor_tensor(u_pad[:, 2:2 + T], PAN[(3 * b + 1) % 2][:, 0:T], c_sb, ALU.mult
                                      ).then_inc(evac["conv_in"], 1)
                    split_lo("conv_in", 3 * b + 3, 12, it)
                    dve.drain()
                    tap = lambda i: vec[:, bass.ds(it * 4 + (V_CONV + i * KB + b), 1)]
                    dve.tensor_scalar(conv_t, u_pad[:, 0:T], tap(0), None, ALU.mult)
                    for i in (1, 2):
                        dve.drain()
                        dve.scalar_tensor_tensor(out=conv_t, in0=u_pad[:, i:i + T], scalar=tap(i), in1=conv_t,
                                                 op0=ALU.mult, op1=ALU.add)
                    dve.drain()
                    wait_product("conv_in", 3 * b + 2, 12, it)
                    dve.tensor_tensor(act32[:, bass.ds((it * 4 + b) * T, T)], PAN[(3 * b + 2) % 2][:, 0:T], conv_t,
                                      ALU.mult).then_inc(evac["conv_in"], 1)
                    ada_block(it * 4 + (4 + b))
            dve.sem_inc(f32_ready, 1)
            split_act(2, act32[:], KB * T)
            add_to_x("conv_out", 0, 1)
            peer(0)
            attention()
            peer(1)


def shape_constants():
    con = np.zeros((P, C_N), np.float32)
    con[:, C_ID:C_ID + P] = np.eye(P)
    con[:, C_ONE:C_ONE + P] = 1.0
    tri = np.where(np.arange(P)[:, None] >= np.arange(P)[None, :], 0.0, -1.0e30)
    con[:, C_MASK:C_MASK + P] = tri
    con[:, C_MASK + 2 * P:C_MASK + 3 * P] = tri
    for j in range(4):
        con[32 * j:32 * j + 32, C_ROW + j * P:C_ROW + (j + 1) * P] = 1.0
        con[32 * j:32 * j + 32, C_ROWCOL + j] = 1.0
    con[:, C_IOTA:C_IOTA + TOPK] = np.arange(TOPK)
    freq = np.float32(10000.0) ** (-np.arange(0, ROPE, 2, dtype=np.float32) / np.float32(ROPE))
    con[:, C_FREQ] = np.tile(freq.astype(np.float32), 4)
    return con


def kernel(x, c, positions, tok_norm, ch_norm, ada_w, ada_b, conv_in_w, conv_w, conv_out_w,
           mla_in_w, q_a_norm, kv_a_norm, q_b_w, kv_b_w, q_norm, k_norm, mla_out_w,
           peer_q_w, peer_subkeys, peer_u, peer_v):
    import concourse.bacc as bacc
    from concourse.bass_utils import run_bass_kernel_spmd

    def cols(v):
        return np.ascontiguousarray(v).reshape(-1, P).T

    def panels(w):
        k, n = w.shape[0] // P, w.shape[1] // P
        return w.reshape(k, P, n, P).transpose(2, 1, 0, 3).reshape(n, P, k * P)

    def packed(p, per):
        n, _, w = p.shape
        out = np.zeros((n // per, P, D), p.dtype)
        out[:, :, 0:per * w] = p.reshape(n // per, per, P, w).transpose(0, 2, 1, 3).reshape(n // per, P, per * w)
        return out

    g = [np.asarray(a) for a in (x, c, positions, tok_norm, ch_norm, ada_w, ada_b, conv_in_w, conv_w, conv_out_w,
                                 mla_in_w, q_a_norm, kv_a_norm, q_b_w, kv_b_w, q_norm, k_norm, mla_out_w,
                                 peer_q_w, peer_subkeys, peer_u, peer_v)]
    (x, c, positions, tok_norm, ch_norm, ada_w, ada_b, conv_in_w, conv_w, conv_out_w, mla_in_w, q_a_norm,
     kv_a_norm, q_b_w, kv_b_w, q_norm, k_norm, mla_out_w, peer_q_w, peer_subkeys, peer_u, peer_v) = g

    ci = panels(conv_in_w[0])
    conv_in = np.stack([ci[KB:2 * KB], ci[2 * KB:3 * KB], ci[0:KB]], 1).reshape(3 * KB, P, D)
    lora = Q_LORA + KV_LORA
    rope_in = [np.tile(mla_in_w[0][:, lora + h * HALF_ROPE:lora + (h + 1) * HALF_ROPE], (1, 4)) for h in range(2)]
    mla_in = panels(np.concatenate([mla_in_w[0][:, 0:lora]] + rope_in, 1))
    qb = q_b_w[0].reshape(Q_LORA, HEADS, QK_HEAD)
    qcols = [qb[:, :, 0:NOPE], qb[:, :, NOPE:NOPE + HALF_ROPE], qb[:, :, NOPE + HALF_ROPE:]]
    q_b = packed(panels(np.concatenate([a.reshape(Q_LORA, -1) for a in qcols], 1)), 2)
    kvb = kv_b_w[0].reshape(KV_LORA, HEADS, NOPE + VH)
    k_b = packed(panels(np.ascontiguousarray(kvb[:, :, 0:NOPE]).reshape(KV_LORA, -1)), 2)
    v_b = np.ascontiguousarray(kvb[:, :, NOPE:]).reshape(KVB, P, D)
    stages = [conv_in, panels(conv_out_w[0]), panels(peer_q_w[0]), mla_in, q_b, k_b, v_b, panels(mla_out_w[0]),
              panels(peer_q_w[1])]
    ropes = lambda v: [np.tile(v[NOPE + h * HALF_ROPE:NOPE + (h + 1) * HALF_ROPE], 4)[:, None] for h in range(2)]
    vec = np.concatenate(
        [cols(tok_norm), cols(ch_norm), cols(ada_b), cols(conv_w[0]), cols(q_a_norm), cols(kv_a_norm),
         cols(q_norm[0][0:NOPE])] + ropes(q_norm[0]) + [cols(k_norm[0][0:NOPE])] + ropes(k_norm[0]), 1)
    vec = np.pad(vec, ((0, 0), (0, V_N - vec.shape[1])))
    arrays = {
        "xT": x[0].T.reshape(KB, P, T).transpose(1, 0, 2).reshape(P, KB * T),
        "c": c[0],
        "positions": positions[0],
        "vectors": vec,
        "constants": shape_constants(),
        "ada_rows": ada_w.transpose(0, 2, 1).reshape(96, P, D),
        "panels": np.concatenate(stages, 0),
        "subkeys": peer_subkeys.reshape(2, PAIRS, KEYS, P).transpose(0, 3, 1, 2).reshape(2, P, PAIRS * KEYS),
        "u0": peer_u[0], "u1": peer_u[1],
        "v0": peer_v[0], "v1": peer_v[1],
    }
    arrays = {n: np.ascontiguousarray(a) for n, a in arrays.items()}
    nc = bacc.Bacc("TRN2", target_bir_lowering=False, num_devices=1)
    ins = [nc.dram_tensor("in_" + n, a.shape, mybir.dt.from_np(a.dtype), kind="ExternalInput").ap() for n, a in arrays.items()]
    out = nc.dram_tensor("out", (P, KB * T), F32, kind="ExternalOutput").ap()
    program(nc, *ins, out)
    got = run_bass_kernel_spmd(nc, [{"in_" + n: a for n, a in arrays.items()}], core_ids=[0]).results[0]["out"]
    return np.ascontiguousarray(got.reshape(P, KB, T).transpose(1, 0, 2).reshape(D, T).T)[None]
```

```python
from contextlib import ExitStack

import numpy as np

import concourse.bass as bass
from concourse import mybir

F32 = mybir.dt.float32
F32R = mybir.dt.float32r
BF16 = mybir.dt.bfloat16
F16 = mybir.dt.float16
U32 = mybir.dt.uint32
I32 = mybir.dt.int32
ALU = mybir.AluOpType
ACT = mybir.ActivationFunctionType
AX = mybir.AxisListType

P = 128
D = 1024
KB = D // P
T = 256
TT = T // P
HEADS = 8
Q_LORA, KV_LORA, ROPE, NOPE, VH = 384, 256, 64, 128, 128
HALF_ROPE = ROPE // 2
QB, KVB = Q_LORA // P, KV_LORA // P
KEYS, TOPK = 128, 16
PAIRS = 2 * HEADS
SEL = HEADS * TOPK
EPS = 1e-6
QK_HEAD = NOPE + ROPE
RAW = 4
HI, LO = 4, 2
HI_LEAD = HI - 1
ADA = 8
QUART = KEYS // 4
AHEAD = QUART
GT = 16
GROUPS = T // GT
G_SCALE = 2.0 ** 14
NEG = -3.0e38

C_ID, C_ONE, C_MASK, C_ROW, C_IOTA, C_ROWCOL, C_FREQ = 0, 128, 256, 640, 1152, 1168, 1172
C_N = 1176
V_TOK, V_CH, V_ADAB, V_CONV, V_QA, V_KVA, V_QN, V_KN = 0, 16, 32, 128, 152, 155, 157, 160
V_N = 164

STAGES = [("conv_in", 24), ("conv_out", 8), ("sel0", 32), ("ahead0", 16), ("mix0", 192), ("last0", 32),
          ("mla_in", 7), ("q_b", 6), ("k_b", 4), ("v_b", 2), ("mla_out", 8),
          ("sel1", 32), ("ahead1", 16), ("mix1", 192), ("last1", 32)]
DENSE, _d = {}, 0
for _name, _count in [("conv_in", 24), ("conv_out", 8), ("peer_q0", 16), ("mla_in", 7), ("q_b", 6), ("k_b", 4),
                      ("v_b", 2), ("mla_out", 8), ("peer_q1", 16)]:
    DENSE[_name] = _d
    _d += _count
BASE, _n = {}, 0
for _name, _count in STAGES:
    BASE[_name] = _n
    _n += _count
WIDTHS = {BASE["q_b"] + _j: 2 * Q_LORA for _j in range(6)} | {BASE["k_b"] + _j: 2 * KV_LORA for _j in range(4)}
TWO_PI = 2.0 * np.pi
PI_1 = 6.28125
PI_2 = float(np.float32(np.floor((TWO_PI - PI_1) * 2.0 ** 21) / 2.0 ** 21))
PI_3 = float(np.float32(TWO_PI - PI_1 - PI_2))
ROUND = 12582912.0


def program(nc, xT_in, c_in, pos_in, vec_in, con_in, ada_in, pan_in, key_in, iota_in, u_in, v_in, out):
    ctx = ExitStack()
    with ctx:
        def sb(name, shape, dt=F32):
            return ctx.enter_context(nc.sbuf_tensor(name, shape, dt))

        def sem(name):
            return ctx.enter_context(nc.semaphore(name))

        xT = sb("xT", [P, KB * T])
        con = sb("con", [P, C_N])
        vec = sb("vec", [P, V_N])
        eps = sb("eps", [P, 1])
        crow = sb("crow", [P, D])
        mod = sb("mod", [P, 96])
        ada_sum = sb("ada_sum", [P, 4])
        gain = sb("gain", [P, KB])
        raw = sb("raw", [P, RAW, D])
        w_hi = sb("w_hi", [P, HI, D], F32R)
        w_lo = sb("w_lo", [P, LO, D], F32R)
        act_hi = sb("act_hi", [P, KB * T], F32R)
        act_lo = sb("act_lo", [P, KB * T], F32R)
        ada1 = sb("ada1", [P, D])
        arena = sb("arena", [P, 2 * QUART * T])
        ring_g = sb("ring_g", [P, AHEAD * T])
        iota_x = sb("iota_x", [P, KEYS * GT], BF16)
        ia_t = sb("ia_t", [P, T], BF16)
        ib_t = sb("ib_t", [P, T], BF16)
        g32_t = sb("g32_t", [P, T])
        gh_t = sb("gh_t", [P, T], F16)
        gl_t = sb("gl_t", [P, T], F16)
        hot_b = sb("hot_b", [P, 2, KEYS * GT], BF16)
        hot_a = sb("hot_a", [P, 2, QUART * GT], BF16)
        hot_gh = sb("hot_gh", [P, 2, QUART * GT], F16)
        hot_gl = sb("hot_gl", [P, 2, QUART * GT], F16)
        w32 = sb("w32", [P, 2 * T])
        wt_hi = sb("wt_hi", [P, 2, 2 * T], F32R)
        wt_lo = sb("wt_lo", [P, 2, 2 * T], F32R)
        zero = sb("zero", [P, P], F32R)
        act32 = ring_g[:, 0:2048]
        s_sb = ring_g[:, 2048:2816].rearrange("p (e n) -> p e n", e=2)
        pT = ring_g[:, 2816:3584].rearrange("p (e n) -> p e n", e=2)
        cosb = ring_g[:, 3584:3840]
        sinb = ring_g[:, 3840:4096]
        rms = ring_g[:, 4096:4608]
        rstd = ring_g[:, 4608:5120]
        q_sb = ring_g[:, 5120:5632].rearrange("p (e n) -> p e n", e=2)
        top_i = ring_g[:, 5632:6144].bitcast(U32).rearrange("p (t n) -> p t n", t=TT)
        best_v = ring_g[:, 6144:6400].rearrange("p (t n) -> p t n", t=TT)
        best_p = ring_g[:, 6400:6656].bitcast(U32).rearrange("p (t n) -> p t n", t=TT)
        gate = ring_g[:, 6656:6912].rearrange("p (t n) -> p t n", t=TT)
        topi = ring_g[:, 6912:6976].bitcast(U32)
        bestp = ring_g[:, 6976:7008].bitcast(U32)
        dec_u = ring_g[:, 7040:7296].bitcast(U32).rearrange("p (x n) -> p x n", x=2)
        ang = ring_g[:, 7296:7552]
        tmp = ring_g[:, 7552:7808]
        posi = ring_g[:, 7808:8064].bitcast(I32)

        ada = arena[:, 8192:8192 + ADA * D].rearrange("p (a d) -> p a d", d=D)
        sq = arena[:, 0:2048]
        c_sb = arena[:, 2048:2048 + T]
        u_pad = arena[:, 2560:2560 + T + 2]
        conv_t = arena[:, 3072:3072 + T]
        qn = arena[:, 0:2048]
        qr = arena[:, 2048:3072]
        kn = arena[:, 3072:5120]
        kr = arena[:, 5120:6144]
        vv = arena[:, 6144:8192]
        sqn = arena[:, 8192:10240]
        sqr = arena[:, 10240:11264]
        rot = arena[:, 11264:12288]
        qz = arena[:, 12288:16384]
        kraw = act32[:, 0:512]
        lat = act32[:, 512:512 + 5 * T]
        smax = sb("smax", [P, 2, 2])
        ssum = sb("ssum", [P, 2, 2])
        topv = arena[:, 0:TT * 2 * TOPK]
        work = arena[:, 256:256 + TT * P]
        cand = arena[:, 512:512 + TT * 256]
        cwork = arena[:, 1024:1024 + TT * 256]
        bestv = arena[:, 1536:1536 + TT * TOPK]
        dec_f = arena[:, 2048:2048 + 2 * SEL]
        tif = arena[:, 2560:2560 + PAIRS * TOPK]
        eq = arena[:, 4096:4096 + SEL * TOPK]
        eab = arena[:, 6144:6144 + TT * 2 * SEL]
        esum = arena[:, 6656:6656 + 16]
        keys = arena[:, 8192:8192 + PAIRS * KEYS]
        yrow = arena[:, 0:TT * D]

        ps = [ctx.enter_context(nc.psum_tensor(f"bank{b}", [P, 512], F32)) for b in range(8)]
        PAN = ps[0:2]
        STAT = ps[2]
        SC = ps[3:5]
        TR = ps[5:7]
        OV = ps[7]
        YB = ps[2:6]
        GB = ps[6:8]

        ident = con[:, C_ID:C_ID + P]
        ones = con[:, C_ONE:C_ONE + P]

        s_const = sem("constants_landed")
        s_eps = sem("eps_set")
        s_key = sem("subkeys_landed")
        s_out = sem("output_stored")
        s_pos = sem("positions_landed")
        landed = [sem(f"panel_landed{i}") for i in range(RAW)]
        hi_done = sem("panel_hi_ready")
        lo_done = sem("panel_lo_ready")
        pan_done = sem("panel_multiplied")
        evac = {n: sem(f"evacuated_{n}") for n, _ in STAGES}
        ada_landed = [sem(f"ada_landed{i}") for i in range(ADA)]
        ada_used = sem("ada_rows_used")
        ada1_landed = sem("ada1_landed")
        ada1_used = sem("ada1_used")
        ada_seen = sem("ada_slot_seen_free")
        s_silu = sem("silu_c_ready")
        x_ready = sem("x_ready")
        sq_ready = sem("squares_ready")
        sum_ready = sem("square_sums_ready")
        rms_ready = sem("rms_ready")
        f32_ready = sem("activations_f32_ready")
        act_hi_ready = sem("activations_hi_ready")
        act_ready = sem("activations_split")
        sc_done = sem("key_scores_ready")
        sc_used = sem("key_scores_used")
        sc_seen = sem("key_scores_seen")
        gate_in = sem("gate_exponents_ready")
        gate_exp = sem("gate_exp_ready")
        dec_done = sem("chosen_experts_decoded")
        idx_done = sem("chosen_experts_turned")
        hot_ready = sem("one_hots_ready")
        g_done = sem("gates_scattered")
        g_read = sem("gates_copied")
        pan_read = [sem(f"bank_read{l}") for l in range(2)]
        w_mul = sem("weighted_gelu_ready")
        wt_hi_ready = sem("weighted_gelu_hi")
        wt_ready = sem("weighted_gelu_split")
        y_copied = sem("y_rows_ready")
        yt_done = sem("y_transposed")
        yt_added = sem("y_added")
        lat_in = sem("latents_copied")
        lat_sq = sem("latent_squares")
        lat_sum = sem("latent_sums")
        lat_rms = sem("latent_rms")
        v_mul = sem("values_multiplied")
        v_copied = sem("values_copied")
        head_sq = sem("head_squares")
        head_sum = sem("head_sums")
        head_rms = sem("head_rms")
        head_rstd = sem("head_rstd")
        trig_in = sem("angles_reduced")
        trig = sem("sin_cos_ready")
        qk_ready = sem("qk_ready")
        s_done = sem("scores_ready")
        s_masked = sem("scores_masked")
        p_exp = sem("probs_exp")
        p_norm = sem("probs_normalised")
        p_tr = sem("probs_transposed")
        p_copied = sem("probs_copied")
        o_done = sem("head_output_ready")
        o_copied = sem("head_output_copied")

        block = ctx.enter_context(nc.Block())

        def ring(stage, j, unroll=0, it=0):
            i = BASE[stage] + j
            step = unroll // RAW * 16
            return i % RAW, i % LO, it * step + 16 * (i // RAW + 1), it * unroll + (i + 1)

        @block.sync
        def _(sp):
            def load(src, index, stage, j, unroll=0, it=0, width=D):
                slot, _, _, n = ring(stage, j, unroll, it)
                sp.wait_ge(lo_done, n)
                sp.dma_start(raw[:, slot, 0:width], src[bass.ds(index, 1), :, 0:width].rearrange("o p n -> p (o n)")
                             ).then_inc(landed[slot], 16)

            def load_panel(stage, j, unroll=0, it=0, width=D):
                load(pan_in, it * unroll + (DENSE[stage] + j), stage, j, unroll, it, width)

            def load_experts(l):
                k0 = KEYS * l
                with sp.Fori(0, 8) as it:
                    for p in range(2):
                        load(pan_in, it * 2 + (DENSE[f"peer_q{l}"] + p), f"sel{l}", 2 * p, 4, it)
                        load(u_in, it * 2 + (k0 + p), f"sel{l}", 2 * p + 1, 4, it)
                with sp.Fori(0, 4) as it:
                    for j in range(4):
                        load(u_in, it * 4 + (k0 + 16 + j), f"ahead{l}", j, 4, it)
                for q in range(3):
                    with sp.Fori(0, 8) as it:
                        for e in range(4):
                            v = k0 + q * QUART + e
                            load(u_in, it * 4 + (v + AHEAD), f"mix{l}", 64 * q + 2 * e, 8, it)
                            load(v_in, it * 4 + v, f"mix{l}", 64 * q + 2 * e + 1, 8, it)
                with sp.Fori(0, 8) as it:
                    for j in range(4):
                        load(v_in, it * 4 + (k0 + 3 * QUART + j), f"last{l}", j, 4, it)

            sp.dma_start(crow[:], c_in.partition_broadcast(P)).then_inc(s_const, 16)
            sp.dma_start(vec[:], vec_in).then_inc(s_const, 16)
            sp.dma_start(xT[:], xT_in).then_inc(s_const, 16)
            sp.dma_start(con[:], con_in).then_inc(s_const, 16)
            sp.dma_start(iota_x[:], iota_in).then_inc(s_const, 16)
            with sp.Fori(0, 2) as it:
                for j in range(12):
                    load_panel("conv_in", j, 12, it)
            with sp.Fori(0, 2) as it:
                for j in range(4):
                    load_panel("conv_out", j, 4, it)
            sp.wait_ge(ada_used, 48 + ADA)
            sp.dma_start(keys, key_in[0]).then_inc(s_key, 16)
            load_experts(0)
            for j in range(RAW):
                load_panel("mla_in", j)
            sp.wait_ge(x_ready, 2)
            sp.dma_start(posi, pos_in.partition_broadcast(P)).then_inc(s_pos, 16)
            for j in range(RAW, 7):
                load_panel("mla_in", j)
            for j in range(6):
                load_panel("q_b", j, width=2 * Q_LORA)
            for j in range(4):
                load_panel("k_b", j, width=2 * KV_LORA)
            for j in range(2):
                load_panel("v_b", j)
            with sp.Fori(0, 2) as it:
                for j in range(4):
                    load_panel("mla_out", j, 4, it)
            sp.wait_ge(act_ready, 6)
            sp.dma_start(keys, key_in[1]).then_inc(s_key, 16)
            load_experts(1)
            sp.wait_ge(x_ready, 4)
            sp.dma_start(out, xT[:]).then_inc(s_out, 16)
            sp.wait_ge(s_out, 16)

        @block.tensor
        def _(pe):
            def product(bank, slots, col0, kb, act0):
                for k in range(kb):
                    w = slice(col0 + k * P, col0 + (k + 1) * P)
                    a = slice((act0 + k) * T, (act0 + k + 1) * T)
                    pe.matmul(bank, w_hi[:, slots[0], w], act_hi[:, a], start=(k == 0), stop=False)
                    pe.matmul(bank, w_hi[:, slots[0], w], act_lo[:, a], start=False, stop=False)
                    last = pe.matmul(bank, w_lo[:, slots[1], w], act_hi[:, a], start=False, stop=(k == kb - 1))
                return last

            def wait_panel(stage, j, unroll=0, it=0):
                slots = wait_split(stage, j, unroll, it)
                pe.wait_ge(evac[stage], it * unroll + (j + 1))
                return slots

            def full_panel(stage, j, unroll=0, it=0):
                slots = wait_panel(stage, j, unroll, it)
                product(PAN[j % 2][:, 0:T], slots, 0, KB, 0).then_inc(pan_done, 1)

            def square_sums(n):
                pe.wait_ge(sq_ready, n)
                for k in range(KB):
                    mm = pe.matmul(STAT[:, 0:T], ones, sq[:, k * T:(k + 1) * T], start=(k == 0), stop=(k == KB - 1))
                mm.then_inc(sum_ready, 1)

            def wait_split(stage, j, unroll, it):
                slot, lo_slot, _, n = ring(stage, j, unroll, it)
                pe.wait_ge(lo_done, n + RAW)
                return slot, lo_slot

            def u_panel(l, stage, j, unroll, it, nth, bank):
                slots = wait_split(stage, j, unroll, it)
                pe.wait_ge(pan_read[l], nth)
                product(bank[:, 0:T], slots, 0, KB, 0).then_inc(pan_done, 1)

            def v_panel(stage, j, unroll, it, par, e):
                slots = wait_split(stage, j, unroll, it)
                for t in range(TT):
                    a = slice(e * T + t * P, e * T + (t + 1) * P)
                    for wt, parts in ((wt_hi, (0, 1)), (wt_lo, (0,))):
                        for v in parts:
                            for n in range(2):
                                mm = pe.matmul(YB[2 * t + n][:], wt[:, par, a], (w_hi, w_lo)[v][:, slots[v], n * 512:(n + 1) * 512],
                                               start=False, stop=False, skip_group_check=True)
                mm.then_inc(pan_done, 1)

            def scatter(l, par, count):
                pe.wait_ge(hot_ready, count)
                pe.wait_ge(g_read, count)
                hb = hot_b[:, par, :].rearrange("p (b t) -> p b t", t=GT)
                for t in range(GT):
                    o = GB[par][:, t * QUART:(t + 1) * QUART]
                    for part in (hot_gh, hot_gl):
                        mm = pe.matmul(o, hb[:, :, t], part[:, par, :].rearrange("p (a t) -> p a t", t=GT)[:, :, t],
                                       start=(part is hot_gh), stop=(part is hot_gl))
                mm.then_inc(g_done, 1)

            def peer(l):
                square_sums(2 * l + 2)
                pe.wait_ge(act_ready, [3, 7][l])
                pe.wait_ge(s_key, 16 * (l + 1))
                with pe.Fori(0, 8) as it:
                    for p in range(2):
                        u_panel(l, f"sel{l}", 2 * p, 4, it, it * 4 + (2 * p + 1), PAN[0])
                        u_panel(l, f"sel{l}", 2 * p + 1, 4, it, it * 4 + (2 * p + 2), PAN[1])
                        pe.wait_ge(pan_read[l], it * 4 + (2 * p + 3))
                        pe.wait_ge(sc_used, it * 2 + (16 * l + p + 1))
                        for t in range(TT):
                            mm = pe.matmul(SC[p][:, t * P:(t + 1) * P], q_sb[:, p, t * P:(t + 1) * P],
                                           keys[:, bass.ds((it * 2 + p) * KEYS, KEYS)], start=True, stop=True)
                        mm.then_inc(sc_done, 1)
                for t in range(TT):
                    pe.wait_ge(dec_done, TT * l + t + 1)
                    for n, src in enumerate((eab[:, (2 * t) * SEL:(2 * t + 1) * SEL],
                                             eab[:, (2 * t + 1) * SEL:(2 * t + 2) * SEL], gate[:, t, :])):
                        mm = pe.transpose(GB[t][:, n * P:(n + 1) * P], src, ident)
                    mm.then_inc(idx_done, 1)
                with pe.Fori(0, 4) as it:
                    for j in range(4):
                        scatter(l, j % 2, it * 4 + (64 * l + j + 1))
                        u_panel(l, f"ahead{l}", j, 4, it, it * 4 + (33 + j), PAN[j % 2])
                for n in range(4):
                    pe.matmul(YB[n][:], zero[:], act_hi[:, 0:512], start=True, stop=False, skip_group_check=True)
                for q in range(3):
                    with pe.Fori(0, 8) as it:
                        for s in range(2):
                            j = 64 * q + 4 * s
                            u_panel(l, f"mix{l}", j, 8, it, it * 4 + (49 + 32 * q + 2 * s), PAN[0])
                            pe.wait_ge(wt_ready, it * 2 + (64 * l + 16 * q + s + 1))
                            v_panel(f"mix{l}", j + 1, 8, it, s, 0)
                            u_panel(l, f"mix{l}", j + 2, 8, it, it * 4 + (50 + 32 * q + 2 * s), PAN[1])
                            scatter(l, s, it * 2 + (64 * l + 16 * (q + 1) + s + 1))
                            v_panel(f"mix{l}", j + 3, 8, it, s, 1)
                with pe.Fori(0, 8) as it:
                    for s in range(2):
                        pe.wait_ge(wt_ready, it * 2 + (64 * l + 48 + s + 1))
                        v_panel(f"last{l}", 2 * s, 4, it, s, 0)
                        v_panel(f"last{l}", 2 * s + 1, 4, it, s, 1)
                pe.wait_ge(y_copied, l + 1)
                for t in range(TT):
                    for g in range(2):
                        if 2 * t + g >= 2:
                            pe.wait_ge(yt_added, 4 * l + 2 * t + g - 1)
                        for k in range(4):
                            o = t * D + (4 * g + k) * P
                            mm = pe.transpose(GB[g][:, k * P:(k + 1) * P], yrow[:, o:o + P], ident)
                        mm.then_inc(yt_done, 1)
                pe.wait_ge(yt_added, 4 * l + 4)

            def attention():
                square_sums(3)
                pe.wait_ge(act_ready, 4)
                for j in range(7):
                    full_panel("mla_in", j)
                pe.wait_ge(lat_sq, 1)
                for k in range(QB):
                    pe.matmul(STAT[:, 0:T], ones, sqn[:, k * T:(k + 1) * T], start=(k == 0), stop=(k == QB - 1))
                for k in range(KVB):
                    mm = pe.matmul(STAT[:, T:2 * T], ones, sqn[:, (QB + k) * T:(QB + k + 1) * T],
                                   start=(k == 0), stop=(k == KVB - 1))
                mm.then_inc(lat_sum, 1)
                pe.wait_ge(act_ready, 5)
                for j in range(6):
                    slots = wait_panel("q_b", j)
                    product(PAN[j % 2][:, 0:T], slots, 0, QB, 0)
                    product(PAN[j % 2][:, T:2 * T], slots, Q_LORA, QB, 0).then_inc(pan_done, 1)
                for j in range(4):
                    slots = wait_panel("k_b", j)
                    product(PAN[j % 2][:, 0:T], slots, 0, KVB, QB)
                    product(PAN[j % 2][:, T:2 * T], slots, KV_LORA, KVB, QB).then_inc(pan_done, 1)
                hi_slots, lo_slots = zip(*[ring("v_b", k)[0:2] for k in range(KVB)])
                pe.wait_ge(lo_done, ring("v_b", KVB - 1)[3] + RAW)
                for n, bank in enumerate((SC[0], SC[1], TR[0], TR[1])):
                    for k in range(KVB):
                        a = slice((QB + k) * T + n // 2 * P, (QB + k) * T + n // 2 * P + P)
                        w = slice(n % 2 * 512, n % 2 * 512 + 512)
                        pe.matmul(bank[:], act_hi[:, a], w_hi[:, hi_slots[k], w], start=(k == 0), stop=False)
                        pe.matmul(bank[:], act_lo[:, a], w_hi[:, hi_slots[k], w], start=False, stop=False)
                        mm = pe.matmul(bank[:], act_hi[:, a], w_lo[:, lo_slots[k], w], start=False, stop=(k == KVB - 1))
                mm.then_inc(pan_done, 2)
                for i in range(8):
                    pe.wait_ge(head_sq, i // 4 + 1)
                    if i >= 2:
                        pe.wait_ge(head_rms, i - 1)
                    for e in range(2):
                        h = 2 * (i % 4) + e
                        o = (OV, STAT)[i % 2][:, e * T:(e + 1) * T]
                        pe.matmul(o, ones, sqn[:, h * T:(h + 1) * T], start=True, stop=False)
                        for x in range(2):
                            row = (h % 4) if i < 4 else 0
                            r = (2 * x + h // 4) if i < 4 else x
                            mm = pe.matmul(o, con[:, C_ROW + row * P:C_ROW + (row + 1) * P], sqr[:, r * T:(r + 1) * T],
                                           start=False, stop=(x == 1))
                    mm.then_inc(head_sum, 1)
                pe.wait_ge(qk_ready, 1)
                pe.wait_ge(v_copied, 1)
                for i in range(HEADS + 2):
                    if i < HEADS:
                        h = i
                        if h >= 2:
                            pe.wait_ge(s_masked, h - 1)
                        for t, (c0, c1) in enumerate(((0, P), (P, 3 * P))):
                            o, n = SC[h % 2][:, c0:c1], c1 - c0
                            q0 = h * T + t * P
                            pe.matmul(o, qn[:, q0:q0 + P], kn[:, h * T:h * T + n], start=True, stop=False)
                            for x in range(2):
                                z0 = (2 * h + x) * T + t * P
                                k0 = (2 * x + h // 4) * T
                                mm = pe.matmul(o, qz[:, z0:z0 + P], rot[:, k0:k0 + n], start=False, stop=(x == 1))
                        mm.then_inc(s_done, 1)
                    if 1 <= i <= HEADS:
                        h = i - 1
                        pe.wait_ge(p_norm, h + 1)
                        if h >= 2:
                            pe.wait_ge(p_copied, h - 1)
                        for b in range(3):
                            mm = pe.transpose(TR[h % 2][:, b * P:(b + 1) * P], s_sb[:, h % 2, b * P:(b + 1) * P], ident)
                        mm.then_inc(p_tr, 1)
                    if i >= 2:
                        h = i - 2
                        pe.wait_ge(p_copied, h + 1)
                        if h >= 2:
                            pe.wait_ge(o_copied, h - 1)
                        o = (OV, STAT)[h % 2]
                        v0, v1 = vv[:, h * VH:(h + 1) * VH], vv[:, D + h * VH:D + (h + 1) * VH]
                        pe.matmul(o[:, 0:P], v0, pT[:, h % 2, 0:P], start=True, stop=True)
                        pe.matmul(o[:, P:2 * P], v0, pT[:, h % 2, P:2 * P], start=True, stop=False)
                        pe.matmul(o[:, P:2 * P], v1, pT[:, h % 2, 2 * P:3 * P], start=False, stop=True
                                  ).then_inc(o_done, 1)
                pe.wait_ge(act_ready, 6)
                with pe.Fori(0, 2) as it:
                    for j in range(4):
                        full_panel("mla_out", j, 4, it)

            pe.sem_inc(pan_done, HI)
            pe.sem_inc(g_done, 2)
            pe.wait_ge(s_const, 80)
            square_sums(1)
            pe.wait_ge(act_ready, 1)
            with pe.Fori(0, 2) as it:
                for j in range(12):
                    full_panel("conv_in", j, 12, it)
            pe.wait_ge(act_ready, 2)
            with pe.Fori(0, 2) as it:
                for j in range(4):
                    full_panel("conv_out", j, 4, it)
            peer(0)
            attention()
            peer(1)

        @block.scalar
        def _(act):
            def split_hi(stage, j, unroll=0, it=0):
                slot, _, count, n = ring(stage, j, unroll, it)
                width = D if unroll else WIDTHS.get(BASE[stage] + j, D)
                act.wait_ge(landed[slot], count)
                act.wait_ge(pan_done, n)
                nc.scalar.copy(w_hi[:, slot, 0:width], raw[:, slot, 0:width]).then_inc(hi_done, 1)

            def split_act(n, src, width):
                act.wait_ge(f32_ready, n)
                nc.scalar.copy(act_hi[:, 0:width], src).then_inc(act_hi_ready, 1)

            def normalise(n):
                if n > 1:
                    act.wait_ge(x_ready, n - 1)
                nc.scalar.activation(sq, xT[:], ACT.Square).then_inc(sq_ready, 1)
                act.wait_ge(sum_ready, n)
                nc.scalar.activation(rms[:, 0:T], STAT[:, 0:T], ACT.Sqrt, bias=eps[:], scale=1.0 / D
                                     ).then_inc(rms_ready, 1)

            def gelu(l, stage, j, unroll, it, bank, slot):
                act.wait_ge(pan_done, ring(stage, j, unroll, it)[3] + HI)
                nc.scalar.activation(ring_g[:, bass.ds(slot * T, T)], bank[:, 0:T], ACT.Gelu).then_inc(pan_read[l], 1)

            def copy_gates(quarter, par, count, token0):
                act.wait_ge(g_done, count + 2)
                g = arena[:, quarter % 2 * QUART * T:(quarter % 2 + 1) * QUART * T].rearrange("p (a t) -> p a t", t=T)
                nc.scalar.mul(g[:, :, bass.ds(token0, GT)], GB[par][:].rearrange("p (t a) -> p a t", a=QUART),
                              1.0 / G_SCALE).then_inc(g_read, 1)

            def split_weighted(par, count):
                act.wait_ge(w_mul, count)
                nc.scalar.copy(wt_hi[:, par, :], w32[:]).then_inc(wt_hi_ready, 1)

            def peer(l):
                normalise(2 * l + 2)
                split_act([3, 7][l], act32, KB * T)
                act.sem_inc(pan_read[l], 2)
                with act.Fori(0, 8) as it:
                    for p in range(2):
                        split_hi(f"sel{l}", 2 * p + HI_LEAD, 4, it)
                        act.wait_ge(pan_done, ring(f"sel{l}", 2 * p, 4, it)[3] + HI)
                        nc.scalar.copy(q_sb[:, p, :], PAN[0][:, 0:T]).then_inc(pan_read[l], 1)
                        split_hi(f"sel{l}", 2 * p + 1 + HI_LEAD, 4, it)
                        gelu(l, f"sel{l}", 2 * p + 1, 4, it, PAN[1], it * 2 + p)
                act.wait_ge(gate_in, l + 1)
                nc.scalar.activation(gate, gate, ACT.Exp).then_inc(gate_exp, 1)
                with act.Fori(0, 4) as it:
                    for j in range(4):
                        split_hi(f"ahead{l}", j + HI_LEAD, 4, it)
                        copy_gates(0, j % 2, it * 4 + (64 * l + j + 1), (it * 4 + j) * GT)
                        gelu(l, f"ahead{l}", j, 4, it, PAN[j % 2], it * 4 + (16 + j))
                split_weighted(0, 64 * l + 1)
                for q in range(3):
                    with act.Fori(0, 8) as it:
                        for s in range(2):
                            j = 64 * q + 4 * s
                            split_hi(f"mix{l}", j + HI_LEAD, 8, it)
                            gelu(l, f"mix{l}", j, 8, it, PAN[0], it * 4 + 2 * s)
                            split_hi(f"mix{l}", j + 1 + HI_LEAD, 8, it)
                            split_hi(f"mix{l}", j + 2 + HI_LEAD, 8, it)
                            gelu(l, f"mix{l}", j + 2, 8, it, PAN[1], it * 4 + (2 * s + 1))
                            copy_gates(q + 1, s, it * 2 + (64 * l + 16 * (q + 1) + s + 1), (it * 2 + s) * GT)
                            split_weighted(1 - s, it * 2 + (64 * l + 16 * q + s + 2))
                            split_hi(f"mix{l}", j + 3 + HI_LEAD, 8, it)

                def last_body(it, end):
                    for s in range(2):
                        if not (end and s and l):
                            split_hi(f"last{l}", 2 * s + HI_LEAD, 4, it)
                        if not (end and s):
                            split_weighted(1 - s, it * 2 + (64 * l + 48 + s + 2))
                        if not (end and l):
                            split_hi(f"last{l}", 2 * s + 1 + HI_LEAD, 4, it)

                with act.Fori(0, 7) as it:
                    last_body(it, False)
                last_body(7, True)
                act.wait_ge(pan_done, ring(f"last{l}", 31)[3] + HI)
                for n in range(4):
                    i = nc.scalar.copy(yrow[:, n * 512:(n + 1) * 512], YB[n][:])
                i.then_inc(y_copied, 1)

            act.sem_inc(g_read, 2)
            act.wait_ge(s_const, 80)
            nc.scalar.activation(crow[:], crow[:], ACT.Silu).then_inc(s_silu, 1)
            for j in range(HI_LEAD):
                split_hi("conv_in", j)
            act.wait_ge(s_eps, 1)
            normalise(1)
            split_act(1, act32, KB * T)
            with act.Fori(0, 2) as it:
                for j in range(12):
                    split_hi("conv_in", j + HI_LEAD, 12, it)
            split_act(2, act32, KB * T)
            with act.Fori(0, 2) as it:
                for j in range(4):
                    split_hi("conv_out", j + HI_LEAD, 4, it)
            peer(0)
            act.wait_ge(trig_in, 1)
            nc.scalar.activation(sinb, sinb, ACT.Sin)
            nc.scalar.activation(cosb, cosb, ACT.Sin).then_inc(trig, 1)
            normalise(3)
            split_act(4, act32, KB * T)
            for j in range(7):
                split_hi("mla_in", j + HI_LEAD)
            act.wait_ge(lat_in, 1)
            nc.scalar.activation(sqn[:, 0:5 * T], lat, ACT.Square).then_inc(lat_sq, 1)
            act.wait_ge(lat_sum, 1)
            nc.scalar.activation(rms[:, 0:T], STAT[:, 0:T], ACT.Sqrt, bias=eps[:], scale=1.0 / Q_LORA)
            nc.scalar.activation(rms[:, T:2 * T], STAT[:, T:2 * T], ACT.Sqrt, bias=eps[:], scale=1.0 / KV_LORA
                                 ).then_inc(lat_rms, 1)
            split_act(5, lat, 5 * T)
            for j in range(6):
                split_hi("q_b", j + HI_LEAD)
            for j in range(4):
                split_hi("k_b", j + HI_LEAD)
            for j in range(KVB):
                split_hi("v_b", j + HI_LEAD)
            act.wait_ge(evac["q_b"], 6 + 2)
            nc.scalar.activation(sqn, qn, ACT.Square)
            nc.scalar.activation(sqr, qr, ACT.Square).then_inc(head_sq, 1)
            for i in range(8):
                if i == 4:
                    act.wait_ge(head_sum, 4)
                    act.wait_ge(evac["k_b"], 4 + 2)
                    nc.scalar.activation(sqn, kn, ACT.Square)
                    nc.scalar.activation(sqr[:, 0:2 * T], kraw, ACT.Square).then_inc(head_sq, 1)
                act.wait_ge(head_sum, i + 1)
                if i >= 1:
                    act.wait_ge(head_rstd, i)
                nc.scalar.activation(rms[:], (OV, STAT)[i % 2][:], ACT.Sqrt, bias=eps[:], scale=1.0 / QK_HEAD
                                     ).then_inc(head_rms, 1)
            for i in range(HEADS + 1):
                if i < HEADS:
                    act.wait_ge(s_masked, i + 1)
                    for t, (c0, c1) in enumerate(((0, P), (P, 3 * P))):
                        e = nc.scalar.activation(s_sb[:, i % 2, c0:c1], s_sb[:, i % 2, c0:c1], ACT.Exp,
                                                 bias=smax[:, i % 2, t:t + 1], scale=float(QK_HEAD) ** -0.5,
                                                 accum_out=ssum[:, i % 2, t:t + 1])
                    e.then_inc(p_exp, 1)
                if i >= 1:
                    act.wait_ge(p_tr, i)
                    nc.scalar.copy(pT[:, (i - 1) % 2, :], TR[(i - 1) % 2][:, 0:384]).then_inc(p_copied, 1)
            split_act(6, act32, KB * T)
            with act.Fori(0, 2) as it:
                for j in range(4):
                    split_hi("mla_out", j + HI_LEAD, 4, it)
            peer(1)

        @block.gpsimd
        def _(pool):
            with pool.Fori(0, 48 // ADA) as it:
                for j in range(ADA):
                    pool.wait_ge(ada_used, it * ADA + (j + 1))
                    pool.sem_inc(ada_seen, 1)
                    pool.dma_start(ada[:, j, :], ada_in[bass.ds(it * ADA + j, 1)].rearrange("o p n -> p (o n)")
                                   ).then_inc(ada_landed[j], 16)
            with pool.Fori(0, 48) as it:
                pool.wait_ge(ada1_used, it + 1)
                pool.sem_inc(ada_seen, 1)
                pool.dma_start(ada1[:], ada_in[bass.ds(it + 48, 1)].rearrange("o p n -> p (o n)")
                               ).then_inc(ada1_landed, 16)

        @block.vector
        def _(dve):
            def split_lo(stage, j, unroll=0, it=0):
                slot, lo_slot, _, n = ring(stage, j, unroll, it)
                width = D if unroll else WIDTHS.get(BASE[stage] + j, D)
                dve.wait_ge(hi_done, n)
                dve.wait_ge(pan_done, n + HI - LO)
                dve.tensor_tensor(w_lo[:, lo_slot, 0:width], raw[:, slot, 0:width], w_hi[:, slot, 0:width].bitcast(F32),
                                  ALU.subtract).then_inc(lo_done, 1)

            def split_act(n, src, width):
                dve.wait_ge(act_hi_ready, n)
                dve.tensor_tensor(act_lo[:, 0:width], src, act_hi[:, 0:width].bitcast(F32), ALU.subtract
                                  ).then_inc(act_ready, 1)

            def wait_product(stage, j, unroll=0, it=0):
                dve.wait_ge(pan_done, ring(stage, j, unroll, it)[3] + HI)

            def mod_col(l, s):
                return l * 48 + s * KB

            def modulation(col, n):
                dve.drain()
                dve.tensor_tensor(mod[:, bass.ds(col, n)], ada_sum[:, 0:n], vec[:, bass.ds(col + V_ADAB, n)], ALU.add)
                dve.drain()

            def ada_rows(m, half, landings):
                for j in range(4):
                    slot = half * 4 + j
                    dve.wait_ge(ada_landed[slot], landings)
                    dve.tensor_tensor_reduce(out=ada[:, slot, :], in0=ada[:, slot, :], in1=crow[:], scale=1.0,
                                             scalar=0.0, op0=ALU.mult, op1=ALU.add, accum_out=ada_sum[:, j:j + 1]
                                             ).then_inc(ada_used, 1)
                modulation(m * 4, 4)

            def ada1_row(n, j):
                dve.wait_ge(ada1_landed, n * 16 + 16)
                dve.tensor_tensor_reduce(out=ada1[:], in0=ada1[:], in1=crow[:], scale=1.0, scalar=0.0, op0=ALU.mult,
                                         op1=ALU.add, accum_out=ada_sum[:, j:j + 1]).then_inc(ada1_used, 1)

            def normalise(n, l, g0, s0):
                sh, sc = mod_col(l, s0), mod_col(l, s0 + 1)
                dve.scalar_tensor_tensor(out=gain[:], in0=mod[:, sc:sc + KB], scalar=1.0, in1=vec[:, g0:g0 + KB],
                                         op0=ALU.add, op1=ALU.mult)
                dve.wait_ge(rms_ready, n)
                dve.reciprocal(rstd[:, 0:T], rms[:, 0:T])
                dve.drain()
                dve.tensor_tensor(act32.rearrange("p (k t) -> p k t", t=T), xT[:].rearrange("p (k t) -> p k t", t=T),
                                  rstd[:, 0:T].unsqueeze(1).broadcast_to([P, KB, T]), ALU.mult)
                dve.drain()
                for k in range(KB):
                    i = dve.tensor_scalar(act32[:, k * T:(k + 1) * T], act32[:, k * T:(k + 1) * T], gain[:, k:k + 1],
                                          mod[:, sh + k:sh + k + 1], ALU.mult, ALU.add)
                i.then_inc(f32_ready, 1)

            def add_to_x(stage, l, last_count):
                dve.sem_inc(evac[stage], 2)
                with dve.Fori(0, 2) as it:
                    for j in range(4):
                        split_lo(stage, j + 1, 4, it)
                        wait_product(stage, j, 4, it)
                        xk = xT[:, bass.ds((it * 4 + j) * T, T)]
                        dve.scalar_tensor_tensor(out=xk, in0=PAN[j % 2][:, 0:T],
                                                 scalar=mod[:, bass.ds(it * 4 + (j + mod_col(l, 2)), 1)], in1=xk,
                                                 op0=ALU.mult, op1=ALU.add).then_inc(evac[stage], 1)
                dve.drain()
                dve.sem_inc(x_ready, 1)

            def top16_first(src, vals, idx, spare, after_read=None):
                for t in range(TT):
                    dve.max(vals[t][:, 0:8], src[t])
                dve.drain()
                for t in range(TT):
                    dve.max_index(idx[t][:, 0:8], vals[t][:, 0:8], src[t])
                for t in range(TT):
                    r = dve.match_replace(spare[t], vals[t][:, 0:8], src[t], NEG)
                if after_read is not None:
                    r.then_inc(after_read, 1)

            def top16_second(vals, idx, spare):
                dve.drain()
                for t in range(TT):
                    dve.max(vals[t][:, 8:16], spare[t])
                dve.drain()
                for t in range(TT):
                    dve.max_index(idx[t][:, 8:16], vals[t][:, 8:16], spare[t])

            def select(l):
                tv = lambda t, p: topv[:, (t * 2 + p) * TOPK:(t * 2 + p + 1) * TOPK]
                ti = lambda t, p: topi[:, (t * 2 + p) * TOPK:(t * 2 + p + 1) * TOPK]
                tiles = range(TT)
                by_tile = lambda a: a.rearrange("p (t n) -> p t n", t=TT)

                def half_first(p, count):
                    dve.wait_ge(sc_done, count)
                    dve.sem_inc(sc_seen, 1)
                    dve.drain()
                    top16_first([SC[p][:, t * P:(t + 1) * P] for t in tiles], [tv(t, p) for t in tiles],
                                [ti(t, p) for t in tiles], [work[:, t * P:(t + 1) * P] for t in tiles], sc_used)

                def half_second(p):
                    top16_second([tv(t, p) for t in tiles], [ti(t, p) for t in tiles],
                                 [work[:, t * P:(t + 1) * P] for t in tiles])

                pairs = [cand[:, t * 256:(t + 1) * 256] for t in tiles]
                pairs_left = [cwork[:, t * 256:(t + 1) * 256] for t in tiles]
                bv16 = [bestv[:, t * TOPK:(t + 1) * TOPK] for t in tiles]
                bp16 = [bestp[:, t * TOPK:(t + 1) * TOPK] for t in tiles]

                def pairs_first():
                    dve.drain()
                    for t in tiles:
                        dve.tensor_tensor(pairs[t].rearrange("p (a b) -> p a b", b=TOPK),
                                          tv(t, 0).unsqueeze(2).broadcast_to([P, TOPK, TOPK]),
                                          tv(t, 1).unsqueeze(1).broadcast_to([P, TOPK, TOPK]), ALU.add)
                    dve.drain()
                    top16_first(pairs, bv16, bp16, pairs_left)

                def pairs_second(head):
                    top16_second(bv16, bp16, pairs_left)
                    dve.drain()
                    dve.tensor_copy(top_i[:, :, bass.ds(head * (2 * TOPK), 2 * TOPK)], by_tile(topi))
                    dve.tensor_copy(best_v[:, :, bass.ds(head * TOPK, TOPK)], by_tile(bestv))
                    dve.tensor_copy(best_p[:, :, bass.ds(head * TOPK, TOPK)], by_tile(bestp))
                    dve.drain()

                def head_step(it, first):
                    split_lo(f"sel{l}", 1, 4, it)
                    if not first:
                        half_first(1, it * 2 + 16 * l)
                        half_second(1)
                    split_lo(f"sel{l}", 2, 4, it)
                    if not first:
                        pairs_first()
                    split_lo(f"sel{l}", 3, 4, it)
                    if not first:
                        pairs_second(it - 1)
                    half_first(0, it * 2 + (16 * l + 1))
                    split_lo(f"sel{l}", 4, 4, it)
                    half_second(0)

                head_step(0, True)
                with dve.Fori(1, 8) as it:
                    head_step(it, False)
                half_first(1, 16 * l + 16)
                half_second(1)
                pairs_first()
                pairs_second(HEADS - 1)
                hk = lambda a: a.rearrange("p t (h k) -> p (t h) k", k=TOPK)
                bv = hk(best_v)
                dve.tensor_tensor(hk(gate), bv, bv[:, :, 0:1].broadcast_to([P, TT * HEADS, TOPK]), ALU.subtract
                                  ).then_inc(gate_in, 1)
                for t in tiles:
                    dve.tensor_scalar(dec_u[:, 0, :], best_p[:, t, :], 4, None, ALU.logical_shift_right)
                    dve.tensor_scalar(dec_u[:, 1, :], best_p[:, t, :], 15, None, ALU.bitwise_and)
                    dve.tensor_copy(tif, top_i[:, t, :])
                    dve.drain()
                    dve.tensor_copy(dec_f, dec_u.rearrange("p x n -> p (x n)"))
                    for x in range(2):
                        dve.drain()
                        e4 = eq.rearrange("p (h k j) -> p h k j", h=HEADS, k=TOPK)
                        place = dec_f[:, x * SEL:(x + 1) * SEL].rearrange("p (h k) -> p h k", k=TOPK)
                        dve.tensor_tensor(e4, place.unsqueeze(3).broadcast_to([P, HEADS, TOPK, TOPK]),
                                          con[:, C_IOTA:C_IOTA + TOPK].unsqueeze(1).unsqueeze(1)
                                          .broadcast_to([P, HEADS, TOPK, TOPK]), ALU.is_equal)
                        dve.drain()
                        key = tif.rearrange("p (h x j) -> p h x j", h=HEADS, x=2)[:, :, x, :]
                        dve.tensor_tensor(e4, e4, key.unsqueeze(2).broadcast_to([P, HEADS, TOPK, TOPK]), ALU.mult)
                        dve.drain()
                        dve.tensor_reduce(eab[:, (2 * t + x) * SEL:(2 * t + x + 1) * SEL],
                                          eq.rearrange("p (n j) -> p n j", j=TOPK), AX.X, ALU.add)
                    if t == 0:
                        dve.wait_ge(gate_exp, l + 1)
                        dve.tensor_reduce(esum, hk(gate), AX.X, ALU.add)
                        dve.drain()
                        dve.reciprocal(esum, esum)
                        dve.drain()
                        dve.tensor_tensor(hk(gate), hk(gate), esum.unsqueeze(2).broadcast_to([P, TT * HEADS, TOPK]),
                                          ALU.mult)
                    dve.drain()
                    dve.sem_inc(dec_done, 1)
                for t in tiles:
                    dve.wait_ge(idx_done, TT * l + t + 1)
                    c = slice(t * P, (t + 1) * P)
                    dve.tensor_copy(ia_t[:, c], GB[t][:, 0:P])
                    dve.tensor_copy(ib_t[:, c], GB[t][:, P:2 * P])
                    dve.tensor_scalar(g32_t[:, c], GB[t][:, 2 * P:3 * P], G_SCALE, None, ALU.mult)
                dve.drain()
                dve.tensor_copy(gh_t[:], g32_t[:])
                dve.drain()
                dve.tensor_tensor(gl_t[:], g32_t[:], gh_t[:], ALU.subtract)
                dve.drain()

            each = lambda a, n, token0: a[:, bass.ds(token0, GT)].unsqueeze(1).broadcast_to([P, n, GT])
            wide = lambda a: a.rearrange("p (b t) -> p b t", t=GT)

            def second_key_hots(par, count, token0):
                dve.wait_ge(g_done, count)
                dve.tensor_tensor(wide(hot_b[:, par, :]), each(ib_t, KEYS, token0), wide(iota_x[:]), ALU.is_equal)

            def first_key_hots(quarter, par, token0):
                dve.tensor_tensor(wide(hot_a[:, par, :]), each(ia_t, QUART, token0),
                                  wide(iota_x[:, quarter * QUART * GT:(quarter + 1) * QUART * GT]), ALU.is_equal)
                dve.drain()
                for part, g in ((hot_gh, gh_t), (hot_gl, gl_t)):
                    i = dve.tensor_tensor(wide(part[:, par, :]), wide(hot_a[:, par, :]), each(g, QUART, token0),
                                          ALU.mult)
                i.then_inc(hot_ready, 1)

            def weigh(slot, key, count):
                dve.drain()
                dve.wait_ge(g_read, count)
                dve.tensor_tensor(w32[:], ring_g[:, bass.ds(slot * T, 2 * T)], arena[:, bass.ds(key * T, 2 * T)],
                                  ALU.mult).then_inc(w_mul, 1)

            def split_weighted(par, count):
                dve.wait_ge(wt_hi_ready, count)
                dve.tensor_tensor(wt_lo[:, par, :], w32[:], wt_hi[:, par, :].bitcast(F32), ALU.subtract
                                  ).then_inc(wt_ready, 1)

            def experts(l):
                with dve.Fori(0, 4) as it:
                    for j in range(4):
                        second_key_hots(j % 2, it * 4 + (64 * l + j + 1), (it * 4 + j) * GT)
                        first_key_hots(0, j % 2, (it * 4 + j) * GT)
                        split_lo(f"ahead{l}", j + 1, 4, it)
                weigh(0, 0, 64 * l + 16 + 2)
                split_weighted(0, 64 * l + 1)

                def mix_body(q, it, end):
                    for s in range(2):
                        j = 64 * q + 4 * s
                        token0 = (it * 2 + s) * GT
                        split_lo(f"mix{l}", j + 1, 8, it)
                        second_key_hots(s, it * 2 + (64 * l + 16 * (q + 1) + s + 1), token0)
                        split_lo(f"mix{l}", j + 2, 8, it)
                        first_key_hots(q + 1, s, token0)
                        split_lo(f"mix{l}", j + 3, 8, it)
                        if l == 0:
                            ada1_row(it * 2 + (16 * q + s), s)
                        if end and s:
                            weigh(0, (q + 1) % 2 * QUART, 64 * l + 16 * (q + 2) + 2)
                        else:
                            weigh(it * 4 + (2 * s + 2), it * 4 + (q % 2 * QUART + 2 * s + 2), 64 * l + 16 * (q + 1) + 2)
                        split_lo(f"mix{l}", j + 4, 8, it)
                        split_weighted(1 - s, it * 2 + (64 * l + 16 * q + s + 2))
                    if l == 0:
                        modulation(it * 2 + (48 + 16 * q), 2)

                for q in range(3):
                    with dve.Fori(0, 7) as it:
                        mix_body(q, it, False)
                    mix_body(q, 7, True)

                def last_body(it, end):
                    for s in range(2):
                        split_lo(f"last{l}", 2 * s + 1, 4, it)
                        if not (end and s):
                            weigh(it * 4 + (2 * s + 2), it * 4 + (QUART + 2 * s + 2), 64 * l + 64 + 2)
                        if not (end and s and l):
                            split_lo(f"last{l}", 2 * s + 2, 4, it)
                        if not (end and s):
                            split_weighted(1 - s, it * 2 + (64 * l + 48 + s + 2))

                with dve.Fori(0, 7) as it:
                    last_body(it, False)
                last_body(7, True)
                for t in range(TT):
                    for g in range(2):
                        dve.wait_ge(yt_done, 4 * l + 2 * t + g + 1)
                        for k in range(4):
                            kk = 4 * g + k
                            xk = xT[:, kk * T + t * P:kk * T + (t + 1) * P]
                            c = mod_col(l, 5) + kk
                            i = dve.scalar_tensor_tensor(out=xk, in0=GB[g][:, k * P:(k + 1) * P],
                                                         scalar=mod[:, c:c + 1], in1=xk, op0=ALU.mult, op1=ALU.add)
                        i.then_inc(yt_added, 1)
                dve.drain()
                dve.sem_inc(x_ready, 1)

            def peer(l):
                normalise(2 * l + 2, l, V_CH + l * KB, 3)
                split_act([3, 7][l], act32, KB * T)
                select(l)
                experts(l)

            def reduced(out_ap, shift):
                dve.tensor_scalar(tmp, ang, 1.0 / TWO_PI, shift / TWO_PI, ALU.mult, ALU.add)
                dve.drain()
                dve.tensor_scalar(tmp, tmp, ROUND, None, ALU.add)
                dve.drain()
                dve.tensor_scalar(tmp, tmp, -ROUND, None, ALU.add)
                dve.drain()
                src = ang
                for part in (PI_1, PI_2, PI_3):
                    dve.scalar_tensor_tensor(out=out_ap, in0=tmp, scalar=-part, in1=src, op0=ALU.mult, op1=ALU.add)
                    dve.drain()
                    src = out_ap
                dve.tensor_scalar(out_ap, out_ap, shift, None, ALU.add)
                dve.drain()
                return dve.tensor_scalar(out_ap, out_ap, 3.1415925, -3.1415925, ALU.min, ALU.max)

            def rotate(src):
                two = lambda ap: ap.rearrange("p (i t) -> p i t", t=T)
                cs = cosb.unsqueeze(1).broadcast_to([P, 2, T])
                sn = sinb.unsqueeze(1).broadcast_to([P, 2, T])
                a, b = two(src[:, 0:2 * T]), two(src[:, 2 * T:4 * T])
                t1, t2 = act32[:, 512:1024], act32[:, 1024:1536]
                for o, (m1, m2, op) in enumerate(((cs, sn, ALU.subtract), (sn, cs, ALU.add))):
                    dve.tensor_tensor(two(t1), a, m1, ALU.mult)
                    dve.tensor_tensor(two(t2), b, m2, ALU.mult)
                    dve.drain()
                    i = dve.tensor_tensor(rot[:, o * 2 * T:(o + 1) * 2 * T], t1, t2, op)
                    dve.drain()
                return i

            def attention():
                dve.wait_ge(s_pos, 16)
                dve.tensor_copy(ang, posi)
                dve.drain()
                dve.tensor_scalar(ang, ang, con[:, C_FREQ:C_FREQ + 1], None, ALU.mult)
                dve.drain()
                reduced(sinb, 0.0)
                dve.drain()
                reduced(cosb, np.pi / 2).then_inc(trig_in, 1)
                normalise(3, 1, V_TOK + KB, 0)
                split_act(4, act32, KB * T)
                dve.sem_inc(evac["mla_in"], 2)
                for j in range(7):
                    split_lo("mla_in", j + 1)
                    wait_product("mla_in", j)
                    dst = lat[:, j * T:(j + 1) * T] if j < 5 else kraw[:, (j - 5) * T:(j - 4) * T]
                    i = dve.tensor_copy(dst, PAN[j % 2][:, 0:T])
                    i.then_inc(evac["mla_in"], 1)
                dve.drain()
                dve.sem_inc(lat_in, 1)
                dve.wait_ge(lat_rms, 1)
                dve.reciprocal(rstd[:], rms[:])
                dve.drain()
                for k in range(5):
                    r = rstd[:, 0:T] if k < QB else rstd[:, T:2 * T]
                    c = V_QA + k
                    lk = lat[:, k * T:(k + 1) * T]
                    i = dve.scalar_tensor_tensor(out=lk, in0=lk, scalar=vec[:, c:c + 1], in1=r, op0=ALU.mult,
                                                 op1=ALU.mult)
                i.then_inc(f32_ready, 1)
                split_act(5, lat, 5 * T)
                dve.sem_inc(evac["q_b"], 2)
                for j in range(6):
                    split_lo("q_b", j + 1)
                    wait_product("q_b", j)
                    dve.tensor_copy(arena[:, j * 2 * T:(j + 1) * 2 * T], PAN[j % 2][:]).then_inc(evac["q_b"], 1)
                dve.sem_inc(evac["k_b"], 2)
                for j in range(4):
                    split_lo("k_b", j + 1)
                    wait_product("k_b", j)
                    dve.tensor_copy(kn[:, j * 2 * T:(j + 1) * 2 * T], PAN[j % 2][:]).then_inc(evac["k_b"], 1)
                split_lo("v_b", 1)
                wait_product("v_b", 1)
                for n, bank in enumerate((SC[0], SC[1], TR[0], TR[1])):
                    i = dve.tensor_copy(vv[:, n * 512:(n + 1) * 512], bank[:])
                i.then_inc(v_copied, 1)
                split_lo("mla_out", 0)
                dve.wait_ge(trig, 1)
                for i in range(8):
                    dve.wait_ge(head_rms, i + 1)
                    dve.reciprocal(rstd[:], rms[:]).then_inc(head_rstd, 1)
                    dve.drain()
                    for e in range(2):
                        h = 2 * (i % 4) + e
                        base, g = (qn, V_QN) if i < 4 else (kn, V_KN)
                        hd = base[:, h * T:(h + 1) * T]
                        dve.scalar_tensor_tensor(out=hd, in0=hd, scalar=vec[:, g:g + 1], in1=rstd[:, e * T:(e + 1) * T],
                                                 op0=ALU.mult, op1=ALU.mult)
                        r = slice(32 * (h % 4), 32 * (h % 4) + 32)
                        for x in range(2):
                            c = slice((2 * x + h // 4) * T, (2 * x + h // 4 + 1) * T)
                            src = qr[r, c] if i < 4 else kraw[r, x * T:(x + 1) * T]
                            dst = qr[r, c] if i < 4 else kr[r, c]
                            dve.scalar_tensor_tensor(out=dst, in0=src, scalar=vec[r, g + 1 + x:g + 2 + x],
                                                     in1=rstd[r, e * T:(e + 1) * T], op0=ALU.mult, op1=ALU.mult)
                    dve.drain()
                    if i == 3:
                        rotate(qr)
                        for h in range(HEADS):
                            z = qz[:, 2 * h * T:(2 * h + 2) * T].rearrange("p (x t) -> p x t", t=T)
                            src = rot.rearrange("p (x i t) -> p x i t", x=2, t=T)[:, :, h // 4, :]
                            c = C_ROWCOL + h % 4
                            dve.tensor_scalar(z, src, con[:, c:c + 1], None, ALU.mult)
                        dve.drain()
                rotate(kr)
                dve.sem_inc(qk_ready, 1)
                for i in range(HEADS + 2):
                    if i < HEADS:
                        h = i
                        dve.wait_ge(s_done, h + 1)
                        dve.tensor_tensor(s_sb[:, h % 2, :], SC[h % 2][:, 0:384], con[:, C_MASK:C_MASK + 384], ALU.add)
                        dve.drain()
                        for t, (c0, c1) in enumerate(((0, P), (P, 3 * P))):
                            dve.tensor_reduce(smax[:, h % 2, t:t + 1], s_sb[:, h % 2, c0:c1], AX.X, ALU.max)
                        dve.drain()
                        dve.tensor_scalar(smax[:, h % 2, :], smax[:, h % 2, :], -float(QK_HEAD) ** -0.5, None, ALU.mult
                                          ).then_inc(s_masked, 1)
                    if 1 <= i <= HEADS:
                        h = i - 1
                        dve.wait_ge(p_exp, h + 1)
                        dve.reciprocal(ssum[:, h % 2, :], ssum[:, h % 2, :])
                        dve.drain()
                        for t, (c0, c1) in enumerate(((0, P), (P, 3 * P))):
                            n = dve.tensor_scalar(s_sb[:, h % 2, c0:c1], s_sb[:, h % 2, c0:c1],
                                                  ssum[:, h % 2, t:t + 1], None, ALU.mult)
                        n.then_inc(p_norm, 1)
                    if i >= 2:
                        h = i - 2
                        dve.wait_ge(o_done, h + 1)
                        dve.tensor_copy(act32[:, h * T:(h + 1) * T], (OV, STAT)[h % 2][:, 0:T]).then_inc(o_copied, 1)
                dve.drain()
                dve.sem_inc(f32_ready, 1)
                split_act(6, act32, KB * T)
                add_to_x("mla_out", 1, 3)

            dve.memset(eps[:], EPS)
            dve.memset(zero[:].bitcast(F32), 0.0)
            dve.memset(u_pad[:, 0:2], 0.0).then_inc(s_eps, 1)
            dve.sem_inc(lo_done, RAW)
            dve.sem_inc(ada_used, ADA)
            dve.sem_inc(ada1_used, 1)
            dve.sem_inc(sc_used, 2)
            dve.wait_ge(s_const, 80)
            dve.wait_ge(s_silu, 1)
            with dve.Fori(0, 2) as it:
                for half in range(2):
                    ada_rows(it * 2 + half, half, it * 16 + 16)
            normalise(1, 0, V_TOK, 0)
            split_act(1, act32, KB * T)
            split_lo("conv_in", 0)
            dve.sem_inc(evac["conv_in"], 2)
            with dve.Fori(0, 2) as it:
                for b in range(4):
                    split_lo("conv_in", 3 * b + 1, 12, it)
                    wait_product("conv_in", 3 * b, 12, it)
                    dve.tensor_copy(c_sb, PAN[3 * b % 2][:, 0:T]).then_inc(evac["conv_in"], 1)
                    split_lo("conv_in", 3 * b + 2, 12, it)
                    dve.drain()
                    wait_product("conv_in", 3 * b + 1, 12, it)
                    dve.tensor_tensor(u_pad[:, 2:2 + T], PAN[(3 * b + 1) % 2][:, 0:T], c_sb, ALU.mult
                                      ).then_inc(evac["conv_in"], 1)
                    split_lo("conv_in", 3 * b + 3, 12, it)
                    dve.drain()
                    ada_rows(it * 4 + (4 + b), b % 2, it * 32 + (16 * (b // 2) + 48))
                    tap = lambda i: vec[:, bass.ds(it * 4 + (V_CONV + i * KB + b), 1)]
                    dve.tensor_scalar(conv_t, u_pad[:, 0:T], tap(0), None, ALU.mult)
                    for i in (1, 2):
                        dve.drain()
                        dve.scalar_tensor_tensor(out=conv_t, in0=u_pad[:, i:i + T], scalar=tap(i), in1=conv_t,
                                                 op0=ALU.mult, op1=ALU.add)
                    dve.drain()
                    wait_product("conv_in", 3 * b + 2, 12, it)
                    dve.tensor_tensor(act32[:, bass.ds((it * 4 + b) * T, T)], PAN[(3 * b + 2) % 2][:, 0:T], conv_t,
                                      ALU.mult).then_inc(evac["conv_in"], 1)
            dve.drain()
            dve.sem_inc(f32_ready, 1)
            split_act(2, act32, KB * T)
            add_to_x("conv_out", 0, 1)
            peer(0)
            attention()
            peer(1)


def shape_constants():
    con = np.zeros((P, C_N), np.float32)
    con[:, C_ID:C_ID + P] = np.eye(P)
    con[:, C_ONE:C_ONE + P] = 1.0
    tri = np.where(np.arange(P)[:, None] >= np.arange(P)[None, :], 0.0, -1.0e30)
    con[:, C_MASK:C_MASK + P] = tri
    con[:, C_MASK + 2 * P:C_MASK + 3 * P] = tri
    for j in range(4):
        con[32 * j:32 * j + 32, C_ROW + j * P:C_ROW + (j + 1) * P] = 1.0
        con[32 * j:32 * j + 32, C_ROWCOL + j] = 1.0
    con[:, C_IOTA:C_IOTA + TOPK] = np.arange(TOPK)
    freq = np.float32(10000.0) ** (-np.arange(0, ROPE, 2, dtype=np.float32) / np.float32(ROPE))
    con[:, C_FREQ] = np.tile(freq.astype(np.float32), 4)
    return con


def kernel(x, c, positions, tok_norm, ch_norm, ada_w, ada_b, conv_in_w, conv_w, conv_out_w,
           mla_in_w, q_a_norm, kv_a_norm, q_b_w, kv_b_w, q_norm, k_norm, mla_out_w,
           peer_q_w, peer_subkeys, peer_u, peer_v):
    import concourse.bacc as bacc
    from concourse.bass_utils import run_bass_kernel_spmd

    def cols(v):
        return np.ascontiguousarray(v).reshape(-1, P).T

    def panels(w):
        k, n = w.shape[0] // P, w.shape[1] // P
        return w.reshape(k, P, n, P).transpose(2, 1, 0, 3).reshape(n, P, k * P)

    def packed(p, per):
        n, _, w = p.shape
        out = np.zeros((n // per, P, D), p.dtype)
        out[:, :, 0:per * w] = p.reshape(n // per, per, P, w).transpose(0, 2, 1, 3).reshape(n // per, P, per * w)
        return out

    g = [np.asarray(a) for a in (x, c, positions, tok_norm, ch_norm, ada_w, ada_b, conv_in_w, conv_w, conv_out_w,
                                 mla_in_w, q_a_norm, kv_a_norm, q_b_w, kv_b_w, q_norm, k_norm, mla_out_w,
                                 peer_q_w, peer_subkeys, peer_u, peer_v)]
    (x, c, positions, tok_norm, ch_norm, ada_w, ada_b, conv_in_w, conv_w, conv_out_w, mla_in_w, q_a_norm,
     kv_a_norm, q_b_w, kv_b_w, q_norm, k_norm, mla_out_w, peer_q_w, peer_subkeys, peer_u, peer_v) = g

    ci = panels(conv_in_w[0])
    conv_in = np.stack([ci[KB:2 * KB], ci[2 * KB:3 * KB], ci[0:KB]], 1).reshape(3 * KB, P, D)
    lora = Q_LORA + KV_LORA
    rope_in = [np.tile(mla_in_w[0][:, lora + h * HALF_ROPE:lora + (h + 1) * HALF_ROPE], (1, 4)) for h in range(2)]
    mla_in = panels(np.concatenate([mla_in_w[0][:, 0:lora]] + rope_in, 1))
    qb = q_b_w[0].reshape(Q_LORA, HEADS, QK_HEAD)
    qcols = [qb[:, :, 0:NOPE], qb[:, :, NOPE:NOPE + HALF_ROPE], qb[:, :, NOPE + HALF_ROPE:]]
    q_b = packed(panels(np.concatenate([a.reshape(Q_LORA, -1) for a in qcols], 1)), 2)
    kvb = kv_b_w[0].reshape(KV_LORA, HEADS, NOPE + VH)
    k_b = packed(panels(np.ascontiguousarray(kvb[:, :, 0:NOPE]).reshape(KV_LORA, -1)), 2)
    v_b = np.ascontiguousarray(kvb[:, :, NOPE:]).reshape(KVB, P, D)
    stages = [conv_in, panels(conv_out_w[0]), panels(peer_q_w[0]), mla_in, q_b, k_b, v_b, panels(mla_out_w[0]),
              panels(peer_q_w[1])]
    ropes = lambda v: [np.tile(v[NOPE + h * HALF_ROPE:NOPE + (h + 1) * HALF_ROPE], 4)[:, None] for h in range(2)]
    vec = np.concatenate(
        [cols(tok_norm), cols(ch_norm), cols(ada_b), cols(conv_w[0]), cols(q_a_norm), cols(kv_a_norm),
         cols(q_norm[0][0:NOPE])] + ropes(q_norm[0]) + [cols(k_norm[0][0:NOPE])] + ropes(k_norm[0]), 1)
    vec = np.pad(vec, ((0, 0), (0, V_N - vec.shape[1])))
    arrays = {
        "xT": x[0].T.reshape(KB, P, T).transpose(1, 0, 2).reshape(P, KB * T),
        "c": c[0],
        "positions": positions[0],
        "vectors": vec,
        "constants": shape_constants(),
        "ada_rows": ada_w.transpose(0, 2, 1).reshape(96, P, D),
        "panels": np.concatenate(stages, 0),
        "subkeys": peer_subkeys.reshape(2, PAIRS, KEYS, P).transpose(0, 3, 1, 2).reshape(2, P, PAIRS * KEYS),
        "key_numbers": np.broadcast_to(np.repeat(np.arange(KEYS), GT), (P, KEYS * GT)).astype(mybir.dt.np(BF16)),
        "u_panels": peer_u.reshape(2 * KEYS, KEYS, KB, P).transpose(0, 3, 2, 1).reshape(2 * KEYS, P, D),
        "v_panels": peer_v.reshape(2 * KEYS, P, D),
    }
    arrays = {n: np.ascontiguousarray(a) for n, a in arrays.items()}
    nc = bacc.Bacc("TRN2", target_bir_lowering=False, num_devices=1)
    ins = [nc.dram_tensor("in_" + n, a.shape, mybir.dt.from_np(a.dtype), kind="ExternalInput").ap() for n, a in arrays.items()]
    out = nc.dram_tensor("out", (P, KB * T), F32, kind="ExternalOutput").ap()
    program(nc, *ins, out)
    got = run_bass_kernel_spmd(nc, [{"in_" + n: a for n, a in arrays.items()}], core_ids=[0]).results[0]["out"]
    return np.ascontiguousarray(got.reshape(P, KB, T).transpose(1, 0, 2).reshape(D, T).T)[None]
```

```python
from contextlib import ExitStack

import numpy as np

import concourse.bass as bass
from concourse import mybir

F32 = mybir.dt.float32
F32R = mybir.dt.float32r
BF16 = mybir.dt.bfloat16
F16 = mybir.dt.float16
U32 = mybir.dt.uint32
I32 = mybir.dt.int32
ALU = mybir.AluOpType
ACT = mybir.ActivationFunctionType
AX = mybir.AxisListType

P = 128
D = 1024
KB = D // P
T = 256
TT = T // P
HEADS = 8
Q_LORA, KV_LORA, ROPE, NOPE, VH = 384, 256, 64, 128, 128
HALF_ROPE = ROPE // 2
QB, KVB = Q_LORA // P, KV_LORA // P
KEYS, TOPK = 128, 16
PAIRS = 2 * HEADS
SEL = HEADS * TOPK
EPS = 1e-6
QK_HEAD = NOPE + ROPE
RAW = 4
HI, LO = 4, 2
HI_LEAD = HI - 1
ADA = 4
ADA_FIRST = 40
QUART = KEYS // 4
AHEAD = QUART
GT = 16
STEPS = ((0, 1), (2,), (3, 4), (5,))
G_SCALE = 2.0 ** 14
NEG = -3.0e38

C_ID, C_ONE, C_MASK = 0, 128, 256
C_HEAD = 640
C_GROUP = C_HEAD + 15
C_FIRST = C_GROUP + 12
C_SPREAD = C_FIRST + 8
C_FREQ = C_SPREAD + 2 * P
C_N = C_FREQ + 1
V_TOK, V_CH, V_ADAB, V_CONV, V_QA, V_KVA, V_QN, V_KN = 0, 16, 32, 128, 152, 155, 157, 160
V_N = 164

STAGES = [("conv_in", 24), ("conv_out", 8), ("sel0", 24), ("ahead0", 24), ("mix0", 192), ("last0", 32),
          ("mla_in", 7), ("q_b", 6), ("k_b", 4), ("v_b", 2), ("mla_out", 8),
          ("sel1", 24), ("ahead1", 24), ("mix1", 192), ("last1", 32)]
DENSE, _d = {}, 0
for _name, _count in [("conv_in", 24), ("conv_out", 8), ("peer_q0", 16), ("mla_in", 7), ("q_b", 6), ("k_b", 4),
                      ("v_b", 2), ("mla_out", 8), ("peer_q1", 16)]:
    DENSE[_name] = _d
    _d += _count
BASE, _n = {}, 0
for _name, _count in STAGES:
    BASE[_name] = _n
    _n += _count
WIDTHS = {BASE["q_b"] + _j: 2 * Q_LORA for _j in range(6)} | {BASE["k_b"] + _j: 2 * KV_LORA for _j in range(4)}
TWO_PI = 2.0 * np.pi
PI_1 = 6.28125
PI_2 = float(np.float32(np.floor((TWO_PI - PI_1) * 2.0 ** 21) / 2.0 ** 21))
PI_3 = float(np.float32(TWO_PI - PI_1 - PI_2))
ROUND = 12582912.0


def program(nc, xT_in, c_in, pos_in, vec_in, con_in, ada_in, pan_in, key_in, iota_in, u_in, v_in, out):
    ctx = ExitStack()
    with ctx:
        def sb(name, shape, dt=F32):
            return ctx.enter_context(nc.sbuf_tensor(name, shape, dt))

        def sem(name):
            return ctx.enter_context(nc.semaphore(name))

        xT = sb("xT", [P, KB * T])
        con = sb("con", [P, C_N])
        vec = sb("vec", [P, V_N])
        eps = sb("eps", [P, 1])
        crow = sb("crow", [P, D])
        mod = sb("mod", [P, 96])
        ada_sum = sb("ada_sum", [P, 4])
        gain = sb("gain", [P, KB])
        raw = sb("raw", [P, RAW, D])
        w_hi = sb("w_hi", [P, HI, D], F32R)
        w_lo = sb("w_lo", [P, LO, D], F32R)
        act_hi = sb("act_hi", [P, KB * T], F32R)
        act_lo = sb("act_lo", [P, KB * T], F32R)
        ada1 = sb("ada1", [P, D])
        arena = sb("arena", [P, 2 * QUART * T])
        ring_g = sb("ring_g", [P, AHEAD * T])
        iota_x = sb("iota_x", [P, KEYS * GT], BF16)
        ia_t = sb("ia_t", [P, T], BF16)
        ib_t = sb("ib_t", [P, T], BF16)
        g32_t = sb("g32_t", [P, T])
        gh_t = sb("gh_t", [P, T], F16)
        gl_t = sb("gl_t", [P, T], F16)
        hot_b = sb("hot_b", [P, 2, KEYS * GT], BF16)
        hot_a = sb("hot_a", [P, 2, QUART * GT], BF16)
        hot_g = sb("hot_g", [P, 2, 2 * QUART * GT], F16)
        w32 = sb("w32", [P, 2 * T])
        wt_hi = sb("wt_hi", [P, 2, 2 * T], F32R)
        wt_lo = sb("wt_lo", [P, 2, 2 * T], F32R)
        zero = sb("zero", [P, P], F32R)
        warm_to = sb("warm_to", [P, 1])
        act32 = ring_g[:, 0:2048]
        s_sb = ring_g[:, 2048:3200].rearrange("p (e n) -> p e n", e=3)
        pT = ring_g[:, 3200:3968].rearrange("p (e n) -> p e n", e=2)
        cosb = ring_g[:, 3584:3840]
        sinb = ring_g[:, 3840:4096]
        rms = ring_g[:, 4096:4608]
        rstd = ring_g[:, 4608:5120]
        q_sb = ring_g[:, 5120:5632].rearrange("p (e n) -> p e n", e=2)
        ang = ring_g[:, 7296:7552]
        tmp = ring_g[:, 7552:7808]
        posi = ring_g[:, 7808:8064].bitcast(I32)

        ada = arena[:, 10240:10240 + ADA * D].rearrange("p (a d) -> p a d", d=D)
        sq = arena[:, 0:2048]
        c_sb = arena[:, 2048:2048 + T]
        u_pad = arena[:, 2560:2560 + T + 2]
        conv_t = arena[:, 3072:3072 + T]
        sq_sum = arena[:, 3328:3328 + T]
        qn = arena[:, 0:2048]
        qr = arena[:, 2048:3072]
        kn = arena[:, 3072:5120]
        kr = arena[:, 5120:6144]
        vv = arena[:, 6144:8192]
        sqn = arena[:, 8192:10240]
        sqr = arena[:, 10240:11264]
        rotq = arena[:, 8192:9216]
        rot = arena[:, 11264:12288]
        sqk = arena[:, 12288:14336]
        sqkr = arena[:, 14336:14848]
        qz = arena[:, 12288:16384]
        kraw = act32[:, 0:512]
        lat = act32[:, 512:512 + 5 * T]
        smax = sb("smax", [P, 3, 2])
        ssum = sb("ssum", [P, 3, 2])
        topv = arena[:, 0:TT * 2 * TOPK]
        work = arena[:, 3072:3072 + 2 * TT * P]
        cand = arena[:, 512:512 + TT * 256]
        cwork = arena[:, 1024:1024 + TT * 256]
        bestv = arena[:, 1536:1536 + TT * TOPK]
        dec_f = arena[:, 2048:2048 + SEL].bitcast(BF16)
        keyx = arena[:, 12288:16384].bitcast(BF16).rearrange("p (c n) -> p c n", c=2 * TT)
        eq = arena[:, 4096:4096 + SEL * TOPK // 2].bitcast(BF16)
        eab = arena[:, 6144:6144 + TT * 2 * SEL]
        esum = arena[:, 6656:6656 + 16]
        top_i = arena[:, 10240:10752].bitcast(U32).rearrange("p (t n) -> p t n", t=TT)
        best_v = arena[:, 10752:11008].rearrange("p (t n) -> p t n", t=TT)
        best_p = arena[:, 11008:11264].bitcast(U32).rearrange("p (t n) -> p t n", t=TT)
        gate = arena[:, 11264:11520].rearrange("p (t n) -> p t n", t=TT)
        topi = arena[:, 11520:11584].bitcast(U32)
        bestp = arena[:, 11584:11616].bitcast(U32)
        dec_u = arena[:, 11648:11904].bitcast(U32).rearrange("p (x n) -> p x n", x=2)
        keys = arena[:, 8192:8192 + PAIRS * KEYS]
        yrow = arena[:, 0:TT * D]

        ps = [ctx.enter_context(nc.psum_tensor(f"bank{b}", [P, 512], F32)) for b in range(8)]
        PAN = ps[0:2]
        STAT = ps[2]
        SC = ps[3:5]
        TR = ps[5:7]
        OV = ps[7]
        YB = ps[2:6]
        GB = ps[6:8]
        BC = [ps[b] for b in (0, 1, 3, 4, 5, 6)]

        ident = con[:, C_ID:C_ID + P]
        ones = con[:, C_ONE:C_ONE + P]

        s_const = sem("constants_landed")
        s_iota = sem("later_constants_landed")
        s_eps = sem("eps_set")
        s_key = sem("subkeys_landed")
        s_out = sem("output_stored")
        s_pos = sem("positions_landed")
        landed = [sem(f"panel_landed{i}") for i in range(RAW)]
        hi_done = sem("panel_hi_ready")
        lo_done = sem("panel_lo_ready")
        pan_done = sem("panel_multiplied")
        evac = {n: sem(f"evacuated_{n}") for n, _ in STAGES}
        ada_landed = [sem(f"ada_landed{i}") for i in range(ADA)]
        ada_used = sem("ada_rows_used")
        ada1_landed = sem("ada1_landed")
        ada1_used = sem("ada1_used")
        ada_seen = sem("ada_slot_seen_free")
        s_silu = sem("silu_c_ready")
        x_ready = sem("x_ready")
        sq_ready = sem("squares_ready")
        sum_ready = sem("square_sums_ready")
        rms_ready = sem("rms_ready")
        sq_block = sem("block_squares_ready")
        sq_summed = sem("square_blocks_summed")
        scaled = sem("x_scaled")
        norm_hi = sem("normalised_hi_ready")
        norm_ready = sem("normalised_split")
        f32_ready = sem("activations_f32_ready")
        act_hi_ready = sem("activations_hi_ready")
        act_ready = sem("activations_split")
        sc_done = sem("key_scores_ready")
        sc_used = sem("key_scores_used")
        sc_seen = sem("key_scores_seen")
        gate_in = sem("gate_exponents_ready")
        gate_exp = sem("gate_exp_ready")
        keyx_ready = sem("best_keys_repeated")
        dec_done = sem("chosen_experts_decoded")
        idx_done = sem("chosen_experts_turned")
        hot_ready = sem("one_hots_ready")
        g_done = sem("gates_scattered")
        g_first = sem("first_parts_of_gates_copied")
        g_read = sem("gates_copied")
        pan_read = [sem(f"bank_read{l}") for l in range(2)]
        w_mul = sem("weighted_gelu_ready")
        wt_hi_ready = sem("weighted_gelu_hi")
        wt_ready = sem("weighted_gelu_split")
        y0_copied = sem("y_rows_of_tile0_ready")
        y1_copied = sem("y_rows_of_tile1_ready")
        yt_done = sem("y_transposed")
        yt_added = sem("y_added")
        conv_gated = sem("gated_convolution_ready")
        conv_hi = sem("gated_convolution_hi")
        conv_split = sem("gated_convolution_split")
        lat_in = sem("latents_copied")
        lat_sq = sem("latent_squares")
        lat_sum = sem("latent_sums")
        lat_rms = sem("latent_rms")
        v_copied = sem("values_copied")
        head_sq = sem("head_squares")
        head_sum = sem("head_sums")
        head_rms = sem("head_rms")
        head_rstd = sem("head_rstd")
        bc_done = sem("head_rstd_spread")
        bc_used = sem("head_rstd_applied")
        q_rotated = sem("q_rotated")
        qz_ready = sem("q_by_head_ready")
        trig_in = sem("angles_reduced")
        trig = sem("sin_cos_ready")
        qk_ready = sem("qk_ready")
        s_done = sem("scores_ready")
        s_masked = sem("scores_masked")
        p_exp = sem("probs_exp")
        p_norm = sem("probs_normalised")
        p_tr = sem("probs_transposed")
        p_copied = sem("probs_copied")
        o_done = sem("head_output_ready")
        o_hi = sem("head_output_hi")
        o_copied = sem("head_output_split")

        block = ctx.enter_context(nc.Block())

        def ring(stage, j, unroll=0, it=0):
            i = BASE[stage] + j
            step = unroll // RAW * 16
            return i % RAW, i % LO, it * step + 16 * (i // RAW + 1), it * unroll + (i + 1)

        @block.sync
        def _(sp):
            def load(src, index, stage, j, unroll=0, it=0, width=D):
                slot, _, _, n = ring(stage, j, unroll, it)
                sp.wait_ge(lo_done, n)
                sp.dma_start(raw[:, slot, 0:width], src[bass.ds(index, 1), :, 0:width].rearrange("o p n -> p (o n)")
                             ).then_inc(landed[slot], 16)

            def load_panel(stage, j, unroll=0, it=0, width=D):
                load(pan_in, it * unroll + (DENSE[stage] + j), stage, j, unroll, it, width)

            def load_ada(n, row, slot):
                sp.wait_ge(ada_used, n + 1)
                sp.dma_start(ada[:, slot, :], ada_in[bass.ds(row, 1)].rearrange("o p n -> p (o n)")
                             ).then_inc(ada_landed[slot], 16)

            def load_experts(l):
                k0 = KEYS * l
                with sp.Fori(0, 2) as it:
                    for h in range(4):
                        for p in range(2):
                            load(pan_in, it * 8 + (DENSE[f"peer_q{l}"] + 2 * h + p), f"sel{l}", 3 * h + p, 12, it)
                        load(u_in, it * 4 + (k0 + h), f"sel{l}", 3 * h + 2, 12, it)
                if l == 0:
                    sp.dma_start(con[:, C_MASK:C_N], con_in[:, C_MASK:C_N]).then_inc(s_iota, 16)
                    sp.dma_start(iota_x[:], iota_in).then_inc(s_iota, 16)
                with sp.Fori(0, 6) as it:
                    for j in range(4):
                        load(u_in, it * 4 + (k0 + HEADS + j), f"ahead{l}", j, 4, it)
                for q in range(3):
                    with sp.Fori(0, 8) as it:
                        for e in range(4):
                            v = k0 + q * QUART + e
                            load(u_in, it * 4 + (v + AHEAD), f"mix{l}", 64 * q + 2 * e, 8, it)
                            load(v_in, it * 4 + v, f"mix{l}", 64 * q + 2 * e + 1, 8, it)
                with sp.Fori(0, 8) as it:
                    for j in range(4):
                        load(v_in, it * 4 + (k0 + 3 * QUART + j), f"last{l}", j, 4, it)

            sp.dma_start(crow[:], c_in.partition_broadcast(P)).then_inc(s_const, 16)
            sp.dma_start(vec[:], vec_in).then_inc(s_const, 16)
            sp.dma_start(xT[:], xT_in).then_inc(s_const, 16)
            sp.dma_start(con[:, 0:C_MASK], con_in[:, 0:C_MASK]).then_inc(s_const, 16)
            for first in (KB, 0):
                with sp.Fori(0, 2) as it:
                    for j in range(ADA):
                        load_ada(it * ADA + (KB - first + j), it * ADA + (first + j), j)
                for j in range(2):
                    load_panel("conv_in", (0 if first else 2) + j)
            with sp.Fori(0, 2) as it:
                for b in range(4):
                    for j in range(2):
                        load_ada(it * 8 + (16 + 2 * b + j), it * 8 + (16 + 2 * b + j), (2 * b + j) % ADA)
                    for j in range(3):
                        load_panel("conv_in", 3 * b + j + RAW, 12, it)
            for j in range(8):
                load_ada(32 + j, 32 + j, j % ADA)
                if j < 4:
                    load_panel("conv_out", RAW + j)
            sp.dma_start(keys, key_in[0]).then_inc(s_key, 16)
            load_experts(0)
            for j in range(RAW):
                load_panel("mla_in", j)
            sp.wait_ge(x_ready, 2)
            sp.dma_start(posi, pos_in.partition_broadcast(P)).then_inc(s_pos, 16)
            for j in range(RAW, 7):
                load_panel("mla_in", j)
            for j in range(6):
                load_panel("q_b", j, width=2 * Q_LORA)
            for j in range(4):
                load_panel("k_b", j, width=2 * KV_LORA)
            for j in range(2):
                load_panel("v_b", j)
            with sp.Fori(0, 2) as it:
                for j in range(4):
                    load_panel("mla_out", j, 4, it)
            sp.wait_ge(o_copied, HEADS)
            sp.dma_start(keys, key_in[1]).then_inc(s_key, 16)
            load_experts(1)
            sp.wait_ge(x_ready, 4)
            sp.dma_start(out, xT[:]).then_inc(s_out, 16)
            sp.wait_ge(s_out, 16)

        @block.tensor
        def _(pe):
            def product(bank, slots, col0, kb, act0, halves=None):
                for k in range(kb):
                    if halves and k % (KB // 2) == 0:
                        pe.wait_ge(halves[0], halves[1] + 1 + k // (KB // 2))
                    w = slice(col0 + k * P, col0 + (k + 1) * P)
                    a = slice((act0 + k) * T, (act0 + k + 1) * T)
                    pe.matmul(bank, w_hi[:, slots[0], w], act_hi[:, a], start=(k == 0), stop=False)
                    pe.matmul(bank, w_hi[:, slots[0], w], act_lo[:, a], start=False, stop=False)
                    last = pe.matmul(bank, w_lo[:, slots[1], w], act_hi[:, a], start=False, stop=(k == kb - 1))
                return last

            def wait_panel(stage, j, unroll=0, it=0):
                slots = wait_split(stage, j, unroll, it)
                pe.wait_ge(evac[stage], it * unroll + (j + 1))
                return slots

            def full_panel(stage, j, unroll=0, it=0, halves=None):
                slots = wait_panel(stage, j, unroll, it)
                product(PAN[j % 2][:, 0:T], slots, 0, KB, 0, halves).then_inc(pan_done, 1)

            def square_sums(n):
                for t in range(TT):
                    pe.wait_ge(sq_ready, n - 1 + t + 1)
                    for k in range(KB):
                        mm = pe.matmul(STAT[:, t * P:(t + 1) * P], ones, sq[:, t * D + k * P:t * D + (k + 1) * P],
                                       start=(k == 0), stop=(k == KB - 1))
                mm.then_inc(sum_ready, 1)

            def block_square_sum(n):
                pe.wait_ge(sq_summed, n // 2)
                pe.matmul(STAT[:, 0:T], ones, sq_sum, start=True, stop=True).then_inc(sum_ready, 1)

            def wait_split(stage, j, unroll, it):
                slot, lo_slot, _, n = ring(stage, j, unroll, it)
                pe.wait_ge(lo_done, n + RAW)
                return slot, lo_slot

            def u_panel(l, stage, j, unroll, it, nth, bank, halves=None):
                slots = wait_split(stage, j, unroll, it)
                pe.wait_ge(pan_read[l], nth)
                product(bank[:, 0:T], slots, 0, KB, 0, halves).then_inc(pan_done, 1)

            def v_panel(stage, j, unroll, it, par, e):
                slots = wait_split(stage, j, unroll, it)
                for t in range(TT):
                    a = slice(e * T + t * P, e * T + (t + 1) * P)
                    for wt, parts in ((wt_hi, (0, 1)), (wt_lo, (0,))):
                        for v in parts:
                            for n in range(2):
                                mm = pe.matmul(YB[2 * t + n][:], wt[:, par, a], (w_hi, w_lo)[v][:, slots[v], n * 512:(n + 1) * 512],
                                               start=False, stop=False, skip_group_check=True)
                mm.then_inc(pan_done, 1)

            def scatter_side(l, par, count):
                pe.wait_ge(hot_ready, count)
                pe.wait_ge(g_read, count + 1)
                hb = hot_b[:, par, :].rearrange("p (b t) -> p b t", t=GT)
                hg = hot_g[:, par, :].rearrange("p (a t) -> p a t", t=GT)
                for t in range(GT):
                    o = t % (GT // 2) * 2 * QUART
                    mm = pe.matmul(GB[t // (GT // 2)][:, o:o + 2 * QUART], hb[:, :, t], hg[:, :, t], start=True,
                                   stop=True)
                mm.then_inc(g_done, 1)

            def scatter(l, par, count):
                pe.wait_ge(hot_ready, count)
                pe.wait_ge(g_read, count)
                hb = hot_b[:, par, :].rearrange("p (b t) -> p b t", t=GT)
                hg = hot_g[:, par, :].rearrange("p (x a t) -> p x a t", x=2, t=GT)
                for t in range(GT):
                    for x in range(2):
                        mm = pe.matmul(GB[par][:, t * QUART:(t + 1) * QUART], hb[:, :, t], hg[:, x, :, t],
                                       start=(x == 0), stop=(x == 1))
                mm.then_inc(g_done, 1)

            def peer(l):
                block_square_sum(2 * l + 2)
                pe.wait_ge(s_key, 16 * (l + 1))
                def scores(it, h, p):
                    pe.wait_ge(pan_read[l], it * 12 + (3 * h + p + 3))
                    pe.wait_ge(sc_used, it * 8 + (16 * l + 2 * h + p + 1))
                    for t in range(TT):
                        mm = pe.matmul(SC[p][:, t * P:(t + 1) * P], q_sb[:, p, t * P:(t + 1) * P],
                                       keys[:, bass.ds((it * 8 + (2 * h + p)) * KEYS, KEYS)], start=True, stop=True)
                    mm.then_inc(sc_done, 1)

                with pe.Fori(0, 2) as it:
                    for h in range(4):
                        for j in range(3):
                            i = 3 * h + j
                            u_panel(l, f"sel{l}", i, 12, it, it * 12 + (i + 1), PAN[i % 2],
                                    halves=None if i else (norm_ready, 4 * l + 2))
                            if j:
                                scores(it, h, j - 1)
                with pe.Fori(0, 3) as it:
                    for j in range(4):
                        u_panel(l, f"ahead{l}", j, 4, it, it * 4 + (25 + j), PAN[j % 2])
                for t in range(TT):
                    pe.wait_ge(dec_done, TT * l + t + 1)
                    for n, src in enumerate((eab[:, (2 * t) * SEL:(2 * t + 1) * SEL],
                                             eab[:, (2 * t + 1) * SEL:(2 * t + 2) * SEL], gate[:, t, :])):
                        mm = pe.transpose(GB[t][:, n * P:(n + 1) * P], src, ident)
                    mm.then_inc(idx_done, 1)
                for j in range(4):
                    u_panel(l, f"ahead{l}", 12 + j, 0, 0, 37 + j, PAN[j % 2])
                    scatter(l, j % 2, 64 * l + j + 1)
                with pe.Fori(0, 2) as it:
                    for j in range(4):
                        u_panel(l, f"ahead{l}", 16 + j, 4, it, it * 4 + (41 + j), PAN[j % 2])
                        for g in STEPS[j]:
                            scatter(l, g % 2, it * 6 + (64 * l + 4 + g + 1))
                for n in range(4):
                    pe.matmul(YB[n][:], zero[:], act_hi[:, 0:512], start=True, stop=False, skip_group_check=True)
                for q in range(3):
                    with pe.Fori(0, 8) as it:
                        for s in range(2):
                            j = 64 * q + 4 * s
                            u_panel(l, f"mix{l}", j, 8, it, it * 4 + (49 + 32 * q + 2 * s), PAN[0])
                            pe.wait_ge(wt_ready, it * 2 + (64 * l + 16 * q + s + 1))
                            v_panel(f"mix{l}", j + 1, 8, it, s, 0)
                            u_panel(l, f"mix{l}", j + 2, 8, it, it * 4 + (50 + 32 * q + 2 * s), PAN[1])
                            scatter_side(l, s, it * 2 + (64 * l + 16 * (q + 1) + s + 1))
                            v_panel(f"mix{l}", j + 3, 8, it, s, 1)
                with pe.Fori(0, 8) as it:
                    for s in range(2):
                        pe.wait_ge(wt_ready, it * 2 + (64 * l + 48 + s + 1))
                        v_panel(f"last{l}", 2 * s, 4, it, s, 0)
                        v_panel(f"last{l}", 2 * s + 1, 4, it, s, 1)
                for t in range(TT):
                    pe.wait_ge((y0_copied, y1_copied)[t], l + 1)
                    for g in range(2):
                        if 2 * t + g >= 2:
                            pe.wait_ge(yt_added, 4 * l + 2 * t + g - 1)
                        for k in range(4):
                            o = t * D + (4 * g + k) * P
                            mm = pe.transpose(GB[g][:, k * P:(k + 1) * P], yrow[:, o:o + P], ident)
                        mm.then_inc(yt_done, 1)

            def latent_sums(bank, n, k0, blocks):
                pe.wait_ge(lat_sq, n)
                for k in range(blocks):
                    mm = pe.matmul(bank[:, 0:T], ones, sqn[:, (k0 + k) * T:(k0 + k + 1) * T],
                                   start=(k == 0), stop=(k == blocks - 1))
                mm.then_inc(lat_sum, 1)

            def head_sums(bank, n, nope, rope):
                pe.wait_ge(head_sq, n)
                for h in range(HEADS):
                    pe.matmul(bank[0:HEADS, 0:T], con[:, C_HEAD + 7 - h:C_HEAD + 15 - h], nope[:, h * T:(h + 1) * T],
                              start=(h == 0), stop=False)
                for i, (src, c) in enumerate(rope):
                    mm = pe.matmul(bank[0:HEADS, 0:T], con[:, c:c + HEADS], src, start=False,
                                   stop=(i == len(rope) - 1))
                mm.then_inc(head_sum, 1)

            def attention():
                square_sums(3)
                for j in range(7):
                    full_panel("mla_in", j, halves=None if j else (norm_ready, 4))
                    if j == 4:
                        latent_sums(OV, 1, 0, QB)
                latent_sums(STAT, 2, QB, KVB)
                pe.wait_ge(act_ready, 1)
                for j in range(6):
                    slots = wait_panel("q_b", j)
                    product(PAN[j % 2][:, 0:T], slots, 0, QB, 0)
                    product(PAN[j % 2][:, T:2 * T], slots, Q_LORA, QB, 0).then_inc(pan_done, 1)
                pe.wait_ge(act_ready, 2)
                for j in range(4):
                    slots = wait_panel("k_b", j)
                    product(PAN[j % 2][:, 0:T], slots, 0, KVB, QB)
                    product(PAN[j % 2][:, T:2 * T], slots, KV_LORA, KVB, QB).then_inc(pan_done, 1)
                head_sums(OV, 1, sqn, [(sqr[:, (2 * x + i) * T:(2 * x + i + 1) * T], C_GROUP + 4 - 4 * i)
                                       for x in range(2) for i in range(2)])
                hi_slots, lo_slots = zip(*[ring("v_b", k)[0:2] for k in range(KVB)])
                pe.wait_ge(lo_done, ring("v_b", KVB - 1)[3] + RAW)
                for n, bank in enumerate((SC[0], SC[1], TR[0], TR[1])):
                    for k in range(KVB):
                        a = slice((QB + k) * T + n // 2 * P, (QB + k) * T + n // 2 * P + P)
                        w = slice(n % 2 * 512, n % 2 * 512 + 512)
                        pe.matmul(bank[:], act_hi[:, a], w_hi[:, hi_slots[k], w], start=(k == 0), stop=False)
                        pe.matmul(bank[:], act_lo[:, a], w_hi[:, hi_slots[k], w], start=False, stop=False)
                        mm = pe.matmul(bank[:], act_hi[:, a], w_lo[:, lo_slots[k], w], start=False, stop=(k == KVB - 1))
                mm.then_inc(pan_done, 2)
                head_sums(STAT, 2, sqk, [(sqkr[:, x * T:(x + 1) * T], C_FIRST) for x in range(2)])
                for i in range(10):
                    x5 = i if i < 2 else (i - 2) // 4
                    r = rstd[0:HEADS, x5 * T:(x5 + 1) * T]
                    if i < 2:
                        pe.wait_ge(head_rstd, i + 1)
                    if i == 2:
                        pe.wait_ge(v_copied, 1)
                    if i >= len(BC):
                        pe.wait_ge(bc_used, i - len(BC) + 1)
                    for e in range(2):
                        if i < 2:
                            w = con[0:HEADS, C_SPREAD + e * P:C_SPREAD + (e + 1) * P]
                        else:
                            h = 2 * ((i - 2) % 4) + e
                            w = ident[0:HEADS, h:h + 1].broadcast_to([HEADS, P])
                        mm = pe.matmul(BC[i % len(BC)][:, e * T:(e + 1) * T], w, r, start=True, stop=True)
                    mm.then_inc(bc_done, 1)
                pe.wait_ge(qz_ready, 1)
                pe.wait_ge(qk_ready, 1)
                for i in range(HEADS + 3):
                    if i < HEADS:
                        h = i
                        if h >= 2:
                            pe.wait_ge(s_masked, h - 1)
                        for t, (c0, c1) in enumerate(((0, P), (P, 3 * P))):
                            o, n = SC[h % 2][:, c0:c1], c1 - c0
                            q0 = h * T + t * P
                            pe.matmul(o, qn[:, q0:q0 + P], kn[:, h * T:h * T + n], start=True, stop=False)
                            for x in range(2):
                                z0 = (2 * h + x) * T + t * P
                                k0 = (2 * x + h // 4) * T
                                mm = pe.matmul(o, qz[:, z0:z0 + P], rot[:, k0:k0 + n], start=False, stop=(x == 1))
                        mm.then_inc(s_done, 1)
                    if 2 <= i <= HEADS + 1:
                        h = i - 2
                        pe.wait_ge(p_norm, h + 1)
                        if h >= 2:
                            pe.wait_ge(p_copied, h - 1)
                        for b in range(3):
                            mm = pe.transpose(TR[h % 2][:, b * P:(b + 1) * P], s_sb[:, h % 3, b * P:(b + 1) * P], ident)
                        mm.then_inc(p_tr, 1)
                    if i >= 3:
                        h = i - 3
                        pe.wait_ge(p_copied, h + 1)
                        if h >= 2:
                            pe.wait_ge(o_copied, h - 1)
                        o = (OV, STAT)[h % 2]
                        v0, v1 = vv[:, h * VH:(h + 1) * VH], vv[:, D + h * VH:D + (h + 1) * VH]
                        pe.matmul(o[:, 0:P], v0, pT[:, h % 2, 0:P], start=True, stop=True)
                        pe.matmul(o[:, P:2 * P], v0, pT[:, h % 2, P:2 * P], start=True, stop=False)
                        pe.matmul(o[:, P:2 * P], v1, pT[:, h % 2, 2 * P:3 * P], start=False, stop=True
                                  ).then_inc(o_done, 1)
                pe.wait_ge(o_copied, HEADS)
                with pe.Fori(0, 2) as it:
                    for j in range(4):
                        full_panel("mla_out", j, 4, it)

            pe.sem_inc(pan_done, HI)
            pe.sem_inc(g_done, 2)
            pe.wait_ge(s_const, 64)
            square_sums(1)
            with pe.Fori(0, 2) as it:
                for j in range(12):
                    full_panel("conv_in", j, 12, it, halves=None if j else (norm_ready, 0))
            with pe.Fori(0, 2) as it:
                for j in range(4):
                    full_panel("conv_out", j, 4, it, halves=None if j else (conv_split, 0))
            peer(0)
            attention()
            peer(1)

        @block.scalar
        def _(act):
            def split_hi(stage, j, unroll=0, it=0):
                slot, _, count, n = ring(stage, j, unroll, it)
                width = D if unroll else WIDTHS.get(BASE[stage] + j, D)
                act.wait_ge(landed[slot], count)
                act.wait_ge(pan_done, n)
                nc.scalar.copy(w_hi[:, slot, 0:width], raw[:, slot, 0:width]).then_inc(hi_done, 1)

            def split_act(n, c0, width):
                act.wait_ge(f32_ready, n)
                nc.scalar.copy(act_hi[:, c0:c0 + width], lat[:, c0:c0 + width]).then_inc(act_hi_ready, 1)

            def warm(func):
                nc.scalar.activation(warm_to[:], eps[:], func)

            def squares(t):
                by_block = lambda a, w: a.rearrange("p (k t) -> p k t", t=w)
                nc.scalar.activation(by_block(sq[:, t * D:(t + 1) * D], P), by_block(xT[:], T)[:, :, t * P:(t + 1) * P],
                                     ACT.Square).then_inc(sq_ready, 1)

            def rms_of(n):
                act.wait_ge(sum_ready, n)
                nc.scalar.activation(rms[:, 0:T], STAT[:, 0:T], ACT.Sqrt, bias=eps[:], scale=1.0 / D
                                     ).then_inc(rms_ready, 1)

            def normalise(n, l, s0):
                for half in range(2):
                    act.wait_ge(scaled, 2 * n - 1 + half)
                    for k in range(half * KB // 2, (half + 1) * KB // 2):
                        c = l * 48 + s0 * KB + k
                        i = nc.scalar.activation(act_hi[:, k * T:(k + 1) * T], act32[:, k * T:(k + 1) * T],
                                                 ACT.Identity, bias=mod[:, c:c + 1])
                    i.then_inc(norm_hi, 1)

            def residual_panels(stage):
                warm(ACT.Sqrt)
                for i in range(KB):
                    act.wait_ge(evac[stage], i + 3)
                    c = slice(i * T, (i + 1) * T)
                    nc.scalar.activation(sq[:, c], xT[:, c], ACT.Square).then_inc(sq_block, 1)
                    if i + HI_LEAD < KB:
                        split_hi(stage, i + HI_LEAD)

            def gelu(l, stage, j, unroll, it, bank, slot):
                act.wait_ge(pan_done, ring(stage, j, unroll, it)[3] + HI)
                nc.scalar.activation(ring_g[:, bass.ds(slot * T, T)], bank[:, 0:T], ACT.Gelu).then_inc(pan_read[l], 1)

            def copy_gates(quarter, par, count, token0):
                act.wait_ge(g_done, count + 2)
                g = arena[:, quarter % 2 * QUART * T:(quarter % 2 + 1) * QUART * T].rearrange("p (a t) -> p a t", t=T)
                nc.scalar.copy(g[:, :, bass.ds(token0, GT)], GB[par][:].rearrange("p (t a) -> p a t", a=QUART)
                               ).then_inc(g_read, 1)

            def copy_first(quarter, count, token0):
                act.wait_ge(g_done, count + 2)
                g = arena[:, quarter % 2 * QUART * T:(quarter % 2 + 1) * QUART * T].rearrange("p (a t) -> p a t", t=T)
                for n in range(2):
                    i = nc.scalar.copy(g[:, :, bass.ds(token0 + n * (GT // 2), GT // 2)],
                                       GB[n][:].rearrange("p (t x a) -> p x a t", x=2, a=QUART)[:, 0])
                i.then_inc(g_first, 1)

            def split_weighted(par, count):
                act.wait_ge(w_mul, count)
                nc.scalar.copy(wt_hi[:, par, :], w32[:]).then_inc(wt_hi_ready, 1)

            def peer(l):
                rms_of(2 * l + 2)
                for j in range(2):
                    split_hi(f"sel{l}", j)
                normalise(2 * l + 2, l, 3)
                split_hi(f"sel{l}", 2)
                warm(ACT.Gelu)
                act.sem_inc(pan_read[l], 2)
                with act.Fori(0, 2) as it:
                    for h in range(4):
                        for j in range(3):
                            i = 3 * h + j
                            split_hi(f"sel{l}", i + HI_LEAD, 12, it)
                            if j < 2:
                                act.wait_ge(pan_done, ring(f"sel{l}", i, 12, it)[3] + HI)
                                nc.scalar.copy(q_sb[:, j, :], PAN[i % 2][:, 0:T]).then_inc(pan_read[l], 1)
                            else:
                                gelu(l, f"sel{l}", i, 12, it, PAN[i % 2], it * 4 + h)

                def ahead_u(j, unroll=0, it=0):
                    split_hi(f"ahead{l}", j + HI_LEAD, unroll, it)
                    gelu(l, f"ahead{l}", j, unroll, it, PAN[j % 2], it * 4 + (HEADS + j))

                for j in range(6):
                    ahead_u(j)
                act.wait_ge(gate_in, l + 1)
                for j in range(4):
                    t, x = j // 2, j % 2
                    nc.scalar.copy(keyx[:, j, :].rearrange("p (h j k) -> p h j k", h=HEADS, k=TOPK),
                                   top_i[:, t, :].rearrange("p (h x j) -> p h x j", h=HEADS, x=2)[:, :, x, :]
                                   .unsqueeze(3).broadcast_to([P, HEADS, TOPK, TOPK])).then_inc(keyx_ready, 1)
                    if j == 0:
                        nc.scalar.activation(gate, gate, ACT.Exp).then_inc(gate_exp, 1)
                        warm(ACT.Gelu)
                    ahead_u(6 + j)
                for j in range(10, 12):
                    ahead_u(j)
                for j in range(4):
                    ahead_u(12 + j)
                    copy_gates(0, j % 2, 64 * l + j + 1, j * GT)
                with act.Fori(0, 2) as it:
                    for j in range(4):
                        ahead_u(16 + j, 4, it)
                        for g in STEPS[j]:
                            copy_gates(0, g % 2, it * 6 + (64 * l + 4 + g + 1), (it * 6 + (4 + g)) * GT)
                split_weighted(0, 64 * l + 1)
                for q in range(3):
                    with act.Fori(0, 8) as it:
                        for s in range(2):
                            j = 64 * q + 4 * s
                            split_hi(f"mix{l}", j + HI_LEAD, 8, it)
                            gelu(l, f"mix{l}", j, 8, it, PAN[0], it * 4 + 2 * s)
                            split_hi(f"mix{l}", j + 1 + HI_LEAD, 8, it)
                            split_hi(f"mix{l}", j + 2 + HI_LEAD, 8, it)
                            gelu(l, f"mix{l}", j + 2, 8, it, PAN[1], it * 4 + (2 * s + 1))
                            copy_first(q + 1, it * 2 + (64 * l + 16 * (q + 1) + s + 1), (it * 2 + s) * GT)
                            split_weighted(1 - s, it * 2 + (64 * l + 16 * q + s + 2))
                            split_hi(f"mix{l}", j + 3 + HI_LEAD, 8, it)

                def last_body(it, end):
                    for s in range(2):
                        if not (end and s and l):
                            split_hi(f"last{l}", 2 * s + HI_LEAD, 4, it)
                        if not (end and s):
                            split_weighted(1 - s, it * 2 + (64 * l + 48 + s + 2))
                        if not (end and l):
                            split_hi(f"last{l}", 2 * s + 1 + HI_LEAD, 4, it)

                with act.Fori(0, 7) as it:
                    last_body(it, False)
                last_body(7, True)
                act.wait_ge(pan_done, ring(f"last{l}", 31)[3] + HI)
                for n in range(2):
                    i = nc.scalar.mul(yrow[:, n * 512:(n + 1) * 512], YB[n][:], 1.0 / G_SCALE)
                i.then_inc(y0_copied, 1)
                if l == 0:
                    warm(ACT.Sqrt)
                    for t in range(TT):
                        act.wait_ge(yt_added, 2 * t + 2)
                        squares(t)

            act.sem_inc(g_read, 2)
            act.wait_ge(s_const, 64)
            nc.scalar.activation(crow[:], crow[:], ACT.Silu).then_inc(s_silu, 1)
            for t in range(TT):
                squares(t)
            act.wait_ge(s_eps, 1)
            warm(ACT.Sqrt)
            rms_of(1)
            for j in range(2):
                split_hi("conv_in", j)
            normalise(1, 0, 0)
            split_hi("conv_in", 2)
            with act.Fori(0, 2) as it:
                for b in range(4):
                    for j in range(3):
                        split_hi("conv_in", 3 * b + j + HI_LEAD, 12, it)
            act.wait_ge(conv_gated, 1)
            for half in range(2):
                c = slice(half * D, (half + 1) * D)
                nc.scalar.copy(act_hi[:, c], act32[:, c]).then_inc(conv_hi, 1)
            residual_panels("conv_out")
            peer(0)
            rms_of(3)
            normalise(3, 1, 0)
            for j in range(7):
                split_hi("mla_in", j + HI_LEAD)
                if j == 3:
                    act.wait_ge(lat_in, 1)
                    nc.scalar.activation(sqn[:, 0:QB * T], lat[:, 0:QB * T], ACT.Square).then_inc(lat_sq, 1)
                if j == 5:
                    act.wait_ge(lat_sum, 1)
                    nc.scalar.activation(rms[:, 0:T], OV[:, 0:T], ACT.Sqrt, bias=eps[:], scale=1.0 / Q_LORA
                                         ).then_inc(lat_rms, 1)
                    act.wait_ge(lat_in, 2)
                    nc.scalar.activation(sqn[:, QB * T:5 * T], lat[:, QB * T:5 * T], ACT.Square).then_inc(lat_sq, 1)
            act.wait_ge(pan_done, ring("mla_in", 6)[3] + HI)
            split_act(1, 0, QB * T)
            act.wait_ge(lat_sum, 2)
            nc.scalar.activation(rms[:, T:2 * T], STAT[:, 0:T], ACT.Sqrt, bias=eps[:], scale=1.0 / KV_LORA
                                 ).then_inc(lat_rms, 1)
            split_act(2, QB * T, KVB * T)
            act.wait_ge(trig_in, 1)
            nc.scalar.activation(sinb, sinb, ACT.Sin)
            nc.scalar.activation(cosb, cosb, ACT.Sin).then_inc(trig, 1)
            warm(ACT.Sqrt)
            for j in range(6):
                split_hi("q_b", j + HI_LEAD)
            for j in range(4):
                split_hi("k_b", j + HI_LEAD)
                if j == 1:
                    act.wait_ge(evac["q_b"], 6 + 2)
                    nc.scalar.activation(sqn, qn, ACT.Square)
                    nc.scalar.activation(sqr, qr, ACT.Square).then_inc(head_sq, 1)
            split_hi("v_b", HI_LEAD)
            act.wait_ge(evac["k_b"], 4 + 2)
            nc.scalar.activation(sqk, kn, ACT.Square)
            nc.scalar.activation(sqkr, kraw, ACT.Square).then_inc(head_sq, 1)
            for i, bank in enumerate((OV, STAT)):
                act.wait_ge(head_sum, i + 1)
                nc.scalar.activation(rms[0:HEADS, i * T:(i + 1) * T], bank[0:HEADS, 0:T], ACT.Sqrt,
                                     bias=eps[0:HEADS], scale=1.0 / QK_HEAD).then_inc(head_rms, 1)
            warm(ACT.Exp)
            split_hi("v_b", 1 + HI_LEAD)
            act.wait_ge(q_rotated, 1)
            for h in range(HEADS):
                z = qz[:, 2 * h * T:(2 * h + 2) * T].rearrange("p (x t) -> p x t", t=T)
                src = rotq.rearrange("p (x i t) -> p x i t", x=2, t=T)[:, :, h // 4, :]
                c = C_GROUP + 4 + h % 4
                n = nc.scalar.activation(z, src, ACT.Copy, scale=con[:, c:c + 1])
            n.then_inc(qz_ready, 1)
            for i in range(HEADS + 3):
                if 2 <= i <= HEADS + 1:
                    act.wait_ge(p_tr, i - 1)
                    nc.scalar.copy(pT[:, i % 2, :], TR[i % 2][:, 0:384]).then_inc(p_copied, 1)
                if i < HEADS:
                    act.wait_ge(s_masked, i + 1)
                    for t, (c0, c1) in enumerate(((0, P), (P, 3 * P))):
                        e = nc.scalar.activation(s_sb[:, i % 3, c0:c1], s_sb[:, i % 3, c0:c1], ACT.Exp,
                                                 bias=smax[:, i % 3, t:t + 1], scale=float(QK_HEAD) ** -0.5,
                                                 accum_out=ssum[:, i % 3, t:t + 1])
                    e.then_inc(p_exp, 1)
                if i >= 3:
                    h = i - 3
                    act.wait_ge(o_done, h + 1)
                    nc.scalar.copy(act_hi[:, h * T:(h + 1) * T], (OV, STAT)[h % 2][:, 0:T]).then_inc(o_hi, 1)
            residual_panels("mla_out")
            peer(1)

        @block.gpsimd
        def _(pool):
            def split_lo(stage, j, unroll=0, it=0):
                slot, lo_slot, _, n = ring(stage, j, unroll, it)
                width = D if unroll else WIDTHS.get(BASE[stage] + j, D)
                pool.wait_ge(hi_done, n)
                pool.wait_ge(pan_done, n + HI - LO)
                pool.tensor_tensor(w_lo[:, lo_slot, 0:width], raw[:, slot, 0:width],
                                   w_hi[:, slot, 0:width].bitcast(F32), ALU.subtract).then_inc(lo_done, 1)

            def select_panels(l):
                with pool.Fori(0, 6) as it:
                    for j in range(4):
                        split_lo(f"sel{l}", j, 4, it)
                with pool.Fori(0, 6) as it:
                    for j in range(4):
                        split_lo(f"ahead{l}", j, 4, it)
                split_lo(f"mix{l}", 0)

            with pool.Fori(0, 2) as it:
                for j in range(12):
                    split_lo("conv_in", j, 12, it)
            with pool.Fori(0, 2) as it:
                for j in range(4):
                    split_lo("conv_out", j, 4, it)
            select_panels(0)
            with pool.Fori(0, 96 - ADA_FIRST) as it:
                pool.wait_ge(ada1_used, it + 1)
                pool.sem_inc(ada_seen, 1)
                pool.dma_start(ada1[:], ada_in[bass.ds(it + ADA_FIRST, 1)].rearrange("o p n -> p (o n)")
                               ).then_inc(ada1_landed, 16)
            pool.wait_ge(lo_done, ring("mla_in", 0)[3] + RAW)
            for j in range(1, 7):
                split_lo("mla_in", j)
            for stage, count in (("q_b", 6), ("k_b", 4), ("v_b", 2)):
                for j in range(count):
                    split_lo(stage, j)
            with pool.Fori(0, 2) as it:
                for j in range(4):
                    split_lo("mla_out", j, 4, it)
            select_panels(1)

        @block.vector
        def _(dve):
            def split_lo(stage, j, unroll=0, it=0):
                slot, lo_slot, _, n = ring(stage, j, unroll, it)
                width = D if unroll else WIDTHS.get(BASE[stage] + j, D)
                dve.wait_ge(hi_done, n)
                dve.wait_ge(pan_done, n + HI - LO)
                dve.tensor_tensor(w_lo[:, lo_slot, 0:width], raw[:, slot, 0:width], w_hi[:, slot, 0:width].bitcast(F32),
                                  ALU.subtract).then_inc(lo_done, 1)

            def split_act(n, c0, width):
                dve.wait_ge(act_hi_ready, n)
                dve.tensor_tensor(act_lo[:, c0:c0 + width], lat[:, c0:c0 + width],
                                  act_hi[:, c0:c0 + width].bitcast(F32), ALU.subtract).then_inc(act_ready, 1)

            def wait_product(stage, j, unroll=0, it=0):
                dve.wait_ge(pan_done, ring(stage, j, unroll, it)[3] + HI)

            def mod_col(l, s):
                return l * 48 + s * KB

            def modulation(col, n):
                dve.drain()
                dve.tensor_tensor(mod[:, bass.ds(col, n)], ada_sum[:, 0:n], vec[:, bass.ds(col + V_ADAB, n)], ALU.add)
                dve.drain()

            def ada_row(row, step, it, j):
                slot = row % ADA
                dve.wait_ge(ada_landed[slot], it * (step // ADA * 16) + 16 * (row // ADA + 1))
                dve.tensor_tensor_reduce(out=ada[:, slot, :], in0=ada[:, slot, :], in1=crow[:], scale=1.0,
                                         scalar=0.0, op0=ALU.mult, op1=ALU.add, accum_out=ada_sum[:, j:j + 1]
                                         ).then_inc(ada_used, 1)

            def ada1_row(n, j):
                dve.wait_ge(ada1_landed, n * 16 + 16)
                dve.tensor_tensor_reduce(out=ada1[:], in0=ada1[:], in1=crow[:], scale=1.0, scalar=0.0, op0=ALU.mult,
                                         op1=ALU.add, accum_out=ada_sum[:, j:j + 1]).then_inc(ada1_used, 1)

            def inverse_rms(n):
                dve.wait_ge(rms_ready, n)
                dve.reciprocal(rstd[:, 0:T], rms[:, 0:T])

            def scale_x(l, g0, s0, release=True):
                sc = mod_col(l, s0 + 1)
                dve.scalar_tensor_tensor(out=gain[:], in0=mod[:, sc:sc + KB], scalar=1.0, in1=vec[:, g0:g0 + KB],
                                         op0=ALU.add, op1=ALU.mult)
                dve.drain()
                for half in range(2):
                    for k in range(half * KB // 2, (half + 1) * KB // 2):
                        c = slice(k * T, (k + 1) * T)
                        dve.scalar_tensor_tensor(out=act32[:, c], in0=xT[:, c], scalar=gain[:, k:k + 1],
                                                 in1=rstd[:, 0:T], op0=ALU.mult, op1=ALU.mult)
                    dve.drain()
                    if release:
                        dve.sem_inc(scaled, 1)

            def normalised_lo(n, l, s0):
                sh = mod_col(l, s0)
                for half in range(2):
                    dve.wait_ge(norm_hi, 2 * n - 1 + half)
                    for k in range(half * KB // 2, (half + 1) * KB // 2):
                        c = slice(k * T, (k + 1) * T)
                        i = dve.scalar_tensor_tensor(out=act_lo[:, c], in0=act32[:, c], scalar=mod[:, sh + k:sh + k + 1],
                                                     in1=act_hi[:, c].bitcast(F32), op0=ALU.add, op1=ALU.subtract)
                    i.then_inc(norm_ready, 1)

            def add_to_x(stage, l, last_count):
                dve.drain()
                dve.sem_inc(evac[stage], 2)
                dve.memset(sq_sum, 0.0)
                with dve.Fori(0, 2) as it:
                    for j in range(4):
                        if l == 0:
                            ada_row(32 + j, 4, it, j)
                        wait_product(stage, j, 4, it)
                        xk = xT[:, bass.ds((it * 4 + j) * T, T)]
                        dve.scalar_tensor_tensor(out=xk, in0=PAN[j % 2][:, 0:T],
                                                 scalar=mod[:, bass.ds(it * 4 + (j + mod_col(l, 2)), 1)], in1=xk,
                                                 op0=ALU.mult, op1=ALU.add).then_inc(evac[stage], 1)
                        dve.drain()
                        dve.wait_ge(sq_block, it * 4 + (8 * l + j + 1))
                        dve.tensor_tensor(sq_sum, sq_sum, sq[:, bass.ds((it * 4 + j) * T, T)], ALU.add)
                    if l == 0:
                        modulation(it * 4 + 32, 4)
                dve.drain()
                dve.sem_inc(sq_summed, 1)
                dve.sem_inc(x_ready, 1)

            def best_first(sets, release=0):
                for src, vals, _, _ in sets:
                    dve.max(vals[:, 0:8], src)
                dve.drain()
                for src, vals, idx, _ in sets:
                    dve.max_index(idx[:, 0:8], vals[:, 0:8], src)
                for i, (src, vals, _, spare) in enumerate(sets):
                    r = dve.match_replace(spare, vals[:, 0:8], src, NEG)
                    if i % TT == TT - 1 and i < release * TT:
                        r.then_inc(sc_used, 1)
                dve.drain()

            def best_second(sets):
                for _, vals, _, spare in sets:
                    dve.max(vals[:, 8:16], spare)
                dve.drain()
                for _, vals, idx, spare in sets:
                    dve.max_index(idx[:, 8:16], vals[:, 8:16], spare)
                dve.drain()

            def select(l):
                tv = lambda t, p: topv[:, (t * 2 + p) * TOPK:(t * 2 + p + 1) * TOPK]
                ti = lambda t, p: topi[:, (t * 2 + p) * TOPK:(t * 2 + p + 1) * TOPK]
                tiles = range(TT)
                by_tile = lambda a: a.rearrange("p (t n) -> p t n", t=TT)

                halves = [(SC[p][:, t * P:(t + 1) * P], tv(t, p), ti(t, p), work[:, (2 * p + t) * P:(2 * p + t + 1) * P])
                          for p in range(2) for t in tiles]
                pairs = [(cand[:, t * 256:(t + 1) * 256], bestv[:, t * TOPK:(t + 1) * TOPK],
                          bestp[:, t * TOPK:(t + 1) * TOPK], cwork[:, t * 256:(t + 1) * 256]) for t in tiles]

                def wait_scores(count):
                    dve.wait_ge(sc_done, count)
                    dve.sem_inc(sc_seen, 1)
                    dve.drain()

                def keep_halves(head):
                    dve.tensor_copy(top_i[:, :, bass.ds(head * (2 * TOPK), 2 * TOPK)], by_tile(topi))
                    for t in tiles:
                        dve.tensor_tensor(pairs[t][0].rearrange("p (a b) -> p a b", b=TOPK),
                                          tv(t, 0).unsqueeze(2).broadcast_to([P, TOPK, TOPK]),
                                          tv(t, 1).unsqueeze(1).broadcast_to([P, TOPK, TOPK]), ALU.add)

                def keep_pairs(head):
                    dve.tensor_copy(best_v[:, :, bass.ds(head * TOPK, TOPK)], by_tile(bestv))
                    dve.tensor_copy(best_p[:, :, bass.ds(head * TOPK, TOPK)], by_tile(bestp))

                wait_scores(16 * l + 2)
                best_first(halves, 2)
                best_second(halves)
                keep_halves(0)
                with dve.Fori(1, HEADS) as it:
                    wait_scores(it * 2 + (16 * l + 2))
                    best_first(halves + pairs, 2)
                    best_second(halves + pairs)
                    keep_pairs(it - 1)
                    keep_halves(it)
                dve.drain()
                best_first(pairs)
                best_second(pairs)
                keep_pairs(HEADS - 1)
                dve.drain()
                hk = lambda a: a.rearrange("p t (h k) -> p (t h) k", k=TOPK)
                bv = hk(best_v)
                dve.tensor_tensor(hk(gate), bv, bv[:, :, 0:1].broadcast_to([P, TT * HEADS, TOPK]), ALU.subtract
                                  ).then_inc(gate_in, 1)
                if l == 0:
                    dve.wait_ge(s_iota, 32)
                for t in tiles:
                    dve.tensor_scalar(dec_u[:, 0, :], best_p[:, t, :], 4, None, ALU.logical_shift_right)
                    dve.tensor_scalar(dec_u[:, 1, :], best_p[:, t, :], 15, None, ALU.bitwise_and)
                    dve.drain()
                    dve.tensor_copy(dec_f, dec_u.rearrange("p x n -> p (x n)"))
                    for x in range(2):
                        dve.drain()
                        e4 = eq.rearrange("p (h j k) -> p h j k", h=HEADS, k=TOPK)
                        place = dec_f[:, x * SEL:(x + 1) * SEL].rearrange("p (h k) -> p h k", k=TOPK)
                        dve.tensor_tensor(e4, place.unsqueeze(2).broadcast_to([P, HEADS, TOPK, TOPK]),
                                          iota_x[:, 0:TOPK * GT].rearrange("p (j k) -> p j k", k=GT).unsqueeze(1)
                                          .broadcast_to([P, HEADS, TOPK, TOPK]), ALU.is_equal)
                        dve.drain()
                        dve.wait_ge(keyx_ready, 2 * TT * l + 2 * t + x + 1)
                        dve.tensor_tensor(eq, eq, keyx[:, 2 * t + x, :], ALU.mult)
                        dve.drain()
                        dve.tensor_reduce(eab[:, (2 * t + x) * SEL:(2 * t + x + 1) * SEL]
                                          .rearrange("p (h k) -> p h k", k=TOPK),
                                          eq.rearrange("p (h j k) -> p h k j", h=HEADS, k=TOPK), AX.X, ALU.add)
                    if t == 0:
                        dve.wait_ge(gate_exp, l + 1)
                        dve.tensor_reduce(esum, hk(gate), AX.X, ALU.add)
                        dve.drain()
                        dve.reciprocal(esum, esum)
                        dve.drain()
                        dve.tensor_tensor(hk(gate), hk(gate), esum.unsqueeze(2).broadcast_to([P, TT * HEADS, TOPK]),
                                          ALU.mult)
                    dve.drain()
                    dve.sem_inc(dec_done, 1)
                for t in tiles:
                    dve.wait_ge(idx_done, TT * l + t + 1)
                    c = slice(t * P, (t + 1) * P)
                    dve.tensor_copy(ia_t[:, c], GB[t][:, 0:P])
                    dve.tensor_copy(ib_t[:, c], GB[t][:, P:2 * P])
                    dve.tensor_scalar(g32_t[:, c], GB[t][:, 2 * P:3 * P], G_SCALE, None, ALU.mult)
                dve.drain()
                dve.tensor_copy(gh_t[:], g32_t[:])
                dve.drain()
                dve.tensor_tensor(gl_t[:], g32_t[:], gh_t[:], ALU.subtract)
                dve.drain()

            each = lambda a, n, token0: a[:, bass.ds(token0, GT)].unsqueeze(1).broadcast_to([P, n, GT])
            wide = lambda a: a.rearrange("p (b t) -> p b t", t=GT)

            def second_key_hots(par, count, token0):
                dve.wait_ge(g_done, count)
                dve.tensor_tensor(wide(hot_b[:, par, :]), each(ib_t, KEYS, token0), wide(iota_x[:]), ALU.is_equal)

            def first_key_hots(quarter, par, token0):
                dve.tensor_tensor(wide(hot_a[:, par, :]), each(ia_t, QUART, token0),
                                  wide(iota_x[:, quarter * QUART * GT:(quarter + 1) * QUART * GT]), ALU.is_equal)
                dve.drain()
                for x, g in enumerate((gh_t, gl_t)):
                    i = dve.tensor_tensor(wide(hot_g[:, par, x * QUART * GT:(x + 1) * QUART * GT]),
                                          wide(hot_a[:, par, :]), each(g, QUART, token0), ALU.mult)
                i.then_inc(hot_ready, 1)

            def add_gates(quarter, nth, token0):
                dve.wait_ge(g_first, nth)
                g = arena[:, quarter % 2 * QUART * T:(quarter % 2 + 1) * QUART * T].rearrange("p (a t) -> p a t", t=T)
                for n in range(2):
                    two = GB[n][:].rearrange("p (t x a) -> p x a t", x=2, a=QUART)
                    to = g[:, :, bass.ds(token0 + n * (GT // 2), GT // 2)]
                    i = dve.tensor_tensor(to, two[:, 1], to, ALU.add)
                i.then_inc(g_read, 1)

            def weigh(slot, key, count):
                dve.drain()
                dve.wait_ge(g_read, count)
                dve.tensor_tensor(w32[:], ring_g[:, bass.ds(slot * T, 2 * T)], arena[:, bass.ds(key * T, 2 * T)],
                                  ALU.mult).then_inc(w_mul, 1)

            def split_weighted(par, count):
                dve.wait_ge(wt_hi_ready, count)
                dve.tensor_tensor(wt_lo[:, par, :], w32[:], wt_hi[:, par, :].bitcast(F32), ALU.subtract
                                  ).then_inc(wt_ready, 1)

            def experts(l):
                with dve.Fori(0, 2) as it:
                    for j in range(8):
                        second_key_hots(j % 2, it * 8 + (64 * l + j + 1), (it * 8 + j) * GT)
                        first_key_hots(0, j % 2, (it * 8 + j) * GT)
                dve.wait_ge(lo_done, ring(f"mix{l}", 0)[3] + RAW)
                weigh(0, 0, 64 * l + 16 + 2)
                split_weighted(0, 64 * l + 1)

                def mix_body(q, it, end):
                    for s in range(2):
                        j = 64 * q + 4 * s
                        token0 = (it * 2 + s) * GT
                        split_lo(f"mix{l}", j + 1, 8, it)
                        second_key_hots(s, it * 2 + (64 * l + 16 * (q + 1) + s + 1), token0)
                        split_lo(f"mix{l}", j + 2, 8, it)
                        first_key_hots(q + 1, s, token0)
                        split_lo(f"mix{l}", j + 3, 8, it)
                        if l == 0:
                            ada1_row(it * 2 + (16 * q + s), s)
                        if not (end and s):
                            weigh(it * 4 + (2 * s + 2), it * 4 + (q % 2 * QUART + 2 * s + 2), 64 * l + 16 * (q + 1) + 2)
                        split_lo(f"mix{l}", j + 4, 8, it)
                        add_gates(q + 1, it * 2 + (48 * l + 16 * q + s + 1), token0)
                        if end and s:
                            weigh(0, (q + 1) % 2 * QUART, 64 * l + 16 * (q + 2) + 2)
                        split_weighted(1 - s, it * 2 + (64 * l + 16 * q + s + 2))
                    if l == 0:
                        modulation(it * 2 + (ADA_FIRST + 16 * q), 2)

                for q in range(3):
                    with dve.Fori(0, 7) as it:
                        mix_body(q, it, False)
                    mix_body(q, 7, True)

                def last_body(it, end):
                    for s in range(2):
                        split_lo(f"last{l}", 2 * s + 1, 4, it)
                        if not (end and s):
                            weigh(it * 4 + (2 * s + 2), it * 4 + (QUART + 2 * s + 2), 64 * l + 64 + 2)
                        if not (end and s and l):
                            split_lo(f"last{l}", 2 * s + 2, 4, it)
                        if not (end and s):
                            split_weighted(1 - s, it * 2 + (64 * l + 48 + s + 2))
                    if l == 0:
                        ada1_row(it + 48, 0)
                        modulation(it + (ADA_FIRST + 48), 1)

                with dve.Fori(0, 7) as it:
                    last_body(it, False)
                last_body(7, True)
                wait_product(f"last{l}", 31)
                for n in range(2, 4):
                    i = dve.tensor_scalar(yrow[:, n * 512:(n + 1) * 512], YB[n][:], 1.0 / G_SCALE, None, ALU.mult)
                i.then_inc(y1_copied, 1)
                for t in range(TT):
                    for g in range(2):
                        dve.wait_ge(yt_done, 4 * l + 2 * t + g + 1)
                        for k in range(4):
                            kk = 4 * g + k
                            xk = xT[:, kk * T + t * P:kk * T + (t + 1) * P]
                            c = mod_col(l, 5) + kk
                            i = dve.scalar_tensor_tensor(out=xk, in0=GB[g][:, k * P:(k + 1) * P],
                                                         scalar=mod[:, c:c + 1], in1=xk, op0=ALU.mult, op1=ALU.add)
                        i.then_inc(yt_added, 1)
                dve.drain()
                dve.sem_inc(x_ready, 1)

            def peer(l):
                inverse_rms(2 * l + 2)
                scale_x(l, V_CH + l * KB, 3)
                normalised_lo(2 * l + 2, l, 3)
                select(l)
                experts(l)

            def reduced(out_ap, shift):
                dve.tensor_scalar(tmp, ang, 1.0 / TWO_PI, shift / TWO_PI, ALU.mult, ALU.add)
                dve.drain()
                dve.tensor_scalar(tmp, tmp, ROUND, None, ALU.add)
                dve.drain()
                dve.tensor_scalar(tmp, tmp, -ROUND, None, ALU.add)
                dve.drain()
                src = ang
                for part in (PI_1, PI_2, PI_3):
                    dve.scalar_tensor_tensor(out=out_ap, in0=tmp, scalar=-part, in1=src, op0=ALU.mult, op1=ALU.add)
                    dve.drain()
                    src = out_ap
                dve.tensor_scalar(out_ap, out_ap, shift, None, ALU.add)
                dve.drain()
                return dve.tensor_scalar(out_ap, out_ap, 3.1415925, -3.1415925, ALU.min, ALU.max)

            def rotate(src, dst):
                two = lambda ap: ap.rearrange("p (i t) -> p i t", t=T)
                cs = cosb.unsqueeze(1).broadcast_to([P, 2, T])
                sn = sinb.unsqueeze(1).broadcast_to([P, 2, T])
                a, b = two(src[:, 0:2 * T]), two(src[:, 2 * T:4 * T])
                t1, t2 = act32[:, 512:1024], act32[:, 1024:1536]
                for o, (m1, m2, op) in enumerate(((cs, sn, ALU.subtract), (sn, cs, ALU.add))):
                    dve.tensor_tensor(two(t1), a, m1, ALU.mult)
                    dve.tensor_tensor(two(t2), b, m2, ALU.mult)
                    dve.drain()
                    i = dve.tensor_tensor(dst[:, o * 2 * T:(o + 1) * 2 * T], t1, t2, op)
                    dve.drain()
                return i

            def attention():
                inverse_rms(3)
                scale_x(1, V_TOK + KB, 0)
                normalised_lo(3, 1, 0)
                dve.sem_inc(evac["mla_in"], 2)
                dve.wait_ge(s_pos, 16)
                dve.tensor_copy(ang, posi)
                dve.drain()
                dve.tensor_scalar(ang, ang, con[:, C_FREQ:C_FREQ + 1], None, ALU.mult)
                dve.drain()
                reduced(sinb, 0.0)
                dve.drain()
                reduced(cosb, np.pi / 2).then_inc(trig_in, 1)
                def latents(n, k0, blocks):
                    r = rstd[:, (n - 1) * T:n * T]
                    dve.wait_ge(lat_rms, n)
                    dve.reciprocal(r, rms[:, (n - 1) * T:n * T])
                    dve.drain()
                    for k in range(k0, k0 + blocks):
                        lk = lat[:, k * T:(k + 1) * T]
                        dve.scalar_tensor_tensor(out=lk, in0=lk, scalar=vec[:, V_QA + k:V_QA + k + 1], in1=r,
                                                 op0=ALU.mult, op1=ALU.mult)
                    dve.drain()
                    dve.sem_inc(f32_ready, 1)

                for j in range(7):
                    wait_product("mla_in", j)
                    dst = lat[:, j * T:(j + 1) * T] if j < 5 else kraw[:, (j - 5) * T:(j - 4) * T]
                    dve.tensor_copy(dst, PAN[j % 2][:, 0:T]).then_inc(evac["mla_in"], 1)
                    if j in (QB - 1, QB + KVB - 1):
                        dve.drain()
                        dve.sem_inc(lat_in, 1)
                    if j == 5:
                        latents(1, 0, QB)
                split_act(1, 0, QB * T)
                latents(2, QB, KVB)
                split_act(2, QB * T, KVB * T)
                dve.drain()
                dve.sem_inc(evac["q_b"], 2)
                for j in range(6):
                    wait_product("q_b", j)
                    dve.tensor_copy(arena[:, j * 2 * T:(j + 1) * 2 * T], PAN[j % 2][:]).then_inc(evac["q_b"], 1)
                dve.drain()
                dve.sem_inc(evac["k_b"], 2)
                for j in range(4):
                    wait_product("k_b", j)
                    dve.tensor_copy(kn[:, j * 2 * T:(j + 1) * 2 * T], PAN[j % 2][:]).then_inc(evac["k_b"], 1)
                dve.wait_ge(head_rms, 1)
                dve.reciprocal(rstd[0:HEADS, 0:T], rms[0:HEADS, 0:T]).then_inc(head_rstd, 1)
                wait_product("v_b", 1)
                for n, bank in enumerate((SC[0], SC[1], TR[0], TR[1])):
                    i = dve.tensor_copy(vv[:, n * 512:(n + 1) * 512], bank[:])
                i.then_inc(v_copied, 1)

                def scaled_heads(i):
                    x5 = i if i < 2 else (i - 2) // 4
                    dve.wait_ge(bc_done, i + 1)
                    b, g = BC[i % len(BC)], (V_QN, V_KN)[x5]
                    two = lambda a: a.rearrange("p (i t) -> p i t", t=T)
                    if i < 2:
                        for x in range(2):
                            dst = (qr, kr)[x5][:, 2 * x * T:(2 * x + 2) * T]
                            src = two(dst) if i == 0 else kraw[:, x * T:(x + 1) * T].unsqueeze(1).broadcast_to([P, 2, T])
                            n = dve.scalar_tensor_tensor(out=two(dst), in0=src, scalar=vec[:, g + 1 + x:g + 2 + x],
                                                         in1=two(b[:]), op0=ALU.mult, op1=ALU.mult)
                    else:
                        p2 = (i - 2) % 4
                        hd = (qn, kn)[x5][:, 2 * p2 * T:2 * (p2 + 1) * T]
                        n = dve.scalar_tensor_tensor(out=hd, in0=hd, scalar=vec[:, g:g + 1], in1=b[:], op0=ALU.mult,
                                                     op1=ALU.mult)
                    n.then_inc(bc_used, 1)

                scaled_heads(0)
                dve.wait_ge(head_rms, 2)
                dve.reciprocal(rstd[0:HEADS, T:2 * T], rms[0:HEADS, T:2 * T]).then_inc(head_rstd, 1)
                dve.drain()
                dve.wait_ge(trig, 1)
                rotate(qr, rotq)
                dve.sem_inc(q_rotated, 1)
                for i in range(1, 5):
                    scaled_heads(i)
                dve.drain()
                rotate(kr, rot)
                for i in range(5, 10):
                    scaled_heads(i)
                dve.drain()
                dve.sem_inc(qk_ready, 1)
                for i in range(HEADS + 3):
                    if 1 <= i <= HEADS:
                        h = i - 1
                        dve.wait_ge(p_exp, h + 1)
                        dve.reciprocal(ssum[:, h % 3, :], ssum[:, h % 3, :])
                        dve.drain()
                        for t, (c0, c1) in enumerate(((0, P), (P, 3 * P))):
                            n = dve.tensor_scalar(s_sb[:, h % 3, c0:c1], s_sb[:, h % 3, c0:c1],
                                                  ssum[:, h % 3, t:t + 1], None, ALU.mult)
                        n.then_inc(p_norm, 1)
                    if i < HEADS:
                        h = i
                        dve.wait_ge(s_done, h + 1)
                        dve.tensor_tensor(s_sb[:, h % 3, :], SC[h % 2][:, 0:384], con[:, C_MASK:C_MASK + 384], ALU.add)
                        dve.drain()
                        for t, (c0, c1) in enumerate(((0, P), (P, 3 * P))):
                            dve.tensor_reduce(smax[:, h % 3, t:t + 1], s_sb[:, h % 3, c0:c1], AX.X, ALU.max)
                        dve.drain()
                        dve.tensor_scalar(smax[:, h % 3, :], smax[:, h % 3, :], -float(QK_HEAD) ** -0.5, None, ALU.mult
                                          ).then_inc(s_masked, 1)
                    if i >= 3:
                        h = i - 3
                        dve.wait_ge(o_hi, h + 1)
                        c = slice(h * T, (h + 1) * T)
                        dve.tensor_tensor(act_lo[:, c], (OV, STAT)[h % 2][:, 0:T], act_hi[:, c].bitcast(F32),
                                          ALU.subtract).then_inc(o_copied, 1)
                add_to_x("mla_out", 1, 3)

            dve.memset(eps[:], EPS)
            dve.memset(zero[:].bitcast(F32), 0.0)
            dve.memset(u_pad[:, 0:2], 0.0).then_inc(s_eps, 1)
            dve.sem_inc(lo_done, RAW)
            dve.sem_inc(ada_used, ADA)
            dve.sem_inc(ada1_used, 1)
            dve.sem_inc(sc_used, 2)
            dve.wait_ge(s_const, 64)
            dve.wait_ge(s_silu, 1)
            with dve.Fori(0, 2) as it:
                for j in range(4):
                    ada_row(j, 4, it, j)
                modulation(it * 4 + KB, 4)
            inverse_rms(1)
            scale_x(0, V_TOK, 0, release=False)
            with dve.Fori(0, 2) as it:
                for j in range(4):
                    ada_row(KB + j, 4, it, j)
                modulation(it * 4, 4)
            dve.sem_inc(scaled, 2)
            normalised_lo(1, 0, 0)
            dve.sem_inc(evac["conv_in"], 2)
            with dve.Fori(0, 2) as it:
                for b in range(4):
                    ada_row(16 + 2 * b, 8, it, 2 * (b % 2))
                    wait_product("conv_in", 3 * b, 12, it)
                    dve.tensor_copy(c_sb, PAN[3 * b % 2][:, 0:T]).then_inc(evac["conv_in"], 1)
                    ada_row(17 + 2 * b, 8, it, 2 * (b % 2) + 1)
                    if b % 2:
                        modulation(it * 8 + (16 + 4 * (b // 2)), 4)
                    dve.drain()
                    wait_product("conv_in", 3 * b + 1, 12, it)
                    dve.tensor_tensor(u_pad[:, 2:2 + T], PAN[(3 * b + 1) % 2][:, 0:T], c_sb, ALU.mult
                                      ).then_inc(evac["conv_in"], 1)
                    dve.drain()
                    tap = lambda i: vec[:, bass.ds(it * 4 + (V_CONV + i * KB + b), 1)]
                    dve.tensor_scalar(conv_t, u_pad[:, 0:T], tap(0), None, ALU.mult)
                    for i in (1, 2):
                        dve.drain()
                        dve.scalar_tensor_tensor(out=conv_t, in0=u_pad[:, i:i + T], scalar=tap(i), in1=conv_t,
                                                 op0=ALU.mult, op1=ALU.add)
                    dve.drain()
                    wait_product("conv_in", 3 * b + 2, 12, it)
                    k = bass.ds((it * 4 + b) * T, T)
                    dve.tensor_tensor(act32[:, k], PAN[(3 * b + 2) % 2][:, 0:T], conv_t, ALU.mult
                                      ).then_inc(evac["conv_in"], 1)
            dve.drain()
            dve.sem_inc(conv_gated, 1)
            for half in range(2):
                dve.wait_ge(conv_hi, half + 1)
                c = slice(half * D, (half + 1) * D)
                dve.tensor_tensor(act_lo[:, c], act32[:, c], act_hi[:, c].bitcast(F32), ALU.subtract
                                  ).then_inc(conv_split, 1)
            add_to_x("conv_out", 0, 1)
            peer(0)
            attention()
            peer(1)


def shape_constants():
    con = np.zeros((P, C_N), np.float32)
    con[:, C_ID:C_ID + P] = np.eye(P)
    con[:, C_ONE:C_ONE + P] = 1.0
    tri = np.where(np.arange(P)[:, None] >= np.arange(P)[None, :], 0.0, -1.0e30)
    con[:, C_MASK:C_MASK + P] = tri
    con[:, C_MASK + 2 * P:C_MASK + 3 * P] = tri
    con[:, C_HEAD + 7] = 1.0
    for j in range(4):
        con[32 * j:32 * j + 32, C_GROUP + 4 + j] = 1.0
    for h in range(HEADS):
        con[h, C_SPREAD + 32 * h:C_SPREAD + 32 * h + 32] = 1.0
    con[0:32, C_FIRST:C_FIRST + HEADS] = 1.0
    freq = np.float32(10000.0) ** (-np.arange(0, ROPE, 2, dtype=np.float32) / np.float32(ROPE))
    con[:, C_FREQ] = np.tile(freq.astype(np.float32), 4)
    return con


def kernel(x, c, positions, tok_norm, ch_norm, ada_w, ada_b, conv_in_w, conv_w, conv_out_w,
           mla_in_w, q_a_norm, kv_a_norm, q_b_w, kv_b_w, q_norm, k_norm, mla_out_w,
           peer_q_w, peer_subkeys, peer_u, peer_v):
    import concourse.bacc as bacc
    from concourse.bass_utils import run_bass_kernel_spmd

    def cols(v):
        return np.ascontiguousarray(v).reshape(-1, P).T

    def panels(w):
        k, n = w.shape[0] // P, w.shape[1] // P
        return w.reshape(k, P, n, P).transpose(2, 1, 0, 3).reshape(n, P, k * P)

    def packed(p, per):
        n, _, w = p.shape
        out = np.zeros((n // per, P, D), p.dtype)
        out[:, :, 0:per * w] = p.reshape(n // per, per, P, w).transpose(0, 2, 1, 3).reshape(n // per, P, per * w)
        return out

    g = [np.asarray(a) for a in (x, c, positions, tok_norm, ch_norm, ada_w, ada_b, conv_in_w, conv_w, conv_out_w,
                                 mla_in_w, q_a_norm, kv_a_norm, q_b_w, kv_b_w, q_norm, k_norm, mla_out_w,
                                 peer_q_w, peer_subkeys, peer_u, peer_v)]
    (x, c, positions, tok_norm, ch_norm, ada_w, ada_b, conv_in_w, conv_w, conv_out_w, mla_in_w, q_a_norm,
     kv_a_norm, q_b_w, kv_b_w, q_norm, k_norm, mla_out_w, peer_q_w, peer_subkeys, peer_u, peer_v) = g

    ci = panels(conv_in_w[0])
    conv_in = np.stack([ci[KB:2 * KB], ci[2 * KB:3 * KB], ci[0:KB]], 1).reshape(3 * KB, P, D)
    lora = Q_LORA + KV_LORA
    rope_in = [np.tile(mla_in_w[0][:, lora + h * HALF_ROPE:lora + (h + 1) * HALF_ROPE], (1, 4)) for h in range(2)]
    mla_in = panels(np.concatenate([mla_in_w[0][:, 0:lora]] + rope_in, 1))
    qb = q_b_w[0].reshape(Q_LORA, HEADS, QK_HEAD)
    qcols = [qb[:, :, 0:NOPE], qb[:, :, NOPE:NOPE + HALF_ROPE], qb[:, :, NOPE + HALF_ROPE:]]
    q_b = packed(panels(np.concatenate([a.reshape(Q_LORA, -1) for a in qcols], 1)), 2)
    kvb = kv_b_w[0].reshape(KV_LORA, HEADS, NOPE + VH)
    k_b = packed(panels(np.ascontiguousarray(kvb[:, :, 0:NOPE]).reshape(KV_LORA, -1)), 2)
    v_b = np.ascontiguousarray(kvb[:, :, NOPE:]).reshape(KVB, P, D)
    stages = [conv_in, panels(conv_out_w[0]), panels(peer_q_w[0]), mla_in, q_b, k_b, v_b, panels(mla_out_w[0]),
              panels(peer_q_w[1])]
    ropes = lambda v: [np.tile(v[NOPE + h * HALF_ROPE:NOPE + (h + 1) * HALF_ROPE], 4)[:, None] for h in range(2)]
    vec = np.concatenate(
        [cols(tok_norm), cols(ch_norm), cols(ada_b), cols(conv_w[0]), cols(q_a_norm), cols(kv_a_norm),
         cols(q_norm[0][0:NOPE])] + ropes(q_norm[0]) + [cols(k_norm[0][0:NOPE])] + ropes(k_norm[0]), 1)
    vec = np.pad(vec, ((0, 0), (0, V_N - vec.shape[1])))
    arrays = {
        "xT": x[0].T.reshape(KB, P, T).transpose(1, 0, 2).reshape(P, KB * T),
        "c": c[0],
        "positions": positions[0],
        "vectors": vec,
        "constants": shape_constants(),
        "ada_rows": ada_w.transpose(0, 2, 1).reshape(96, P, D),
        "panels": np.concatenate(stages, 0),
        "subkeys": peer_subkeys.reshape(2, PAIRS, KEYS, P).transpose(0, 3, 1, 2).reshape(2, P, PAIRS * KEYS),
        "key_numbers": np.broadcast_to(np.repeat(np.arange(KEYS), GT), (P, KEYS * GT)).astype(mybir.dt.np(BF16)),
        "u_panels": peer_u.reshape(2 * KEYS, KEYS, KB, P).transpose(0, 3, 2, 1).reshape(2 * KEYS, P, D),
        "v_panels": peer_v.reshape(2 * KEYS, P, D),
    }
    arrays = {n: np.ascontiguousarray(a) for n, a in arrays.items()}
    nc = bacc.Bacc("TRN2", target_bir_lowering=False, num_devices=1)
    ins = [nc.dram_tensor("in_" + n, a.shape, mybir.dt.from_np(a.dtype), kind="ExternalInput").ap() for n, a in arrays.items()]
    out = nc.dram_tensor("out", (P, KB * T), F32, kind="ExternalOutput").ap()
    program(nc, *ins, out)
    got = run_bass_kernel_spmd(nc, [{"in_" + n: a for n, a in arrays.items()}], core_ids=[0]).results[0]["out"]
    return np.ascontiguousarray(got.reshape(P, KB, T).transpose(1, 0, 2).reshape(D, T).T)[None]
```
